# Optimizing a Trainium2 kernel written in Bass

```python
import jax, jax.numpy as jnp
from jax import lax
import numpy as np

D_MODEL = 1024
BATCH = 1
SEQ = 256
DEPTH = 2

N_MIXERS = 2
HEAD_DIM = 64
N_HEADS = D_MODEL // HEAD_DIM
N_KV = 4
GQA = N_HEADS // N_KV
ROT_DIM = HEAD_DIM // 4
ROPE_THETA = 500000.0
NORM_EPS = 1e-6
Q_W = N_HEADS * HEAD_DIM
KV_W = N_KV * HEAD_DIM

CMP_LEN = 32
CMP_STRIDE = 16
CMP_HID = 4 * HEAD_DIM
SEL_BLOCK = 64
SEL_COUNT = 8
WINDOW = 256
NSA_Q_BLOCK = 32
NSA_IN = 2 * Q_W + 6 * KV_W + 3 * N_HEADS

MOBA_BLOCK = 256
MOBA_TOPK = 3
MOBA_Q_BLOCK = 8
MOBA_IN = 2 * Q_W + 2 * KV_W

N_A = (DEPTH + 1) // 2
N_B = DEPTH // 2


def rms_norm(x, g):
    xf = x.astype(jnp.float32)
    y = xf * lax.rsqrt(jnp.mean(xf * xf, axis=-1, keepdims=True) + NORM_EPS)
    return (y * g.astype(jnp.float32)).astype(x.dtype)

def rope_tables(pos):
    inv_freq = ROPE_THETA ** (-jnp.arange(0, ROT_DIM, 2, dtype=jnp.float32) / ROT_DIM)
    ang = pos.astype(jnp.float32)[..., None] * inv_freq
    return jnp.cos(ang), jnp.sin(ang)

def partial_rope(x, cos, sin):
    half = ROT_DIM // 2
    c = cos[:, :, None, :].astype(x.dtype)
    s = sin[:, :, None, :].astype(x.dtype)
    x1, x2, rest = x[..., :half], x[..., half:ROT_DIM], x[..., ROT_DIM:]
    return jnp.concatenate([x1 * c - x2 * s, x2 * c + x1 * s, rest], axis=-1)

def masked_softmax(s, mask):
    s = jnp.where(mask, s.astype(jnp.float32), -jnp.inf)
    m = jnp.max(s, axis=-1, keepdims=True)
    e = jnp.exp(s - jnp.where(jnp.isfinite(m), m, 0.0))
    return e / jnp.maximum(jnp.sum(e, axis=-1, keepdims=True), 1e-30)

def split_cols(a, widths):
    return jnp.split(a, np.cumsum(widths)[:-1].tolist(), axis=-1)

def cmp_to_sel_weights(n_cmp, n_sel):
    cs = np.arange(n_cmp)[:, None] * CMP_STRIDE
    ss = np.arange(n_sel)[None, :] * SEL_BLOCK
    shared = np.clip(np.minimum(cs + CMP_LEN, ss + SEL_BLOCK) - np.maximum(cs, ss), 0, None)
    return jnp.asarray(shared / CMP_LEN, dtype=jnp.float32)

def nsa_mixer(h, cos, sin, positions, w_in, w_out, q_g, k_g, cmp_pe, cmp_w1, cmp_b1, cmp_w2, gate_b):
    B, S, _ = h.shape
    q, kc, vc, ks, vs, kw, vw, gl, z = split_cols(h @ w_in, [Q_W] + [KV_W] * 6 + [3 * N_HEADS, Q_W])
    q = partial_rope(rms_norm(q.reshape(B, S, N_HEADS, HEAD_DIM), q_g), cos, sin)
    q = q.reshape(B, S, N_KV, GQA, HEAD_DIM)
    gates = jax.nn.sigmoid(gl + gate_b).reshape(B, S, N_KV, GQA, 3)
    scale = HEAD_DIM ** -0.5

    n_cmp = (S - CMP_LEN) // CMP_STRIDE + 1
    blk_idx = np.arange(n_cmp)[:, None] * CMP_STRIDE + np.arange(CMP_LEN)[None, :]
    cmp_end = blk_idx[:, -1]

    def compress(t, i):
        blocks = t.reshape(B, S, N_KV, HEAD_DIM)[:, blk_idx] + cmp_pe[i][None, None, :, None, :]
        flat = blocks.transpose(0, 1, 3, 2, 4).reshape(B, n_cmp, N_KV, CMP_LEN * HEAD_DIM)
        return jax.nn.gelu(flat @ cmp_w1[i] + cmp_b1[i]) @ cmp_w2[i]

    cos_c, sin_c = rope_tables(positions[:, cmp_end])
    k_cmp = partial_rope(rms_norm(compress(kc, 0), k_g[0]), cos_c, sin_c)
    v_cmp = compress(vc, 1)
    cmp_end_j = jnp.asarray(cmp_end, dtype=jnp.int32)

    n_sel = S // SEL_BLOCK
    k_sel = min(SEL_COUNT, n_sel)
    sel_w = cmp_to_sel_weights(n_cmp, n_sel)
    ks = partial_rope(rms_norm(ks.reshape(B, S, N_KV, HEAD_DIM), k_g[1]), cos, sin)
    ks_blk = ks.reshape(B, n_sel, SEL_BLOCK, N_KV, HEAD_DIM).transpose(0, 3, 1, 2, 4)
    vs_blk = vs.reshape(B, n_sel, SEL_BLOCK, N_KV, HEAD_DIM).transpose(0, 3, 1, 2, 4)

    pad = ((0, 0), (WINDOW, 0), (0, 0), (0, 0))
    kw_pad = jnp.pad(partial_rope(rms_norm(kw.reshape(B, S, N_KV, HEAD_DIM), k_g[2]), cos, sin), pad)
    vw_pad = jnp.pad(vw.reshape(B, S, N_KV, HEAD_DIM), pad)

    b_i = jnp.arange(B)[:, None, None, None]
    g_i = jnp.arange(N_KV)[None, None, :, None]
    sel_blocks = jnp.arange(n_sel)
    C = NSA_Q_BLOCK

    def q_block(ci):
        t0 = ci * C
        t = t0 + jnp.arange(C)
        qc = lax.dynamic_slice_in_dim(q, t0, C, axis=1)
        gc = lax.dynamic_slice_in_dim(gates, t0, C, axis=1)
        m_cmp = (cmp_end_j[None, :] <= t[:, None])[None, :, None, None, :]
        p_cmp = masked_softmax(jnp.einsum('bcgrd,bngd->bcgrn', qc, k_cmp) * scale, m_cmp)
        o_cmp = jnp.einsum('bcgrn,bngd->bcgrd', p_cmp.astype(v_cmp.dtype), v_cmp)
        imp = jnp.einsum('bcgrn,nj->bcgj', p_cmp, sel_w)
        cur = (t // SEL_BLOCK)[:, None]
        valid = sel_blocks[None, :] <= cur
        forced = (sel_blocks[None, :] == 0) | (sel_blocks[None, :] == cur) | (sel_blocks[None, :] == cur - 1)
        score = jnp.where(forced[None, :, None, :], jnp.inf,
                          jnp.where(valid[None, :, None, :], imp, -jnp.inf))
        _, sel = lax.top_k(score, k_sel)
        kg_sel = ks_blk[b_i, g_i, sel].reshape(B, C, N_KV, k_sel * SEL_BLOCK, HEAD_DIM)
        vg_sel = vs_blk[b_i, g_i, sel].reshape(B, C, N_KV, k_sel * SEL_BLOCK, HEAD_DIM)
        kpos = (sel[..., None] * SEL_BLOCK + jnp.arange(SEL_BLOCK)).reshape(B, C, N_KV, 1, k_sel * SEL_BLOCK)
        m_slc = kpos <= t[None, :, None, None, None]
        p_slc = masked_softmax(jnp.einsum('bcgrd,bcgnd->bcgrn', qc, kg_sel) * scale, m_slc)
        o_slc = jnp.einsum('bcgrn,bcgnd->bcgrd', p_slc.astype(vg_sel.dtype), vg_sel)
        kwc = lax.dynamic_slice_in_dim(kw_pad, t0, C + WINDOW, axis=1)
        vwc = lax.dynamic_slice_in_dim(vw_pad, t0, C + WINDOW, axis=1)
        kp = t0 - WINDOW + jnp.arange(C + WINDOW)
        dist = t[:, None] - kp[None, :]
        m_win = ((dist >= 0) & (dist < WINDOW) & (kp[None, :] >= 0))[None, :, None, None, :]
        p_win = masked_softmax(jnp.einsum('bcgrd,bkgd->bcgrk', qc, kwc) * scale, m_win)
        o_win = jnp.einsum('bcgrk,bkgd->bcgrd', p_win.astype(vwc.dtype), vwc)
        return gc[..., 0:1] * o_cmp + gc[..., 1:2] * o_slc + gc[..., 2:3] * o_win

    o = lax.map(q_block, jnp.arange(S // C))
    o = jnp.moveaxis(o, 0, 1).reshape(B, S, Q_W)
    return (o * jax.nn.silu(z)) @ w_out

def moba_mixer(h, cos, sin, w_in, w_out, q_g, k_g):
    B, S, _ = h.shape
    q, k, v, z = split_cols(h @ w_in, [Q_W, KV_W, KV_W, Q_W])
    q = partial_rope(rms_norm(q.reshape(B, S, N_HEADS, HEAD_DIM), q_g), cos, sin)
    q = q.reshape(B, S, N_KV, GQA, HEAD_DIM)
    k = partial_rope(rms_norm(k.reshape(B, S, N_KV, HEAD_DIM), k_g), cos, sin)
    v = v.reshape(B, S, N_KV, HEAD_DIM)
    scale = HEAD_DIM ** -0.5

    n_blk = -(-S // MOBA_BLOCK)
    pad = ((0, 0), (0, n_blk * MOBA_BLOCK - S), (0, 0), (0, 0))
    k_pad = jnp.pad(k, pad)
    v_pad = jnp.pad(v, pad)
    k_blk = k_pad.reshape(B, n_blk, MOBA_BLOCK, N_KV, HEAD_DIM)
    k_mean = jnp.mean(k_blk.astype(jnp.float32), axis=2).astype(k.dtype)
    k_blk_t = k_blk.transpose(0, 3, 1, 2, 4)
    v_blk_t = v_pad.reshape(B, n_blk, MOBA_BLOCK, N_KV, HEAD_DIM).transpose(0, 3, 1, 2, 4)
    k_top = min(MOBA_TOPK, n_blk - 1)
    b_i = jnp.arange(B)[:, None, None, None, None]
    g_i = jnp.arange(N_KV)[None, None, :, None, None]
    blk = jnp.arange(n_blk)
    C = MOBA_Q_BLOCK

    def q_block(ci):
        t0 = ci * C
        t = t0 + jnp.arange(C)
        qc = lax.dynamic_slice_in_dim(q, t0, C, axis=1)
        own = t0 // MOBA_BLOCK
        bstart = own * MOBA_BLOCK
        k_own = lax.dynamic_slice_in_dim(k_pad, bstart, MOBA_BLOCK, axis=1)
        v_own = lax.dynamic_slice_in_dim(v_pad, bstart, MOBA_BLOCK, axis=1)
        kpos = bstart + jnp.arange(MOBA_BLOCK)
        m_own = jnp.broadcast_to((kpos[None, :] <= t[:, None])[None, :, None, None, :],
                                 (B, C, N_KV, GQA, MOBA_BLOCK))
        s_own = jnp.einsum('bcgrd,bkgd->bcgrk', qc, k_own) * scale
        if k_top > 0:
            s_gate = jnp.einsum('bcgrd,bjgd->bcgrj', qc, k_mean).astype(jnp.float32)
            s_gate = jnp.where(blk < own, s_gate, -jnp.inf)
            _, sel = lax.top_k(s_gate, k_top)
            kg = k_blk_t[b_i, g_i, sel]
            vg = v_blk_t[b_i, g_i, sel].reshape(B, C, N_KV, GQA, k_top * MOBA_BLOCK, HEAD_DIM)
            s_past = jnp.einsum('bcgrd,bcgrkld->bcgrkl', qc, kg).reshape(B, C, N_KV, GQA, k_top * MOBA_BLOCK) * scale
            m_past = jnp.broadcast_to((sel < own)[..., None],
                                      (B, C, N_KV, GQA, k_top, MOBA_BLOCK)).reshape(B, C, N_KV, GQA, k_top * MOBA_BLOCK)
            p = masked_softmax(jnp.concatenate([s_past, s_own], axis=-1),
                               jnp.concatenate([m_past, m_own], axis=-1)).astype(v.dtype)
            n_past = k_top * MOBA_BLOCK
            return (jnp.einsum('bcgrn,bcgrnd->bcgrd', p[..., :n_past], vg)
                    + jnp.einsum('bcgrk,bkgd->bcgrd', p[..., n_past:], v_own))
        p = masked_softmax(s_own, m_own).astype(v.dtype)
        return jnp.einsum('bcgrk,bkgd->bcgrd', p, v_own)

    o = lax.map(q_block, jnp.arange(S // C))
    o = jnp.moveaxis(o, 0, 1).reshape(B, S, Q_W)
    return (o * jax.nn.silu(z)) @ w_out

def first_inputs(seed: int = 0) -> dict:
    key = jax.random.key(seed)
    ks = jax.random.split(key, 20)
    D = D_MODEL

    def nrm(k, shape, s):
        return jax.random.normal(k, shape, jnp.float32) * s

    x = nrm(ks[0], (BATCH, SEQ, D), 1.0)
    c = nrm(ks[1], (BATCH, D), 1.0)
    offset = jax.random.randint(ks[2], (BATCH, 1), 0, 4096, dtype=jnp.int32)
    positions = offset + jnp.arange(SEQ, dtype=jnp.int32)[None, :]
    return {
        "x": x,
        "c": c,
        "positions": positions,
        "norm_g": 1.0 + nrm(ks[3], (DEPTH, D), 0.02),
        "ada_w": nrm(ks[4], (DEPTH, D, 3 * D), 0.5 * D ** -0.5),
        "ada_b": nrm(ks[5], (DEPTH, 3 * D), 0.02),
        "nsa_w_in": nrm(ks[6], (N_A, D, NSA_IN), D ** -0.5),
        "nsa_w_out": nrm(ks[7], (N_A, Q_W, D), Q_W ** -0.5),
        "nsa_q_norm": 1.0 + nrm(ks[8], (N_A, HEAD_DIM), 0.02),
        "nsa_k_norm": 1.0 + nrm(ks[9], (N_A, 3, HEAD_DIM), 0.02),
        "nsa_cmp_pe": nrm(ks[10], (N_A, 2, CMP_LEN, HEAD_DIM), 0.1),
        "nsa_cmp_w1": nrm(ks[11], (N_A, 2, CMP_LEN * HEAD_DIM, CMP_HID), (CMP_LEN * HEAD_DIM) ** -0.5),
        "nsa_cmp_b1": nrm(ks[12], (N_A, 2, CMP_HID), 0.02),
        "nsa_cmp_w2": nrm(ks[13], (N_A, 2, CMP_HID, HEAD_DIM), CMP_HID ** -0.5),
        "nsa_gate_b": nrm(ks[14], (N_A, 3 * N_HEADS), 0.1),
        "moba_w_in": nrm(ks[15], (N_B, D, MOBA_IN), D ** -0.5),
        "moba_w_out": nrm(ks[16], (N_B, Q_W, D), Q_W ** -0.5),
        "moba_q_norm": 1.0 + nrm(ks[17], (N_B, HEAD_DIM), 0.02),
        "moba_k_norm": 1.0 + nrm(ks[18], (N_B, HEAD_DIM), 0.02),
    }

def first_block(x, c, positions, norm_g, ada_w, ada_b, nsa_w_in, nsa_w_out, nsa_q_norm, nsa_k_norm,
              nsa_cmp_pe, nsa_cmp_w1, nsa_cmp_b1, nsa_cmp_w2, nsa_gate_b,
              moba_w_in, moba_w_out, moba_q_norm, moba_k_norm):
    cos, sin = rope_tables(positions)
    cond = jax.nn.silu(c)
    for i in range(DEPTH):
        shift, scale, gate = jnp.split(cond @ ada_w[i] + ada_b[i], 3, axis=-1)
        h = rms_norm(x, norm_g[i]) * (1 + scale[:, None, :]) + shift[:, None, :]
        j = i // N_MIXERS
        if i % N_MIXERS == 0:
            y = nsa_mixer(h, cos, sin, positions, nsa_w_in[j], nsa_w_out[j], nsa_q_norm[j], nsa_k_norm[j],
                          nsa_cmp_pe[j], nsa_cmp_w1[j], nsa_cmp_b1[j], nsa_cmp_w2[j], nsa_gate_b[j])
        else:
            y = moba_mixer(h, cos, sin, moba_w_in[j], moba_w_out[j], moba_q_norm[j], moba_k_norm[j])
        x = x + gate[:, None, :] * y
    return x


DEPTH_2 = 1

FFN_HIDDEN = 2816
FFN_RESIDUAL_WEIGHT = 0.5

MLA_HEADS = 8
MLA_NOPE_DIM = 64
MLA_ROPE_DIM = 32
MLA_V_DIM = 64
Q_LORA_RANK = 192
KV_LORA_RANK = 128
ROPE_THETA_2 = 10000.0
MAX_POS_OFFSET = 1024

FOX_HEADS = 8
FOX_HEAD_DIM = 64
FOX_WIDTH = FOX_HEADS * FOX_HEAD_DIM
FOX_BF_MIN = 1.0
FOX_BF_MAX = 6.0

MLA_WIDTH = MLA_HEADS * MLA_V_DIM
Q_BLOCK = 128
RMS_EPS = 1e-6

IN_SPLIT_SIZES = (Q_LORA_RANK, KV_LORA_RANK, MLA_ROPE_DIM,
                  FOX_WIDTH, FOX_WIDTH, FOX_WIDTH, FOX_HEADS,
                  D_MODEL, D_MODEL)
IN_WIDTH = sum(IN_SPLIT_SIZES)


def rms_norm_2(x, gain):
    xf = x.astype(jnp.float32)
    y = xf * lax.rsqrt(jnp.mean(xf * xf, axis=-1, keepdims=True) + RMS_EPS)
    return (y * gain.astype(jnp.float32)).astype(x.dtype)

def swiglu(x, w_gate, w_up, w_down):
    return (jax.nn.silu(x @ w_gate) * (x @ w_up)) @ w_down

def rope_tables_2(positions):
    half = MLA_ROPE_DIM // 2
    inv_freq = ROPE_THETA_2 ** (-jnp.arange(half, dtype=jnp.float32) / half)
    ang = positions.astype(jnp.float32)[..., None] * inv_freq
    return jnp.cos(ang), jnp.sin(ang)

def apply_rotary(x, cos, sin):
    half = x.shape[-1] // 2
    xf = x.astype(jnp.float32)
    x1, x2 = xf[..., :half], xf[..., half:]
    return jnp.concatenate([x1 * cos - x2 * sin, x2 * cos + x1 * sin], axis=-1).astype(x.dtype)

def to_heads(t):
    return t.transpose(0, 2, 1, 3)

def from_heads(t):
    b, h, s, d = t.shape
    return t.transpose(0, 2, 1, 3).reshape(b, s, h * d)

def blocked_causal_attention(q, k, v, log_decay_cum=None):
    b, h, s, dk = q.shape
    dv = v.shape[-1]
    n_blocks = s // Q_BLOCK
    scale = dk ** -0.5
    k_pos = jnp.arange(s)

    def one_block(i):
        start = i * Q_BLOCK
        q_blk = lax.dynamic_slice_in_dim(q, start, Q_BLOCK, axis=2)
        logits = jnp.einsum('bhqd,bhkd->bhqk', q_blk, k,
                            preferred_element_type=jnp.float32) * scale
        if log_decay_cum is not None:
            c_q = lax.dynamic_slice_in_dim(log_decay_cum, start, Q_BLOCK, axis=2)
            logits = logits + (c_q[..., :, None] - log_decay_cum[..., None, :])
        q_pos = start + jnp.arange(Q_BLOCK)
        logits = jnp.where(k_pos[None, :] <= q_pos[:, None], logits, -jnp.inf)
        probs = jax.nn.softmax(logits, axis=-1)
        return jnp.einsum('bhqk,bhkd->bhqd', probs.astype(v.dtype), v)

    out = lax.map(one_block, jnp.arange(n_blocks))
    return out.transpose(1, 2, 0, 3, 4).reshape(b, h, s, dv)

def mla_mixer(q_lat, kv_lat, k_rope, cos, sin, q_lat_norm, w_qb, kv_lat_norm, w_kvb,
              q_nope_gain, q_rope_gain, k_nope_gain, k_rope_gain):
    b, s, _ = q_lat.shape
    q = (rms_norm_2(q_lat, q_lat_norm) @ w_qb).reshape(b, s, MLA_HEADS, MLA_NOPE_DIM + MLA_ROPE_DIM)
    q_nope = rms_norm_2(q[..., :MLA_NOPE_DIM], q_nope_gain)
    q_rope = apply_rotary(rms_norm_2(q[..., MLA_NOPE_DIM:], q_rope_gain),
                          cos[:, :, None, :], sin[:, :, None, :])
    kv = (rms_norm_2(kv_lat, kv_lat_norm) @ w_kvb).reshape(b, s, MLA_HEADS, MLA_NOPE_DIM + MLA_V_DIM)
    k_nope = rms_norm_2(kv[..., :MLA_NOPE_DIM], k_nope_gain)
    v = kv[..., MLA_NOPE_DIM:]
    k_r = apply_rotary(rms_norm_2(k_rope, k_rope_gain), cos, sin)
    k_r = jnp.broadcast_to(k_r[:, :, None, :], (b, s, MLA_HEADS, MLA_ROPE_DIM))
    q_full = jnp.concatenate([q_nope, q_rope], axis=-1)
    k_full = jnp.concatenate([k_nope, k_r], axis=-1)
    out = blocked_causal_attention(to_heads(q_full), to_heads(k_full), to_heads(v))
    return from_heads(out)

def fox_mixer(fq, fk, fv, f_logit, q_gain, k_gain, b_f):
    b, s, _ = fq.shape
    q = rms_norm_2(fq.reshape(b, s, FOX_HEADS, FOX_HEAD_DIM), q_gain)
    k = rms_norm_2(fk.reshape(b, s, FOX_HEADS, FOX_HEAD_DIM), k_gain)
    v = fv.reshape(b, s, FOX_HEADS, FOX_HEAD_DIM)
    log_f = jax.nn.log_sigmoid((f_logit + b_f).astype(jnp.float32))
    c = jnp.cumsum(log_f, axis=1).transpose(0, 2, 1)
    out = blocked_causal_attention(to_heads(q), to_heads(k), to_heads(v), c)
    return from_heads(out)

def second_inputs(seed: int = 0) -> dict:
    key = jax.random.key(seed)
    ks = iter(jax.random.split(key, 40))
    f32 = jnp.float32

    def w(shape, fan_in):
        return jax.random.normal(next(ks), (DEPTH_2,) + shape, f32) * (fan_in ** -0.5)

    def gain(*shape):
        return 1.0 + 0.02 * jax.random.normal(next(ks), (DEPTH_2,) + shape, f32)

    x = jax.random.normal(next(ks), (BATCH, SEQ, D_MODEL), f32)
    offsets = jax.random.randint(next(ks), (BATCH, 1), 0, MAX_POS_OFFSET, dtype=jnp.int32)
    positions = (offsets + jnp.arange(SEQ, dtype=jnp.int32)[None, :]).astype(jnp.int32)
    return {
        "x": x,
        "positions": positions,
        "ffn1_norm": gain(D_MODEL),
        "ffn1_w_gate": w((D_MODEL, FFN_HIDDEN), D_MODEL),
        "ffn1_w_up": w((D_MODEL, FFN_HIDDEN), D_MODEL),
        "ffn1_w_down": w((FFN_HIDDEN, D_MODEL), FFN_HIDDEN),
        "mix_norm": gain(D_MODEL),
        "w_in": w((D_MODEL, IN_WIDTH), D_MODEL),
        "mla_q_lat_norm": gain(Q_LORA_RANK),
        "mla_w_qb": w((Q_LORA_RANK, MLA_HEADS * (MLA_NOPE_DIM + MLA_ROPE_DIM)), Q_LORA_RANK),
        "mla_kv_lat_norm": gain(KV_LORA_RANK),
        "mla_w_kvb": w((KV_LORA_RANK, MLA_HEADS * (MLA_NOPE_DIM + MLA_V_DIM)), KV_LORA_RANK),
        "mla_q_nope_gain": gain(MLA_NOPE_DIM),
        "mla_q_rope_gain": gain(MLA_ROPE_DIM),
        "mla_k_nope_gain": gain(MLA_NOPE_DIM),
        "mla_k_rope_gain": gain(MLA_ROPE_DIM),
        "fox_q_gain": gain(FOX_HEAD_DIM),
        "fox_k_gain": gain(FOX_HEAD_DIM),
        "fox_b_f": jax.random.uniform(next(ks), (DEPTH_2, FOX_HEADS), f32, FOX_BF_MIN, FOX_BF_MAX),
        "w_branch_mla": w((MLA_WIDTH, D_MODEL), MLA_WIDTH),
        "w_branch_fox": w((FOX_WIDTH, D_MODEL), FOX_WIDTH),
        "b_gate": 0.02 * jax.random.normal(next(ks), (DEPTH_2, 2, D_MODEL), f32),
        "w_o": w((D_MODEL, D_MODEL), D_MODEL),
        "ffn2_norm": gain(D_MODEL),
        "ffn2_w_gate": w((D_MODEL, FFN_HIDDEN), D_MODEL),
        "ffn2_w_up": w((D_MODEL, FFN_HIDDEN), D_MODEL),
        "ffn2_w_down": w((FFN_HIDDEN, D_MODEL), FFN_HIDDEN),
    }

def second_block(x, positions, ffn1_norm, ffn1_w_gate, ffn1_w_up, ffn1_w_down, mix_norm, w_in,
              mla_q_lat_norm, mla_w_qb, mla_kv_lat_norm, mla_w_kvb, mla_q_nope_gain,
              mla_q_rope_gain, mla_k_nope_gain, mla_k_rope_gain, fox_q_gain, fox_k_gain,
              fox_b_f, w_branch_mla, w_branch_fox, b_gate, w_o, ffn2_norm, ffn2_w_gate,
              ffn2_w_up, ffn2_w_down):
    split_points = [int(p) for p in np.cumsum(IN_SPLIT_SIZES)[:-1]]
    cos, sin = rope_tables_2(positions)
    for l in range(DEPTH_2):
        x = x + FFN_RESIDUAL_WEIGHT * swiglu(rms_norm_2(x, ffn1_norm[l]),
                                             ffn1_w_gate[l], ffn1_w_up[l], ffn1_w_down[l])
        h = rms_norm_2(x, mix_norm[l])
        proj = h @ w_in[l]
        (q_lat, kv_lat, k_rope, fq, fk, fv, f_logit,
         g_mla, g_fox) = jnp.split(proj, split_points, axis=-1)
        y_mla = mla_mixer(q_lat, kv_lat, k_rope, cos, sin, mla_q_lat_norm[l], mla_w_qb[l],
                          mla_kv_lat_norm[l], mla_w_kvb[l], mla_q_nope_gain[l],
                          mla_q_rope_gain[l], mla_k_nope_gain[l], mla_k_rope_gain[l])
        y_fox = fox_mixer(fq, fk, fv, f_logit, fox_q_gain[l], fox_k_gain[l], fox_b_f[l])
        mixed = (jax.nn.sigmoid(g_mla + b_gate[l, 0]) * (y_mla @ w_branch_mla[l])
                 + jax.nn.sigmoid(g_fox + b_gate[l, 1]) * (y_fox @ w_branch_fox[l]))
        x = x + mixed @ w_o[l]
        x = x + FFN_RESIDUAL_WEIGHT * swiglu(rms_norm_2(x, ffn2_norm[l]),
                                             ffn2_w_gate[l], ffn2_w_up[l], ffn2_w_down[l])
    return x


def setup_inputs(seed=0):
    out = dict(first_inputs(seed))
    for name, value in second_inputs(seed + 1).items():
        if name != "x":
            out[name + "_2"] = value
    return out


def reference(
    x, c, positions, norm_g, ada_w, ada_b, nsa_w_in, nsa_w_out, nsa_q_norm, nsa_k_norm,
    nsa_cmp_pe, nsa_cmp_w1, nsa_cmp_b1, nsa_cmp_w2, nsa_gate_b, moba_w_in, moba_w_out,
    moba_q_norm, moba_k_norm, positions_2, ffn1_norm_2, ffn1_w_gate_2, ffn1_w_up_2,
    ffn1_w_down_2, mix_norm_2, w_in_2, mla_q_lat_norm_2, mla_w_qb_2, mla_kv_lat_norm_2,
    mla_w_kvb_2, mla_q_nope_gain_2, mla_q_rope_gain_2, mla_k_nope_gain_2, mla_k_rope_gain_2,
    fox_q_gain_2, fox_k_gain_2, fox_b_f_2, w_branch_mla_2, w_branch_fox_2, b_gate_2, w_o_2,
    ffn2_norm_2, ffn2_w_gate_2, ffn2_w_up_2, ffn2_w_down_2,
):
    x = first_block(
        x, c, positions, norm_g, ada_w, ada_b, nsa_w_in, nsa_w_out, nsa_q_norm, nsa_k_norm,
        nsa_cmp_pe, nsa_cmp_w1, nsa_cmp_b1, nsa_cmp_w2, nsa_gate_b, moba_w_in, moba_w_out,
        moba_q_norm, moba_k_norm,
    )
    return second_block(
        x, positions_2, ffn1_norm_2, ffn1_w_gate_2, ffn1_w_up_2, ffn1_w_down_2, mix_norm_2,
        w_in_2, mla_q_lat_norm_2, mla_w_qb_2, mla_kv_lat_norm_2, mla_w_kvb_2, mla_q_nope_gain_2,
        mla_q_rope_gain_2, mla_k_nope_gain_2, mla_k_rope_gain_2, fox_q_gain_2, fox_k_gain_2,
        fox_b_f_2, w_branch_mla_2, w_branch_fox_2, b_gate_2, w_o_2, ffn2_norm_2, ffn2_w_gate_2,
        ffn2_w_up_2, ffn2_w_down_2,
    )


_drawn_inputs = setup_inputs


def setup_inputs(seed=0):
    import zlib

    import numpy as np

    out = dict(_drawn_inputs(seed))
    spreads = {}
    factors = {'norm_g': 8.0,
     'ada_b': 5.153,
     'nsa_q_norm': 8.0,
     'nsa_k_norm': 8.0,
     'nsa_cmp_pe': 7.2,
     'nsa_cmp_b1': 8.0,
     'nsa_gate_b': 8.0,
     'moba_q_norm': 8.0,
     'moba_k_norm': 8.0,
     'ffn1_norm_2': 6.582,
     'mix_norm_2': 8.0,
     'mla_q_lat_norm_2': 8.0,
     'mla_kv_lat_norm_2': 22.754,
     'mla_q_nope_gain_2': 22.884,
     'mla_q_rope_gain_2': 27.446,
     'mla_k_nope_gain_2': 21.895,
     'mla_k_rope_gain_2': 32.736,
     'fox_q_gain_2': 8.0,
     'fox_k_gain_2': 8.0,
     'b_gate_2': 64.0,
     'ffn2_norm_2': 25.868}
    for name, (base, spread) in spreads.items():
        noise = np.random.default_rng([zlib.crc32(name.encode()), seed]).standard_normal(out[name].shape)
        drawn = base * np.exp(spread * noise) if base else spread * noise
        out[name] = __import__('jax').numpy.asarray(drawn.astype(out[name].dtype))
    for name, factor in factors.items():
        out[name] = (out[name] * factor).astype(out[name].dtype)
    return out
```

```python
import numpy as np
import concourse.bass as bass
from concourse import mybir
from concourse.alu_op_type import AluOpType as ALU
from contextlib import ExitStack

F32, F32R, I32 = mybir.dt.float32, mybir.dt.float32r, mybir.dt.int32
ACT = mybir.ActivationFunctionType
AX = mybir.AxisListType

P = 128
D = 1024
S = 256
TT = S // P
KT = D // P
HD = 64
NH, NKV = 16, 4
NP = NH // 2
FFN = 2816
FT = FFN // P
CMP_LEN, CMP_STRIDE = 32, 16
NCMP = (S - CMP_LEN) // CMP_STRIDE + 1
CPAD = 32
CJ = CMP_LEN // 2
MH, MN, MR = 8, 64, 32
MQ = MN + MR
FH, FK = 8, HD + 2
QL, KVL = 192, 128
LAT = QL + KVL + MR + FH
EPS = 1e-6
NEG, FLOOR = -1e30, -1e29
UNIT = 2048
TWO_PI = 6.283185307179586
PI_PARTS = (6.28125, 0.0019340515136718750, 1.2554228305816650e-06)
PI_PARTS = PI_PARTS + (TWO_PI - sum(PI_PARTS),)
PI_LOW = 3.1415925
ROUND = 12582912.0


def chunk_list():
    ada = lambda i: [(f"ada{i}_{n}", KT, 512, False) for n in range(6)]
    ffn = lambda i: ([(f"ffn{i}_up{n}", KT, 512, True) for n in range(FT // 2)]
                     + [(f"ffn{i}_down{n}", FT, 512, True) for n in range(2)])
    two = lambda name, k: [(f"{name}{n}", k, 512, True) for n in range(2)]
    return (ada(0)
            + [("nsa_kcvc", KT, 512, True), ("nsa_gate", KT, 48, True)] + two("nsa_q", KT)
            + [("nsa_kskw", KT, 512, True), ("nsa_vsvw", KT, 512, True)]
            + [("cmp_w1_0", CJ, 256, False), ("cmp_w1_1", CJ, 256, False)]
            + two("nsa_z", KT) + ada(1) + two("nsa_out", KT)
            + two("moba_q", KT) + [("moba_kv", KT, 512, True)] + two("moba_z", KT) + two("moba_out", KT)
            + ffn(1)
            + [("mix_lat", KT, LAT, True), ("mla_qn", 2, 512, True), ("mla_qr", 2, 256, True),
               ("mla_kn", 1, 512, True), ("mla_v", 1, 512, True),
               ("fox_q", KT, 512, True), ("fox_k", KT, 512, True), ("fox_v", KT, 512, True)]
            + two("gate_mla", KT) + two("gate_fox", KT)
            + two("br_mla", KT // 2) + two("br_fox", KT // 2) + two("mix_out", KT)
            + ffn(2))


def unit_list():
    units, at = [], 0
    for name, kt, n, split in chunk_list():
        per = UNIT // n
        for k in range(0, kt, per):
            m = min(per, kt - k)
            units.append((name, k, m, n, split, at))
            at += m * n
    return units, at


def layout(sizes):
    at, out = 0, {}
    for name, n in sizes:
        out[name] = (at, at + n)
        at += n
    return out, at


COLS, NCOLS = layout([("c", KT), ("norm0", KT), ("norm1", KT), ("ada0", 3 * KT), ("ada1", 3 * KT),
                      ("ffn1", KT), ("mix", KT), ("ffn2", KT), ("gate_mla", KT), ("gate_fox", KT),
                      ("b1_0", 2), ("b1_1", 2), ("q_lat", 2), ("kv_lat", 1), ("pe0", CJ), ("pe1", CJ),
                      ("w2_0", 2 * HD), ("w2_1", 2 * HD)])
ROWS, NROWS = layout([("nsa_q", HD), ("nsa_kc", HD), ("nsa_ks", HD), ("nsa_kw", HD), ("gate_b", 3 * NH),
                      ("moba_q", HD), ("moba_k", HD), ("mla_qn", MN), ("mla_qr", MR), ("mla_kn", MN),
                      ("mla_kr", MR), ("fox_q", HD), ("fox_k", HD), ("fox_bf", FH)])
ANG, NANG = layout([("tok", TT * 8), ("cmp", 8), ("tok2", TT * 16)])
CONST, NCONST = layout([("ident", P), ("causal", S), ("pair", P // 2), ("parity", 2), ("cmp_mask", TT * CPAD),
                        ("upto", P), ("ones", P), ("freq", NANG), ("lat_eps", 3)])


def shape_constants():
    c = np.zeros((P, NCONST), np.float32)
    put = lambda name, a: c.__setitem__((slice(None), slice(*CONST[name])), a)
    p = np.arange(P)[:, None]
    put("ident", np.eye(P))
    put("causal", np.where(np.arange(S)[None, :] - P <= p, 0.0, NEG))
    put("pair", p // 2 == np.arange(P // 2)[None, :])
    put("parity", p % 2 == np.arange(2)[None, :])
    ends = np.arange(CPAD) * CMP_STRIDE + CMP_LEN - 1
    ok = (ends[None, None, :] <= p[:, :, None] + P * np.arange(TT)[None, :, None]) & (np.arange(CPAD) < NCMP)
    put("cmp_mask", np.where(ok, 0.0, NEG).reshape(P, -1))
    put("upto", p <= np.arange(P)[None, :])
    put("ones", 1.0)
    f1 = np.float32(500000.0) ** (-np.arange(0, 16, 2, dtype=np.float32) / np.float32(16))
    f2 = np.float32(10000.0) ** (-np.arange(16, dtype=np.float32) / np.float32(16))
    put("freq", np.concatenate([np.tile(f1, TT), f1, np.tile(f2, TT)])[None, :])
    return c


class Engine:

    def __init__(self, sem):
        self.sem, self.count, self.steps = sem, 0, []

    def __call__(self, waits, emit):
        self.count += 1
        self.steps.append((list(waits), emit))
        return (self.sem, self.count)

    def run(self, eng):
        met = {}
        for waits, emit in self.steps:
            for sem, value in waits:
                if met.get(sem.name, 0) < value:
                    eng.wait_ge(sem, value)
                    met[sem.name] = value
            emit(eng).then_inc(self.sem, 1)


class Buf:

    def __init__(self, t):
        self.t, self.free = t, []


def drain_steps(gen):
    while True:
        try:
            next(gen)
        except StopIteration as e:
            return e.value


def program(nc, wts, cols_d, rows_d, const_d, pos_d, x_d, out_d):
    units, _ = unit_list()
    ctx = ExitStack()
    with ctx:
        sem = lambda n: ctx.enter_context(nc.semaphore(n))

        def sb(name, shape, dt=F32, on=ctx):
            return on.enter_context(nc.sbuf_tensor(name, shape, dt))

        PE, VE, SE, GP = (Engine(sem(n)) for n in ("pe_done", "dve_done", "act_done", "pool_done"))
        sync_steps = []

        NRAW, NSPLIT = 4, 2
        raw = [Buf(sb(f"w_raw{i}", [P, UNIT])) for i in range(NRAW)]
        raw_sem = [sem(f"w_raw{i}_in") for i in range(NRAW)]
        w_hi = [Buf(sb(f"w_hi{i}", [P, UNIT], F32R)) for i in range(NSPLIT)]
        w_lo = [sb(f"w_lo{i}", [P, UNIT], F32R) for i in range(NSPLIT)]
        x = sb("x", [P, TT, D])
        h_hi, h_lo = (sb(n, [P, KT, S], F32R) for n in ("h_hi", "h_lo"))
        scr = sb("scr", [P, TT, D])
        gate_row = sb("gate_row", [P, D])
        cols, rows, const = sb("cols", [P, NCOLS]), sb("rows", [P, NROWS]), sb("const", [P, NCONST])
        pos = sb("pos", [P, NANG], I32)
        ada = sb("ada", [P, 2, 3 * KT])
        cond = sb("cond", [P, KT])
        stats = sb("stats", [P, 1100])
        tmp = [Buf(sb(f"tmp{i}", [P, 512])) for i in range(2)]
        banks = [Buf(ctx.enter_context(nc.psum_tensor(f"bank{i}", [P, 512], F32))) for i in range(8)]

        col = lambda n: cols[:, COLS[n][0]:COLS[n][1]]
        row = lambda n: rows[:, ROWS[n][0]:ROWS[n][1]]
        con = lambda n: const[:, CONST[n][0]:CONST[n][1]]
        ident = con("ident")

        used = [0]

        def stat(n):
            used[0] += n
            assert used[0] <= 1100
            return stats[:, used[0] - n:used[0]]

        def load(dst, src, name):
            s = sem(name)
            sync_steps.append(([], lambda e: e.dma_start(dst, src).then_inc(s, 16)))
            return (s, 16)

        const_in = load(const[:, :], const_d, "const_in")
        cols_in = load(cols[:, :], cols_d, "cols_in")

        fetched, split_done, turn = {}, {}, {}
        next_split = [0, 0]

        def fetch(u):
            if u >= len(units):
                return
            _, _, m, n, _, at = units[u]
            b, s = raw[u % NRAW], raw_sem[u % NRAW]
            sync_steps.append((list(b.free), lambda e: e.dma_start(
                b.t[:, 0:m * n], wts[:, at:at + m * n]).then_inc(s, 16)))
            fetched[u] = (s, 16 * (u // NRAW + 1))

        def split(u):
            _, _, m, n, _, _ = units[u]
            i = next_split[1] % NSPLIT
            next_split[1] += 1
            r, hi, lo = raw[u % NRAW], w_hi[i], w_lo[i]
            c = m * n
            a = SE([fetched[u], *hi.free], lambda e: e.activation(hi.t[:, 0:c], r.t[:, 0:c], ACT.Copy))
            b = VE([a, *hi.free], lambda e: e.tensor_tensor(lo[:, 0:c], r.t[:, 0:c], hi.t[:, 0:c].bitcast(F32),
                                                            ALU.subtract))
            r.free = [b]
            turn[u], split_done[u] = i, [a, b]
            fetch(u + NRAW)

        taken = [0]

        def take(name):
            u = taken[0]
            taken[0] += 1
            assert units[u][0] == name, (units[u][0], name)
            while next_split[0] <= min(u + 1, len(units) - 1):
                v = next_split[0]
                next_split[0] += 1
                if units[v][4]:
                    split(v)
            return u

        def used_split(u, t):
            w_hi[turn[u]].free = [t]

        def used_raw(u, t):
            raw[u % NRAW].free = [t]
            fetch(u + NRAW)

        acc_turn = [0]

        def acc_pair():
            acc_turn[0] += 1
            i = 2 * (acc_turn[0] % 2)
            return banks[i], banks[i + 1]

        def chunk_size(name):
            return next((kt, n) for c, kt, n, _ in chunk_list() if c == name)

        def linear(name, lhs, ready, tokens_out, k0=0):
            pair = acc_pair()
            hi, lo = lhs
            kts, n = chunk_size(name)
            done, k, ticket = 0, 0, None
            while k < kts:
                u = take(name)
                _, _, m, _, _, _ = units[u]
                wh, wl = w_hi[turn[u]].t, w_lo[turn[u]]

                def products(e, k=k, m=m, wh=wh, wl=wl):
                    for kk in range(m):
                        a = k0 + k + kk
                        if tokens_out:
                            for t in range(TT):
                                o = pair[t].t[:, 0:n]
                                xs = [z[:, a, t * P:(t + 1) * P] for z in (hi, lo)]
                                ws = [z[:, kk * n:(kk + 1) * n] for z in (wh, wl)]
                                for i, (q, w) in enumerate(((0, 0), (0, 1), (1, 0))):
                                    mm = e.matmul(o, xs[q], ws[w], start=(k + kk == 0 and i == 0),
                                                  stop=(k + kk == kts - 1 and i == 2))
                        else:
                            for b in range(n // P):
                                o = pair[b // 2].t[:, (b % 2) * S:(b % 2) * S + S]
                                xs = [z[:, a, :] for z in (hi, lo)]
                                ws = [z[:, kk * n + b * P:kk * n + (b + 1) * P] for z in (wh, wl)]
                                for i, (w, q) in enumerate(((0, 0), (0, 1), (1, 0))):
                                    mm = e.matmul(o, ws[w], xs[q], start=(k + kk == 0 and i == 0 and b % 2 == 0),
                                                  stop=(k + kk == kts - 1 and i == 2 and b % 2 == 1),
                                                  skip_group_check=True)
                    return mm

                waits = [*split_done[u], *ready] + (pair[0].free + pair[1].free if k == 0 else [])
                ticket = PE(waits, products)
                used_split(u, ticket)
                k += m
                yield
            return pair, ticket

        aux_turn = [0]

        def aux():
            aux_turn[0] += 1
            return banks[4 + aux_turn[0] % 3]

        def transposes(bank, waits, parts):
            def emit(e):
                for o, src in parts:
                    mm = e.transpose(bank.t[0:src.shape[1], o:o + src.shape[0]], src, ident)
                return mm
            return PE([*waits, *bank.free, const_in], emit)

        def split_to(hi, lo, src, waits, scale=1.0):
            a = SE(waits, lambda e: e.activation(hi, src, ACT.Copy, scale=scale))
            b = VE([a, *waits], lambda e: e.scalar_tensor_tensor(lo, src, scale, hi.bitcast(F32), ALU.mult,
                                                                 ALU.subtract))
            return [a, b]

        tmp_turn = [0]

        def scratch():
            tmp_turn[0] += 1
            return tmp[tmp_turn[0] % 2]

        minus_half = stat(2 * NH)
        fill = GP([], lambda e: e.memset(minus_half, -0.5))

        def rsqrt(out, ms, waits):
            n = ms.shape[1]
            a = GP([*waits, fill], lambda e: e.tensor_scalar(ms, ms, EPS, None, ALU.add))
            return GP([a], lambda e: e.tensor_tensor(out, ms, minus_half[:, 0:n], ALU.pow))

        scr_buf = Buf(scr)

        def norm(ready, sc, sh=None, sc_ready=()):
            ms, rs = stat(TT), stat(TT)
            sq = [SE([*ready, *scr_buf.free], lambda e, t=t: e.activation(
                scr[:, t, :], x[:, t, :], ACT.Square, scale=D ** -0.5, accum_out=ms[:, t:t + 1])) for t in range(TT)]
            r = rsqrt(rs, ms, sq)
            xn = [VE([r, *ready], lambda e, t=t: e.tensor_scalar(scr[:, t, :], x[:, t, :], rs[:, t:t + 1], None,
                                                                 ALU.mult)) for t in range(TT)]
            out = []
            for k in range(0, KT, 2):
                b = aux()
                tr = transposes(b, xn, [((kk - k) * S + t * P, scr[:, t, kk * P:(kk + 1) * P])
                                        for kk in (k, k + 1) for t in range(TT)])
                v = scratch()
                for i, kk in enumerate((k, k + 1)):
                    src, dst = b.t[:, i * S:(i + 1) * S], v.t[:, i * S:(i + 1) * S]
                    w = [tr, *v.free, *sc_ready]
                    if sh is None:
                        last = VE(w, lambda e, s=src, d=dst, kk=kk: e.tensor_scalar(
                            d, s, sc[:, kk:kk + 1], None, ALU.mult))
                    else:
                        last = VE(w, lambda e, s=src, d=dst, kk=kk: e.tensor_scalar(
                            d, s, sc[:, kk:kk + 1], sh[:, kk:kk + 1], ALU.mult, ALU.add))
                b.free = [last]
                out = split_to(h_hi[:, k:k + 2, :], h_lo[:, k:k + 2, :],
                               v.t[:, :].rearrange("p (k t) -> p k t", k=2), [last])
                v.free = out
            scr_buf.free = [tr]
            return out

        def bcast(a, shape):
            return a.to_broadcast(shape)

        sq_buf = Buf(sb("squares", [P, TT, 512]))

        def head_norm(pair, ready, parts, heads, dim, c0=0):
            ms, rs = stat(TT * heads), stat(TT * heads)
            tr = []
            for t in range(TT):
                src = pair[t].t[:, c0:c0 + heads * dim]
                a = SE([*ready, *sq_buf.free], lambda e, t=t, s=src: e.activation(
                    sq_buf.t[:, t, 0:heads * dim], s, ACT.Square, scale=dim ** -0.5))
                tr.append(VE([a], lambda e, t=t: e.reduce_sum(
                    ms[:, t * heads:(t + 1) * heads],
                    sq_buf.t[:, t, 0:heads * dim].rearrange("p (h d) -> p h d", d=dim), AX.X)))
            sq_buf.free = tr
            r = rsqrt(rs, ms, tr)
            out = []
            for t in range(TT):
                for h0, n, gain, dst in parts:
                    src = pair[t].t[:, c0 + h0 * dim:c0 + (h0 + n) * dim].rearrange("p (h d) -> p h d", d=dim)
                    rr = rs[:, t * heads + h0:t * heads + h0 + n].unsqueeze(2)
                    a = VE([r, *ready], lambda e, s=src, rr=rr, d=dst(t), n=n: e.tensor_tensor(
                        d, s, bcast(rr, [P, n, dim]), ALU.mult))
                    out.append(VE([a, rows_in], lambda e, d=dst(t), g=gain, n=n: e.tensor_tensor(
                        d, d, bcast(g.unsqueeze(1), [P, n, dim]), ALU.mult)))
            return out

        def rope(v, cs, sn, n, dim, ready):
            half = dim // 2
            t1, t2 = scratch(), scratch()
            a1 = t1.t[:, 0:n * dim].rearrange("p (h d) -> p h d", d=dim)
            a2 = t2.t[:, 0:n * dim].rearrange("p (h d) -> p h d", d=dim)
            s = lambda z, a, b: bcast(z[:, a:b].unsqueeze(1), [P, n, b - a])
            w = [*ready, trig]
            i = VE([*w, *t1.free], lambda e: e.tensor_tensor(a1, v, s(cs, 0, dim), ALU.mult))
            j = VE([*w, *t2.free], lambda e: e.tensor_tensor(a2[:, :, 0:half], v[:, :, half:dim], s(sn, 0, half),
                                                             ALU.mult))
            k = VE([*w, *t2.free], lambda e: e.tensor_tensor(a2[:, :, half:dim], v[:, :, 0:half],
                                                             s(sn, half, dim), ALU.mult))
            last = VE([i, j, k], lambda e: e.tensor_tensor(v, a1, a2, ALU.add))
            t1.free = t2.free = [last]
            return last

        fetch(0)
        x_in = load(x[:, :, :], x_d.rearrange("o (t p) d -> p (o t) d", p=P), "x_in")
        pos_in = load(pos[:, :], pos_d, "pos_in")
        rows_in = load(rows[:, :], rows_d.to_broadcast([P, NROWS]), "rows_in")
        for u in range(1, NRAW):
            fetch(u)

        cond_in = SE([cols_in], lambda e: e.activation(cond[:, :], col("c"), ACT.Silu))

        ang, turns, sin_t, cos_t = (sb(n, [P, NANG]) for n in ("ang", "turns", "sin_t", "cos_t"))
        a = VE([pos_in, const_in], lambda e: e.tensor_copy(ang[:, :], pos[:, :]))
        a = VE([a], lambda e: e.tensor_tensor(ang[:, :], ang[:, :], con("freq"), ALU.mult))
        a = VE([a], lambda e: e.tensor_scalar(turns[:, :], ang[:, :], 1.0 / TWO_PI, None, ALU.mult))
        a = VE([a], lambda e: e.tensor_scalar(turns[:, :], turns[:, :], ROUND, None, ALU.add))
        a = VE([a], lambda e: e.tensor_scalar(turns[:, :], turns[:, :], -ROUND, None, ALU.add))
        for part in PI_PARTS:
            a = VE([a], lambda e, c=part: e.scalar_tensor_tensor(ang[:, :], turns[:, :], -c, ang[:, :], ALU.mult,
                                                                 ALU.add))
        b = VE([a], lambda e: e.tensor_scalar(cos_t[:, :], ang[:, :], TWO_PI / 4, None, ALU.add))
        c = VE([b], lambda e: e.tensor_scalar(turns[:, :], cos_t[:, :], TWO_PI / 2, -TWO_PI, ALU.is_gt, ALU.mult))
        c = VE([c], lambda e: e.tensor_tensor(cos_t[:, :], cos_t[:, :], turns[:, :], ALU.add))
        c = VE([c], lambda e: e.tensor_scalar(cos_t[:, :], cos_t[:, :], PI_LOW, -PI_LOW, ALU.min, ALU.max))
        a = VE([a], lambda e: e.tensor_scalar(ang[:, :], ang[:, :], PI_LOW, -PI_LOW, ALU.min, ALU.max))
        sin_in = SE([a, c], lambda e: e.activation(sin_t[:, :], ang[:, :], ACT.Sin))
        cos_in = SE([c], lambda e: e.activation(cos_t[:, :], cos_t[:, :], ACT.Sin))
        cs1, sn1 = (sb(n, [P, TT + 1, 2, 8]) for n in ("cs1", "sn1"))
        cs2, sn2 = (sb(n, [P, TT, 2, 16]) for n in ("cs2", "sn2"))
        for cs, sn, n, w, lo in ((cs1, sn1, TT + 1, 8, 0), (cs2, sn2, TT, 16, (TT + 1) * 8)):
            ca = cos_t[:, lo:lo + n * w].rearrange("p (t f) -> p t f", f=w)
            sa = sin_t[:, lo:lo + n * w].rearrange("p (t f) -> p t f", f=w)
            for i in range(2):
                trig = VE([cos_in], lambda e, d=cs[:, :, i, :], s=ca: e.tensor_copy(d, s))
                trig = VE([sin_in], lambda e, d=sn[:, :, i, :], s=sa, i=i: e.tensor_scalar(
                    d, s, 2.0 * i - 1.0, None, ALU.mult))
        table = lambda z, t: z[:, t, :, :].rearrange("p a f -> p (a f)")

        ada_done, gate_cols = {}, {}

        def adaptive(i):
            last = []
            for n in range(6):
                pair = acc_pair()
                bank = pair[0]
                for half in range(2):
                    u = take(f"ada{i}_{n}")
                    m = units[u][2]

                    def products(e, half=half, m=m, w=raw[u % NRAW].t, bank=bank):
                        for kk in range(m):
                            for b in range(4):
                                mm = e.matmul(bank.t[:, b:b + 1], w[:, kk * 512 + b * P:kk * 512 + (b + 1) * P],
                                              cond[:, half * m + kk:half * m + kk + 1],
                                              start=(half == 0 and kk == 0 and b == 0),
                                              stop=(half == 1 and kk == m - 1 and b == 3), skip_group_check=True)
                        return mm

                    t = PE([fetched[u], cond_in, *(bank.free if half == 0 else [])], products)
                    used_raw(u, t)
                    if half == 0:
                        yield
                bias = col(f"ada{i}")
                e_ = VE([t, cols_in], lambda e, n=n, bank=bank: e.tensor_tensor(
                    ada[:, i, 4 * n:4 * n + 4], bank.t[:, 0:4], bias[:, 4 * n:4 * n + 4], ALU.add))
                bank.free = [e_]
                last = [e_]
                if n == 3:
                    ada_done[i] = VE([e_], lambda e: e.scalar_tensor_tensor(
                        ada[:, i, KT:2 * KT], ada[:, i, KT:2 * KT], 1.0, col(f"norm{i}"), ALU.add, ALU.mult))
                yield
            gate_cols[i] = last

        def gate_as_row(i):
            pair = acc_pair()

            def spread(e):
                for k in range(KT):
                    mm = e.matmul(pair[k // 4].t[:, (k % 4) * P:(k % 4 + 1) * P],
                                  ada[:, i, 2 * KT + k:2 * KT + k + 1].to_broadcast([P, P]), ident,
                                  start=True, stop=True)
                return mm

            t = PE([*gate_cols[i], const_in, *pair[0].free, *pair[1].free], spread)
            cp = [SE([t, *gate_free], lambda e, j=j: e.activation(gate_row[:, j * 512:(j + 1) * 512],
                                                                  pair[j].t[:, :], ACT.Copy)) for j in range(2)]
            pair[0].free, pair[1].free = [cp[0]], [cp[1]]
            gate_ready[:] = cp
            yield

        gate_ready, gate_free = [], []

        def attention(items, pt, sm, o_bank, background, per_slot):
            state = {}

            def scores(i):
                it, bank, m = items[i], banks[4 + i % 2], sm[i % len(sm)]
                mx, ng, su, rc = (stat(TT) for _ in range(4))

                def emit(e):
                    e.matmul(bank.t[:, 0:P], it["q"](0), it["k"](P), start=True, stop=True)
                    return e.matmul(bank.t[:, P:3 * P], it["q"](1), it["k"](S), start=True, stop=True)

                t = PE([*it["ready"], *bank.free], emit)
                mask = con("causal")
                a = VE([t, *m.free], lambda e: e.tensor_tensor_reduce(
                    m.t[:, 0:P], bank.t[:, 0:P], mask[:, P:S], 1.0, -3e38, ALU.add, ALU.max, mx[:, 0:1]))
                b = VE([t, *m.free], lambda e: e.tensor_tensor_reduce(
                    m.t[:, P:3 * P], bank.t[:, P:3 * P], mask, 1.0, -3e38, ALU.add, ALU.max, mx[:, 1:2]))
                bank.free = [b]
                c = VE([a, b], lambda e: e.tensor_scalar(ng, mx, -it["scale"], None, ALU.mult))
                d = SE([c], lambda e: e.activation(m.t[:, 0:P], m.t[:, 0:P], ACT.Exp, bias=ng[:, 0:1],
                                                   scale=it["scale"], accum_out=su[:, 0:1]))
                d = SE([c], lambda e: e.activation(m.t[:, P:3 * P], m.t[:, P:3 * P], ACT.Exp, bias=ng[:, 1:2],
                                                   scale=it["scale"], accum_out=su[:, 1:2]))
                state[i] = [m, su, rc, d]

            def divide(i):
                it = items[i]
                m, su, rc, d = state[i]
                a = VE([d], lambda e: e.reciprocal(rc, su))
                if it["gate"] is not None:
                    a = VE([a, *it["gate_ready"]], lambda e: e.tensor_tensor(rc, rc, it["gate"], ALU.mult))
                b = VE([a], lambda e: e.tensor_scalar(m.t[:, 0:P], m.t[:, 0:P], rc[:, 0:1], None, ALU.mult))
                b = VE([a], lambda e: e.tensor_scalar(m.t[:, P:3 * P], m.t[:, P:3 * P], rc[:, 1:2], None, ALU.mult))
                state[i].append(b)

            def turn_over(i):
                m, p, bank = state[i][0], pt[i % len(pt)], banks[6]
                t = transposes(bank, [state[i][-1]], [(0, m.t[:, 0:P]), (P, m.t[:, P:2 * P]),
                                                      (2 * P, m.t[:, 2 * P:3 * P])])
                m.free = [t]
                a = SE([t, *p.free], lambda e: e.activation(p.t[:, :], bank.t[:, 0:3 * P], ACT.Copy))
                bank.free = [a]
                state[i] = [p, a]

            def values(i):
                it = items[i]
                p, a = state.pop(i)
                o = it["out"]

                def emit(e):
                    if it["before"]:
                        it["before"](e)
                    e.matmul(o, it["v"](0), p.t[:, 0:S], start=it["first"] and not it["before"], stop=False,
                             skip_group_check=True)
                    return e.matmul(o[:, P:S], it["v"](1), p.t[:, S:S + P], start=False, stop=it["last"],
                                    skip_group_check=True)

                t = PE([a, *it["v_ready"], *(it["o_buf"].free if it["first"] else [])], emit)
                p.free = [t]
                if it["close"]:
                    it["close"](t)

            n = len(items)
            for i in range(n + 2):
                if 0 <= i - 1 < n:
                    divide(i - 1)
                if i < n:
                    scores(i)
                if 0 <= i - 1 < n:
                    turn_over(i - 1)
                if 0 <= i - 2 < n:
                    values(i - 2)
                for _ in range(per_slot):
                    next(background, None)
            for _ in background:
                pass

        def gqa_item(q_t, k_t, pr, half, v, ready, v_ready, o_buf, out, **more):
            hs = slice(half * HD, (half + 1) * HD)
            return dict(q=lambda t: q_t[hs, pr, t * P:(t + 1) * P], k=lambda n: k_t[hs, 0:n], v=v, ready=ready,
                        v_ready=v_ready, scale=HD ** -0.5, o_buf=o_buf, out=out, **more)

        def residual(names, lhs, ready, scale, x_ready, src=None):
            last = []
            for j, name in enumerate(names):
                pair, t = yield from linear(name, lhs, ready, True)
                for tt in range(TT):
                    o = x[:, tt, j * 512:(j + 1) * 512]
                    if scale is None:
                        v = scratch()
                        a = VE([t, *gate_ready, *v.free], lambda e, v=v, tt=tt, j=j, pair=pair: e.tensor_tensor(
                            v.t[:, :], pair[tt].t[:, :], gate_row[:, j * 512:(j + 1) * 512], ALU.mult))
                        b = VE([a, *x_ready], lambda e, v=v, o=o: e.tensor_tensor(o, o, v.t[:, :], ALU.add))
                        v.free = [b]
                        pair[tt].free = [a]
                    else:
                        b = VE([t, *x_ready], lambda e, o=o, tt=tt, pair=pair: e.scalar_tensor_tensor(
                            o, pair[tt].t[:, :], scale, o, ALU.mult, ALU.add))
                        pair[tt].free = [b]
                    last.append(b)
            return last

        mix = ExitStack()
        tokq = sb("tokq", [P, TT, 1024], on=mix)
        tokk = sb("tokk", [P, TT, MH * MQ], on=mix)
        tokv = sb("tokv", [P, TT, 1024], on=mix)
        q_t = sb("q_t", [P, NP, S], on=mix)
        k_t = sb("k_t", [P, NP, S], on=mix)
        zs = sb("zs", [P, 16, S], on=mix)
        o_hi, o_lo = (sb(n, [P, KT, S], F32R, on=mix) for n in ("o_hi", "o_lo"))
        soft = [Buf(sb(f"soft{i}", [P, 3 * P], on=mix)) for i in range(3)]
        prob_t = [Buf(sb(f"prob_t{i}", [P, 3 * P], on=mix)) for i in range(2)]

        def q_heads(names, gain, ready, dst=tokq, rotate=True):
            out = []
            for j, name in enumerate(names):
                pair, t = yield from linear(name, (h_hi, h_lo), ready, True)
                view = lambda tt, j=j: dst[:, tt, j * 512:(j + 1) * 512].rearrange("p (h d) -> p h d", d=HD)
                nr = head_norm(pair, [t], [(0, 8, row(gain), view)], 8, HD)
                pair[0].free = pair[1].free = nr
                rp = [rope(view(tt)[:, :, 0:16], table(cs1, tt), table(sn1, tt), 8, 16, nr) for tt in range(TT)]
                for p2 in range(2):
                    b = aux()
                    tr = transposes(b, rp, [((pp * TT + tt) * P, dst[:, tt, (j * 4 + 2 * p2 + pp) * P:
                                                                    (j * 4 + 2 * p2 + pp + 1) * P])
                                            for pp in range(2) for tt in range(TT)])
                    c = SE([tr], lambda e, b=b, k=j * 4 + 2 * p2: e.activation(
                        q_t[:, k:k + 2, :].rearrange("p k t -> p (k t)"), b.t[:, :], ACT.Copy))
                    b.free = [c]
                    out.append(c)
            return out

        def z_gate(names, ready):
            out = []
            for j, name in enumerate(names):
                pair, t = yield from linear(name, (h_hi, h_lo), ready, False)
                for i in range(2):
                    v = scratch()
                    a = SE([t, *v.free], lambda e, v=v, i=i, pair=pair: e.activation(v.t[:, :], pair[i].t[:, :],
                                                                                     ACT.Tanh, scale=0.5))
                    k = j * 4 + 2 * i
                    b = VE([a], lambda e, v=v, i=i, k=k, pair=pair: e.scalar_tensor_tensor(
                        zs[:, k:k + 2, :].rearrange("p k t -> p (k t)"), v.t[:, :], 1.0, pair[i].t[:, :], ALU.add,
                        ALU.mult))
                    v.free = [b]
                    pair[i].free = [b]
                    out.append(b)
            zs_ready[:] = out

        zs_ready = []
        o_acc = Buf(banks[7].t[:, 0:S])

        def close_gated(pr, ob):
            def close(t):
                v = scratch()
                a = VE([t, *zs_ready, *v.free], lambda e, v=v: e.scalar_tensor_tensor(
                    v.t[:, 0:S], ob.t, 0.5, zs[:, pr, :], ALU.mult, ALU.mult))
                ob.free = [a]
                v.free = split_to(o_hi[:, pr, :], o_lo[:, pr, :], v.t[:, 0:S], [a])
                o_ready.extend(v.free)
            return close

        o_ready = []

        drain_steps(adaptive(0))
        h0 = norm([x_in], ada[:, 0, KT:2 * KT], ada[:, 0, 0:KT], [ada_done[0]])

        by_parity = scr[:, :, :].rearrange("p t (i g l d) -> p t i g l d", i=1, g=8, l=2)
        pair, t = drain_steps(linear("nsa_kcvc", (h_hi, h_lo), h0, True))
        bp = []
        for tt in range(TT):
            for lo in range(2):
                src = pair[tt].t[:, :].rearrange("p (g d) -> p g d", d=HD)
                par = con("parity")[:, lo:lo + 1]
                if lo == 0:
                    e_ = VE([t, *scr_buf.free], lambda e, tt=tt, s=src, par=par: e.tensor_scalar(
                        by_parity[:, tt, 0, :, 0, :], s, par, None, ALU.mult))
                else:
                    e_ = SE([t, *scr_buf.free, e_], lambda e, tt=tt, s=src, par=par: e.activation(
                        by_parity[:, tt, 0, :, 1, :], s, ACT.Copy, scale=par))
                bp.append(e_)
        pair[0].free = pair[1].free = list(bp)

        gates = sb("gates", [P, TT, 3 * NH], on=mix)
        pair, t = drain_steps(linear("nsa_gate", (h_hi, h_lo), h0, True))
        gates_ready = []
        for tt in range(TT):
            a = VE([t, rows_in], lambda e, tt=tt, pair=pair: e.tensor_tensor(
                gates[:, tt, :], pair[tt].t[:, 0:3 * NH], row("gate_b"), ALU.add))
            pair[tt].free = [a]
            b = SE([a], lambda e, tt=tt: e.activation(gates[:, tt, :], gates[:, tt, :], ACT.Tanh, scale=0.5))
            gates_ready.append(VE([b], lambda e, tt=tt: e.tensor_scalar(gates[:, tt, :], gates[:, tt, :], 1.0, 0.5,
                                                                        ALU.add, ALU.mult)))

        NB = NKV * NCMP
        flat = [zs[:, 8 + 4 * i:12 + 4 * i, :].rearrange("p k t -> p (k t)")[:, 0:CJ * (NB + 1)]
                .rearrange("p (j n) -> p j n", j=CJ) for i in range(2)]
        flat_ready = []
        for i in range(2):
            b = aux()

            def emit(e, i=i, b=b):
                for g in range(NKV):
                    for tt in range(TT):
                        mm = e.matmul(b.t[:, g * P + tt * 64:g * P + (tt + 1) * 64],
                                      by_parity[:, tt, 0, i * NKV + g, :, :].rearrange("p l d -> p (l d)"),
                                      con("pair"), start=True, stop=True)
                return mm

            t = PE([*bp, const_in, *b.free], emit)
            window = bass.AP(b.t[:, :].tensor, b.t[:, :].offset,
                             [list(b.t[:, :].ap[0]), [1, CJ], [P, NKV], [CMP_STRIDE // 2, NCMP]])
            a = VE([t], lambda e, i=i, w=window: e.tensor_copy(
                flat[i][:, :, 0:NB].rearrange("p j (g n) -> p j g n", g=NKV), w))
            c = VE([cols_in], lambda e, i=i: e.tensor_copy(flat[i][:, :, NB:NB + 1], col(f"pe{i}").unsqueeze(2)))
            b.free = [a]
            scr_buf.free = [t]
            flat_ready.append([a, c])

        q_ready = drain_steps(q_heads(["nsa_q0", "nsa_q1"], "nsa_q", h0))

        def k_pairs(branch, n_branch, ready):
            b = aux()
            tr = transposes(b, ready, [((g2 * TT + tt) * P, tokk[:, tt, branch * S + g2 * P:branch * S + (g2 + 1) * P])
                                       for g2 in range(2) for tt in range(TT)])
            c = None
            for g2 in range(2):
                c = SE([tr], lambda e, b=b, g2=g2: e.activation(k_t[:, g2 * n_branch + branch, :],
                                                                b.t[:, g2 * S:(g2 + 1) * S], ACT.Copy))
            b.free = [c]
            return c

        pair, t = drain_steps(linear("nsa_kskw", (h_hi, h_lo), h0, True))
        kv = lambda tt, c0, n: tokk[:, tt, c0:c0 + n * HD].rearrange("p (h d) -> p h d", d=HD)
        nr = head_norm(pair, [t], [(0, 4, row("nsa_ks"), lambda tt: kv(tt, 0, 4)),
                                   (4, 4, row("nsa_kw"), lambda tt: kv(tt, S, 4))], 8, HD)
        pair[0].free = pair[1].free = nr
        rp = [rope(kv(tt, 0, 8)[:, :, 0:16], table(cs1, tt), table(sn1, tt), 8, 16, nr) for tt in range(TT)]
        k_ready = [k_pairs(br, 2, rp) for br in range(2)]

        pair, t = drain_steps(linear("nsa_vsvw", (h_hi, h_lo), h0, True))
        v_ready = []
        for tt in range(TT):
            a = SE([t], lambda e, tt=tt, pair=pair: e.activation(tokv[:, tt, 0:512], pair[tt].t[:, :], ACT.Copy))
            pair[tt].free = [a]
            v_ready.append(a)

        hid = sb("hid", [P, 2, 2, NKV, CPAD], on=mix)
        hz = GP([], lambda e: e.memset(hid[:, :, :, :, :], 0.0))
        kc2 = sb("kc2", [P, 2, HD], on=mix)
        vc = sb("vc", [P, HD], on=mix)
        kc_t = sb("kc_t", [P, P], on=mix)
        for i in range(2):
            pair = acc_pair()
            bank = pair[0]
            for half in range(2):
                u = take(f"cmp_w1_{i}")

                def products(e, half=half, i=i, w=raw[u % NRAW].t, bank=bank):
                    for kk in range(8):
                        for b in range(2):
                            mm = e.matmul(bank.t[:, b * 64:b * 64 + NB + 1],
                                          w[:, kk * 256 + b * P:kk * 256 + (b + 1) * P],
                                          flat[i][:, half * 8 + kk, :],
                                          start=(half == 0 and kk == 0 and b == 0),
                                          stop=(half == 1 and kk == 7 and b == 1), skip_group_check=True)
                    return mm

                t = PE([fetched[u], *flat_ready[i], *(bank.free if half == 0 else [])], products)
                used_raw(u, t)
            bias = stat(2)
            b1 = col(f"b1_{i}")
            ev = []
            a = VE([t, cols_in], lambda e, bias=bias, bank=bank, b1=b1: e.tensor_tensor(
                bias, bank.t[:, NB:NB + 65:64], b1, ALU.add))
            for b in range(2):
                ev.append(SE([a, hz], lambda e, b=b, i=i, bias=bias, bank=bank: e.activation(
                    hid[:, i, b, :, 0:NCMP], bank.t[:, b * 64:b * 64 + NB].rearrange("p (g n) -> p g n", g=NKV),
                    ACT.Gelu_apprx_tanh, bias=bias[:, b:b + 1])))
            bank.free = ev
            b2 = aux()
            w2 = col(f"w2_{i}")

            def emit(e, i=i, w2=w2, b2=b2):
                for b in range(2):
                    mm = e.matmul(b2.t[:, 0:HD], hid[:, i, b, :, :].rearrange("p g n -> p (g n)"),
                                  w2[:, b * HD:(b + 1) * HD], start=(b == 0), stop=(b == 1))
                return mm

            t = PE([*ev, *b2.free], emit)
            if i == 1:
                vc_ready = SE([t], lambda e, b2=b2: e.activation(vc[:, :], b2.t[:, 0:HD], ACT.Copy))
                b2.free = [vc_ready]
                continue
            ms, rs = stat(1), stat(1)
            a = SE([t], lambda e, b2=b2, ms=ms: e.activation(kc2[:, 0, :], b2.t[:, 0:HD], ACT.Square, scale=HD ** -0.5,
                                                      accum_out=ms))
            r = rsqrt(rs, ms, [a])
            a = VE([r, rows_in], lambda e, b2=b2, rs=rs: e.scalar_tensor_tensor(
                kc2[:, 0, :], b2.t[:, 0:HD], rs, row("nsa_kc"), ALU.mult, ALU.mult))
            b2.free = [a]
            a = rope(kc2[:, 0:1, 0:16], table(cs1, TT), table(sn1, TT), 1, 16, [a])
            a = VE([a], lambda e: e.tensor_copy(kc2[:, 1, :], kc2[:, 0, :]))
            b3 = aux()
            t = transposes(b3, [a], [(0, kc2[:, :, :].rearrange("p a d -> p (a d)"))])
            kc_ready = SE([t], lambda e, b3=b3: e.activation(kc_t[:, :], b3.t[:, 0:P], ACT.Copy))
            b3.free = [kc_ready]

        pc_t = sb("pc_t", [P, NKV, S], on=mix)
        cmp_ready = []
        for tt in range(TT):
            two_banks = banks[4], banks[5]
            s_ = scr[:, tt, 0:512]
            sv = s_.rearrange("p (h n) -> p h n", n=CPAD)
            hb = lambda z: bcast(z.unsqueeze(2), [P, NH, CPAD])

            def emit(e, tt=tt):
                for r in range(4):
                    for g in range(NKV):
                        hs = slice((g % 2) * HD, (g % 2 + 1) * HD)
                        x_ = r * 2 + g // 2
                        mm = e.matmul(banks[4 + g % 2].t[:, x_ * CPAD:(x_ + 1) * CPAD],
                                      q_t[hs, (g // 2) * 4 + r, tt * P:(tt + 1) * P],
                                      kc_t[hs, g * CPAD:(g + 1) * CPAD], start=True, stop=True)
                return mm

            t = PE([*q_ready, kc_ready, *two_banks[0].free, *two_banks[1].free], emit)
            mx, su = stat(NH), stat(NH)
            mask = con("cmp_mask")[:, tt * CPAD:(tt + 1) * CPAD].unsqueeze(1)
            for i in range(2):
                a = VE([t, *scr_buf.free], lambda e, i=i, sv=sv, mask=mask: e.tensor_tensor(
                    sv.rearrange("p (x a) n -> p x a n", a=2)[:, :, i, :],
                    banks[4 + i].t[:, 0:NH // 2 * CPAD].rearrange("p (h n) -> p h n", n=CPAD),
                    bcast(mask, [P, NH // 2, CPAD]), ALU.add))
                two_banks[i].free = [a]
            c = VE([a], lambda e, sv=sv, mx=mx: e.reduce_max(mx, sv, AX.X))
            c = VE([c], lambda e, mx=mx: e.tensor_scalar(mx, mx, FLOOR, None, ALU.max))
            c = VE([c], lambda e, sv=sv, mx=mx, hb=hb: e.tensor_tensor(sv, sv, hb(mx), ALU.subtract))
            d = SE([c], lambda e, s_=s_: e.activation(s_, s_, ACT.Exp, scale=HD ** -0.5))
            c = VE([d], lambda e, sv=sv, su=su: e.reduce_sum(su, sv, AX.X))
            c = VE([c], lambda e, su=su: e.tensor_scalar(su, su, 1e-30, None, ALU.max))
            c = VE([c], lambda e, su=su: e.reciprocal(su, su))
            c = VE([c, *gates_ready], lambda e, su=su, tt=tt: e.tensor_tensor(su, su, gates[:, tt, 0:NH], ALU.mult))
            c = VE([c], lambda e, sv=sv, su=su, hb=hb: e.tensor_tensor(sv, sv, hb(su), ALU.mult))
            b6 = banks[6]
            t = transposes(b6, [c], [(r * P, s_[:, r * P:(r + 1) * P]) for r in range(4)])
            a = SE([t], lambda e, tt=tt, b6=b6: e.activation(pc_t[:, :, tt * P:(tt + 1) * P],
                                                             b6.t[:, :].rearrange("p (r t) -> p r t", r=4), ACT.Copy))
            b6.free = [a]
            cmp_ready.append(a)
        scr_buf.free = [t]

        items = []
        for pr in range(NP):
            for half in range(2):
                g, r = 2 * (pr // 4) + half, pr % 4
                ob = o_acc
                out = ob.t[half * HD:(half + 1) * HD, :]

                def before(e, g=g, r=r, out=out):
                    gs = slice(g * CPAD, (g + 1) * CPAD)
                    e.matmul(out, vc[gs, :], pc_t[gs, r, :], start=True, stop=False, skip_group_check=True)

                for br in range(2):
                    c = (br + 1) * NH + r * NKV + g
                    items.append(gqa_item(
                        q_t, k_t[:, (pr // 4) * 2 + br, :], pr, half,
                        lambda j, br=br, g=g: tokv[:, j, br * S + g * HD:br * S + (g + 1) * HD],
                        [*q_ready, *k_ready], [*v_ready, *cmp_ready, vc_ready], ob, out,
                        gate=gates[:, :, c:c + 1].rearrange("p t o -> p (t o)"), gate_ready=gates_ready,
                        first=br == 0, last=br == 1, before=before if br == 0 else None,
                        close=close_gated(pr, ob) if br == 1 and half == 1 else None))

        def nsa_background():
            yield from z_gate(["nsa_z0", "nsa_z1"], h0)
            yield from adaptive(1)
            yield from gate_as_row(0)

        bg = nsa_background()
        for _ in range(4):
            next(bg)
        attention(items, prob_t, soft, banks[7], bg, 1)
        x0 = drain_steps(residual(["nsa_out0", "nsa_out1"], (o_hi, o_lo), list(o_ready), None, [x_in]))
        gate_free = x0

        h1 = norm(x0, ada[:, 1, KT:2 * KT], ada[:, 1, 0:KT], [ada_done[1]])
        q_ready = drain_steps(q_heads(["moba_q0", "moba_q1"], "moba_q", h1))
        pair, t = drain_steps(linear("moba_kv", (h_hi, h_lo), h1, True))
        v_ready = [SE([t], lambda e, tt=tt, pair=pair: e.activation(tokv[:, tt, 0:S], pair[tt].t[:, S:2 * S], ACT.Copy))
                   for tt in range(TT)]
        nr = head_norm(pair, v_ready, [(0, 4, row("moba_k"), lambda tt: kv(tt, 0, 4))], 4, HD)
        pair[0].free = pair[1].free = nr
        rp = [rope(kv(tt, 0, 4)[:, :, 0:16], table(cs1, tt), table(sn1, tt), 4, 16, nr) for tt in range(TT)]
        k_ready = [k_pairs(0, 1, rp)]
        items = []
        o_ready.clear()
        for pr in range(NP):
            for half in range(2):
                g = 2 * (pr // 4) + half
                ob = o_acc
                items.append(gqa_item(
                    q_t, k_t[:, pr // 4, :], pr, half, lambda j, g=g: tokv[:, j, g * HD:(g + 1) * HD],
                    [*q_ready, *k_ready], v_ready, ob, ob.t[half * HD:(half + 1) * HD, :], gate=None, first=True,
                    last=True, before=None, close=close_gated(pr, ob) if half == 1 else None))
        def moba_background():
            yield from z_gate(["moba_z0", "moba_z1"], h1)
            yield from gate_as_row(1)

        bg = moba_background()
        for _ in range(4):
            next(bg, None)
        attention(items, prob_t, soft, banks[7], bg, 1)
        x1 = drain_steps(residual(["moba_out0", "moba_out1"], (o_hi, o_lo), list(o_ready), None, x0))
        mix.close()

        def ffn(i, ready):
            with ExitStack() as own:
                a_hi, a_lo = (sb(f"a{i}_{n}", [P, FT, S], F32R, on=own) for n in ("hi", "lo"))
                act = [Buf(sb(f"act{i}_{n}", [P, 512], on=own)) for n in range(2)]
                hr = norm(ready, col(f"ffn{i}"), None, [cols_in])
                out = []
                for n in range(FT // 2):
                    pair, t = drain_steps(linear(f"ffn{i}_up{n}", (h_hi, h_lo), hr, False))
                    v = act[n % 2]
                    a = SE([t, *v.free], lambda e, v=v, pair=pair: e.activation(
                        v.t[:, :], pair[0].t[:, :], ACT.Silu))
                    b = VE([a], lambda e, v=v, pair=pair: e.tensor_tensor(v.t[:, :], v.t[:, :], pair[1].t[:, :],
                                                                          ALU.mult))
                    pair[0].free, pair[1].free = [a], [b]
                    v.free = split_to(a_hi[:, 2 * n:2 * n + 2, :], a_lo[:, 2 * n:2 * n + 2, :],
                                      v.t[:, :].rearrange("p (k t) -> p k t", k=2), [b])
                    out = out + v.free
                return drain_steps(residual([f"ffn{i}_down0", f"ffn{i}_down1"], (a_hi, a_lo), out[-2:], 0.5, ready))

        x2 = ffn(1, x1)

        mix = ExitStack()
        tok2_q = sb("tokq2", [P, TT, MH * MQ], on=mix)
        tok2_k = sb("tokk2", [P, TT, MH * MQ], on=mix)
        tok2_v = sb("tokv2", [P, TT, 1024], on=mix)
        q2_t = sb("q_t2", [P, NP, S], on=mix)
        k2_t = sb("k_t2", [P, NP, S], on=mix)
        gate2 = sb("zs2", [P, 16, S], on=mix)
        o2_hi, o2_lo = (sb(n, [P, KT, S], F32R, on=mix) for n in ("o2_hi", "o2_lo"))
        soft2 = [Buf(sb(f"soft2_{i}", [P, 3 * P], on=mix)) for i in range(3)]
        prob2_t = [Buf(sb(f"prob2_t{i}", [P, 3 * P], on=mix)) for i in range(2)]
        lat = sb("lat", [P, TT, LAT], on=mix)
        l_hi, l_lo = (sb(n, [P, 3, S], F32R, on=mix) for n in ("l_hi", "l_lo"))
        decay = sb("decay", [P, 3, TT, FH], on=mix)
        lz = [GP([*x2], lambda e, z=z: e.memset(z[:, 1, :].bitcast(F32), 0.0)) for z in (l_hi, l_lo)]

        h2 = norm(x2, col("mix"), None, [cols_in])
        pair, t = drain_steps(linear("mix_lat", (h_hi, h_lo), h2, True))
        lat_in = [SE([t], lambda e, tt=tt, pair=pair: e.activation(lat[:, tt, :], pair[tt].t[:, 0:LAT], ACT.Copy))
                  for tt in range(TT)]
        for tt in range(TT):
            pair[tt].free = [lat_in[tt]]
        parts = ((0, QL), (QL, KVL), (QL + KVL, MR))
        ms, rs = stat(TT * 3), stat(TT * 3)
        sq = []
        for tt in range(TT):
            for j, (c0, n) in enumerate(parts):
                sq.append(SE([lat_in[tt], *sq_buf.free], lambda e, tt=tt, j=j, c0=c0, n=n: e.activation(
                    sq_buf.t[:, tt, c0:c0 + n], lat[:, tt, c0:c0 + n], ACT.Square, scale=n ** -0.5,
                    accum_out=ms[:, tt * 3 + j:tt * 3 + j + 1])))
        r = rsqrt(rs, ms, sq)
        sq_buf.free = [r]
        ln = []
        for tt in range(TT):
            for j, (c0, n) in enumerate(parts):
                ln.append(VE([r, *sq], lambda e, tt=tt, j=j, c0=c0, n=n: e.tensor_scalar(
                    lat[:, tt, c0:c0 + n], lat[:, tt, c0:c0 + n], rs[:, tt * 3 + j:tt * 3 + j + 1], None, ALU.mult)))
        l_ready = list(lz)
        for j, (c0, n, gain) in enumerate(((0, P, col("q_lat")[:, 0:1]), (P, QL - P, col("q_lat")[:, 1:2]),
                                           (QL, KVL, col("kv_lat")))):
            b = aux()
            t = transposes(b, ln, [(tt * P, lat[:, tt, c0:c0 + n]) for tt in range(TT)])
            v = scratch()
            a = VE([t, cols_in, *v.free], lambda e, v=v, b=b, n=n, gain=gain: e.tensor_scalar(
                v.t[0:n, 0:S], b.t[0:n, 0:S], gain[0:n, :], None, ALU.mult))
            b.free = [a]
            v.free = split_to(l_hi[0:n, j, :], l_lo[0:n, j, :], v.t[0:n, 0:S], [a, *lz])
            l_ready += v.free

        heads = lambda z, tt, w: z[:, tt, 0:MH * w].rearrange("p (h d) -> p h d", d=w)
        pair, t = drain_steps(linear("mla_qn", (l_hi, l_lo), l_ready, True))
        qn = head_norm(pair, [t], [(0, MH, row("mla_qn"), lambda tt: heads(tok2_q, tt, MQ)[:, :, 0:MN])], MH, MN)
        pair[0].free = pair[1].free = qn
        pair, t = drain_steps(linear("mla_qr", (l_hi, l_lo), l_ready, True))
        qr = head_norm(pair, [t], [(0, MH, row("mla_qr"), lambda tt: heads(tok2_q, tt, MQ)[:, :, MN:MQ])], MH, MR)
        pair[0].free = pair[1].free = qr
        qr = [rope(heads(tok2_q, tt, MQ)[:, :, MN:MQ], table(cs2, tt), table(sn2, tt), MH, MR, qr) for tt in range(TT)]
        pair, t = drain_steps(linear("mla_kn", (l_hi, l_lo), l_ready, True, k0=2))
        kn = head_norm(pair, [t], [(0, MH, row("mla_kn"), lambda tt: heads(tok2_k, tt, MQ)[:, :, 0:MN])], MH, MN)
        pair[0].free = pair[1].free = kn
        pair, t = drain_steps(linear("mla_v", (l_hi, l_lo), l_ready, True, k0=2))
        mv = [SE([t], lambda e, tt=tt, pair=pair: e.activation(tok2_v[:, tt, 0:512], pair[tt].t[:, :], ACT.Copy))
              for tt in range(TT)]
        for tt in range(TT):
            pair[tt].free = [mv[tt]]
        kr = []
        for tt in range(TT):
            k1 = lat[:, tt, QL + KVL:QL + KVL + MR].unsqueeze(1)
            a = VE([*ln, rows_in], lambda e, k1=k1: e.tensor_tensor(k1, k1, row("mla_kr").unsqueeze(1), ALU.mult))
            a = rope(k1, table(cs2, tt), table(sn2, tt), 1, MR, [a])
            kr.append(VE([a], lambda e, tt=tt, k1=k1: e.tensor_copy(heads(tok2_k, tt, MQ)[:, :, MN:MQ],
                                                                    bcast(k1, [P, MH, MR]))))

        def heads_turned(src, dst, w, ready, war=()):
            out = []
            for h in range(0, 8, 2):
                b = aux()
                t = transposes(b, ready, [((j * TT + tt) * P, heads(src, tt, w)[:, h + j, :])
                                          for j in range(2) for tt in range(TT)])
                c = SE([t, *war], lambda e, b=b, h=h: e.activation(
                    dst[0:w, h:h + 2, :].rearrange("p k t -> p (k t)"), b.t[0:w, :], ACT.Copy))
                b.free = [c]
                out.append(c)
            return out, t

        q_ready, _ = heads_turned(tok2_q, q2_t, MQ, [*qn, *qr])
        k_ready, turned = heads_turned(tok2_k, k2_t, MQ, [*kn, *kr])

        o_ready.clear()

        def close_plain(kt, ob):
            def close(t):
                o_ready.extend(split_to(o2_hi[:, kt, :], o2_lo[:, kt, :], ob.t, [t]))
                ob.free = o_ready[-2:]
            return close

        def head_items(w, scale, v0, kt0, ready, vr):
            out = []
            for h in range(8):
                ob = o_acc
                out.append(dict(
                    q=lambda t, h=h: q2_t[0:w, h, t * P:(t + 1) * P], k=lambda n, h=h: k2_t[0:w, h, 0:n],
                    v=lambda j, h=h: tok2_v[:, j, v0 + h * HD:v0 + (h + 1) * HD], ready=ready, v_ready=vr, scale=scale,
                    o_buf=ob, out=ob.t[(h % 2) * HD:(h % 2 + 1) * HD, :], gate=None, first=True, last=True,
                    before=None, close=close_plain(kt0 + h // 2, ob) if h % 2 else None))
            return out

        fl = []
        for tt in range(TT):
            f, s1 = decay[:, 0, tt, :], decay[:, 1, tt, :]
            a = VE([lat_in[tt], rows_in], lambda e, tt=tt, f=f: e.tensor_tensor(
                f, lat[:, tt, LAT - FH:LAT], row("fox_bf"), ALU.add))
            b = VE([a], lambda e, f=f, s1=s1: e.tensor_scalar(s1, f, -1.0, None, ALU.mult))
            b = VE([b], lambda e, f=f, s1=s1: e.tensor_tensor(s1, s1, f, ALU.min))
            c = SE([b], lambda e, s1=s1: e.activation(s1, s1, ACT.Exp))
            c = SE([c], lambda e, s1=s1: e.activation(s1, s1, ACT.Ln, bias=1.0))
            fl.append(VE([c], lambda e, f=f, s1=s1: e.scalar_tensor_tensor(f, f, 0.0, s1, ALU.min, ALU.subtract)))

        def fox_setup():
            fq = lambda tt: heads(tok2_q, tt, FK)
            fk = lambda tt: heads(tok2_k, tt, FK)
            b = aux()

            def emit(e):
                e.matmul(b.t[:, 0:FH], con("upto"), decay[:, 0, 0, :], start=True, stop=True)
                e.matmul(b.t[:, FH:2 * FH], con("ones"), decay[:, 0, 0, :], start=True, stop=False)
                return e.matmul(b.t[:, FH:2 * FH], con("upto"), decay[:, 0, 1, :], start=False, stop=True)

            t = PE([*fl, *b.free], emit)
            cum = VE([t], lambda e: e.tensor_copy(decay[:, 2, :, :].rearrange("p t h -> p (t h)"), b.t[:, 0:2 * FH]))
            b.free = [cum]
            pair, t = yield from linear("fox_q", (h_hi, h_lo), h2, True)
            qn = head_norm(pair, [t, turned], [(0, FH, row("fox_q"), lambda tt: fq(tt)[:, :, 0:HD])], FH, HD)
            pair[0].free = pair[1].free = qn
            pair, t = yield from linear("fox_k", (h_hi, h_lo), h2, True)
            kn = head_norm(pair, [t, turned], [(0, FH, row("fox_k"), lambda tt: fk(tt)[:, :, 0:HD])], FH, HD)
            pair[0].free = pair[1].free = kn
            pair, t = yield from linear("fox_v", (h_hi, h_lo), h2, True)
            fv = [SE([t], lambda e, tt=tt, pair=pair: e.activation(tok2_v[:, tt, 512:1024], pair[tt].t[:, :], ACT.Copy))
                  for tt in range(TT)]
            for tt in range(TT):
                pair[tt].free = [fv[tt]]
            ex = []
            for tt in range(TT):
                cu = decay[:, 2, tt, :].unsqueeze(2)
                ex.append(VE([*qn], lambda e, tt=tt: e.tensor_scalar(fq(tt)[:, :, 0:HD], fq(tt)[:, :, 0:HD],
                                                                     HD ** -0.5, None, ALU.mult)))
                ex.append(VE([cum, turned], lambda e, tt=tt, cu=cu: e.tensor_copy(fq(tt)[:, :, HD:HD + 1], cu)))
                ex.append(VE([turned], lambda e, tt=tt: e.memset(fq(tt)[:, :, HD + 1:HD + 2], 1.0)))
                ex.append(VE([turned], lambda e, tt=tt: e.memset(fk(tt)[:, :, HD:HD + 1], 1.0)))
                ex.append(VE([cum, turned], lambda e, tt=tt, cu=cu: e.tensor_scalar(
                    fk(tt)[:, :, HD + 1:HD + 2], cu, -1.0, None, ALU.mult)))
            return [*qn, *kn, *ex], fv

        result = []

        def keep(gen):
            result.append((yield from gen))

        attention(head_items(MQ, MQ ** -0.5, 0, 0, [*q_ready, *k_ready], mv), prob2_t, soft2, banks[7],
                  keep(fox_setup()), 1)
        mla_scored = (PE.sem, PE.count)
        (fox_ready, fv), = result
        q_ready, _ = heads_turned(tok2_q, q2_t, FK, fox_ready, [mla_scored])
        k_ready, _ = heads_turned(tok2_k, k2_t, FK, fox_ready, [mla_scored])

        half_b = sb("half_b", [P, 2 * KT], on=mix)
        hb_ready = VE([cols_in, *x2], lambda e: e.tensor_scalar(
            half_b[:, :], cols[:, COLS["gate_mla"][0]:COLS["gate_fox"][1]], 0.5, None, ALU.mult))

        def gates_2():
            for j, name in enumerate(("gate_mla0", "gate_mla1", "gate_fox0", "gate_fox1")):
                pair, t = yield from linear(name, (h_hi, h_lo), h2, False)
                for i in range(2):
                    for b in range(2):
                        k = 4 * j + 2 * i + b
                        a = SE([t, hb_ready], lambda e, k=k, i=i, b=b, pair=pair: e.activation(
                            gate2[:, k, :], pair[i].t[:, b * S:(b + 1) * S], ACT.Tanh, bias=half_b[:, k:k + 1],
                            scale=0.5))
                    pair[i].free = [a]
            result.append(a)

        attention(head_items(FK, 1.0, 512, 4, [*q_ready, *k_ready], fv), prob2_t, soft2, banks[7], gates_2(), 2)
        gates2_ready = result[-1]

        mixed = scr[:, :, :].rearrange("p t (k s) -> p (t k) s", s=S)
        mm_ready = []
        for j in range(2):
            pair, t = drain_steps(linear(f"br_mla{j}", (o2_hi, o2_lo), list(o_ready), False))
            for i in range(2):
                k = 4 * j + 2 * i
                a = VE([t, gates2_ready, *scr_buf.free], lambda e, k=k, i=i, pair=pair: e.scalar_tensor_tensor(
                    mixed[:, k:k + 2, :], gate2[:, k:k + 2, :], 1.0,
                    pair[i].t[:, :].rearrange("p (k s) -> p k s", k=2), ALU.add, ALU.mult))
                pair[i].free = [a]
                mm_ready.append(a)
        m_ready = []
        for j in range(2):
            pair, t = drain_steps(linear(f"br_fox{j}", (o2_hi, o2_lo), list(o_ready), False, k0=4))
            for i in range(2):
                k = 4 * j + 2 * i
                v = scratch()
                vv = v.t[:, :].rearrange("p (k s) -> p k s", k=2)
                a = VE([t, *v.free], lambda e, k=k, i=i, vv=vv, pair=pair: e.scalar_tensor_tensor(
                    vv, gate2[:, 8 + k:10 + k, :], 1.0, pair[i].t[:, :].rearrange("p (k s) -> p k s", k=2),
                    ALU.add, ALU.mult))
                pair[i].free = [a]
                a = VE([a, *mm_ready], lambda e, k=k, vv=vv: e.tensor_tensor(vv, vv, mixed[:, k:k + 2, :], ALU.add))
                v.free = split_to(h_hi[:, k:k + 2, :], h_lo[:, k:k + 2, :], vv, [a], 0.5)
                m_ready += v.free
        scr_buf.free = [a]
        x3 = drain_steps(residual(["mix_out0", "mix_out1"], (h_hi, h_lo), m_ready, 1.0, x2))
        mix.close()

        x4 = ffn(2, x3)
        assert taken[0] == len(units)

        out_sem = sem("out_stored")
        sync_steps.append((x4, lambda e: e.dma_start(out_d.rearrange("o (t p) d -> p (o t) d", p=P),
                                                     x[:, :, :]).then_inc(out_sem, 16)))

        block = ctx.enter_context(nc.Block())

        @block.sync
        def _(e):
            met = {}
            for waits, emit in sync_steps:
                for s, value in waits:
                    if met.get(s.name, 0) < value:
                        e.wait_ge(s, value)
                        met[s.name] = value
                emit(e)
            e.wait_ge(out_sem, 16)

        @block.tensor
        def _(e):
            PE.run(e)

        @block.vector
        def _(e):
            VE.run(e)

        @block.scalar
        def _(e):
            SE.run(e)

        @block.gpsimd
        def _(e):
            GP.run(e)


def chunk_arrays(a):
    heads_ = np.arange(NH)
    pairs = [(gp * 8 + half * 4 + r) for gp in range(2) for r in range(4) for half in range(2)]
    hd = lambda hs: np.concatenate([np.arange(h * HD, (h + 1) * HD) for h in hs])
    perm = hd(pairs)
    w = a["nsa_w_in"][0]
    q, kc, vc, ks, vs, kw, vw, gl, z = np.split(w, np.cumsum([D] + [256] * 6 + [48])[:8], axis=1)
    out = {}
    for i in range(2):
        for n in range(6):
            out[f"ada{i}_{n}"] = a["ada_w"][i][:, n * 512:(n + 1) * 512]
    halves = lambda name, m: out.update({f"{name}{j}": m[:, j * 512:(j + 1) * 512] for j in range(2)})
    cat = lambda *m: np.concatenate(m, axis=1)
    out["nsa_kcvc"], out["nsa_kskw"], out["nsa_vsvw"] = cat(kc, vc), cat(ks, kw), cat(vs, vw)
    out["nsa_gate"] = gl.reshape(D, NKV, 4, 3).transpose(0, 3, 2, 1).reshape(D, 48)
    halves("nsa_q", q[:, perm])
    halves("nsa_z", z[:, perm])
    halves("nsa_out", a["nsa_w_out"][0][perm])
    for i in range(2):
        out[f"cmp_w1_{i}"] = a["nsa_cmp_w1"][0, i]
    q, k, v, z = np.split(a["moba_w_in"][0], np.cumsum([D, 256, 256]), axis=1)
    halves("moba_q", q[:, perm])
    out["moba_kv"] = cat(k, v)
    halves("moba_z", z[:, perm])
    halves("moba_out", a["moba_w_out"][0][perm])
    for i in (1, 2):
        g, u, d = (a[f"ffn{i}_w_{n}_2"][0] for n in ("gate", "up", "down"))
        for n in range(FT // 2):
            out[f"ffn{i}_up{n}"] = cat(g[:, n * 256:(n + 1) * 256], u[:, n * 256:(n + 1) * 256])
        halves(f"ffn{i}_down", d)
    ql, kvl, kr, fq, fk, fv, fl, gm, gf = np.split(
        a["w_in_2"][0], np.cumsum([QL, KVL, MR, 512, 512, 512, FH, D]), axis=1)
    out["mix_lat"] = cat(ql, kvl, kr, fl)
    out["fox_q"], out["fox_k"], out["fox_v"] = fq, fk, fv
    halves("gate_mla", gm)
    halves("gate_fox", gf)
    qb = a["mla_w_qb_2"][0].reshape(QL, MH, MQ)
    qb = np.concatenate([qb, np.zeros((2 * P - QL, MH, MQ), qb.dtype)])
    out["mla_qn"], out["mla_qr"] = qb[:, :, :MN].reshape(2 * P, -1), qb[:, :, MN:].reshape(2 * P, -1)
    kvb = a["mla_w_kvb_2"][0].reshape(KVL, MH, 2 * MN)
    out["mla_kn"], out["mla_v"] = kvb[:, :, :MN].reshape(KVL, -1), kvb[:, :, MN:].reshape(KVL, -1)
    halves("br_mla", a["w_branch_mla_2"][0])
    halves("br_fox", a["w_branch_fox_2"][0])
    halves("mix_out", a["w_o_2"][0])
    return out


def packed_weights(a):
    units, total = unit_list()
    mats = chunk_arrays(a)
    out = np.empty((P, total), np.float32)
    for name, k, m, n, _, at in units:
        part = mats[name][k * P:(k + m) * P]
        out[:, at:at + m * n] = part.reshape(m, P, n).transpose(1, 0, 2).reshape(P, m * n)
    return out


def packed_columns(a):
    out = np.zeros((P, NCOLS), np.float32)
    put = lambda name, v: out.__setitem__((slice(None), slice(*COLS[name])), v)
    by = lambda v: v.reshape(-1, P).T
    put("c", by(a["c"][0]))
    for i in range(2):
        put(f"norm{i}", by(a["norm_g"][i]))
        put(f"ada{i}", by(a["ada_b"][i]))
        put(f"b1_{i}", by(a["nsa_cmp_b1"][0, i]))
        put(f"pe{i}", a["nsa_cmp_pe"][0, i].reshape(CJ, P).T)
        put(f"w2_{i}", a["nsa_cmp_w2"][0, i].reshape(2, P, HD).transpose(1, 0, 2).reshape(P, 2 * HD))
    put("ffn1", by(a["ffn1_norm_2"][0]))
    put("mix", by(a["mix_norm_2"][0]))
    put("ffn2", by(a["ffn2_norm_2"][0]))
    put("gate_mla", by(a["b_gate_2"][0, 0]))
    put("gate_fox", by(a["b_gate_2"][0, 1]))
    ql = a["mla_q_lat_norm_2"][0]
    put("q_lat", by(np.concatenate([ql, np.zeros(2 * P - QL, ql.dtype)])))
    put("kv_lat", by(a["mla_kv_lat_norm_2"][0]))
    return out


def packed_rows(a):
    kn = a["nsa_k_norm"][0]
    gb = a["nsa_gate_b"][0].reshape(NKV, 4, 3).transpose(2, 1, 0).reshape(-1)
    return np.concatenate([a["nsa_q_norm"][0], kn[0], kn[1], kn[2], gb, a["moba_q_norm"][0], a["moba_k_norm"][0],
                           a["mla_q_nope_gain_2"][0], a["mla_q_rope_gain_2"][0], a["mla_k_nope_gain_2"][0],
                           a["mla_k_rope_gain_2"][0], a["fox_q_gain_2"][0], a["fox_k_gain_2"][0],
                           a["fox_b_f_2"][0]])[None, :]


def packed_positions(a):
    by = lambda v: v.reshape(TT, P).T
    p1, p2 = a["positions"][0], a["positions_2"][0]
    ends = np.zeros(P, p1.dtype)
    at = np.arange(NKV)[:, None] * CPAD + np.arange(NCMP)[None, :]
    ends[at] = p1[np.arange(NCMP) * CMP_STRIDE + CMP_LEN - 1][None, :]
    return np.concatenate([np.repeat(by(p1), 8, axis=1), np.repeat(ends[:, None], 8, axis=1),
                           np.repeat(by(p2), 16, axis=1)], axis=1)


def kernel(**inputs):
    import concourse.bacc as bacc
    from concourse.bass_utils import run_bass_kernel_spmd

    a = {k: np.asarray(v) for k, v in inputs.items()}
    arrays = {"in_weights": packed_weights(a), "in_columns": packed_columns(a), "in_rows": packed_rows(a),
              "in_constants": shape_constants(), "in_positions": packed_positions(a), "in_x": a["x"]}
    arrays = {k: np.ascontiguousarray(v) for k, v in arrays.items()}
    nc = bacc.Bacc("TRN2", target_bir_lowering=False, num_devices=1)
    args = [nc.dram_tensor(k, v.shape, mybir.dt.from_np(v.dtype), kind="ExternalInput").ap()
            for k, v in arrays.items()]
    out = nc.dram_tensor("out", a["x"].shape, F32, kind="ExternalOutput").ap()
    program(nc, *args, out)
    return run_bass_kernel_spmd(nc, [arrays], core_ids=[0]).results[0]["out"]
```

```python
import numpy as np
import concourse.bass as bass
from concourse import mybir
from concourse.alu_op_type import AluOpType as ALU
from contextlib import ExitStack

F32, F32R, I32 = mybir.dt.float32, mybir.dt.float32r, mybir.dt.int32
ACT = mybir.ActivationFunctionType
AX = mybir.AxisListType

P = 128
D = 1024
S = 256
TT = S // P
KT = D // P
HD = 64
NH, NKV = 16, 4
NP = NH // 2
FFN = 2816
FT = FFN // P
CMP_LEN, CMP_STRIDE = 32, 16
NCMP = (S - CMP_LEN) // CMP_STRIDE + 1
CPAD = 32
CJ = CMP_LEN // 2
MH, MN, MR = 8, 64, 32
MQ = MN + MR
FH, FK = 8, HD + 2
QL, KVL = 192, 128
LAT = QL + KVL + MR + FH
EPS = 1e-6
NEG, FLOOR = -1e30, -1e29
UNIT = 1024
NRAW, NSPLIT = 8, 4
TWO_PI = 6.283185307179586
PI_PARTS = (6.28125, 0.0019340515136718750, 1.2554228305816650e-06)
PI_PARTS = PI_PARTS + (TWO_PI - sum(PI_PARTS),)
PI_LOW = 3.1415925
ROUND = 12582912.0


def chunk_list():
    ada = lambda i: [(f"ada{i}_{n}", KT, 512, False) for n in range(6)]
    ffn = lambda i: ([(f"ffn{i}_up{n}", KT, 512, True) for n in range(FT // 2)]
                     + [(f"ffn{i}_down{n}", FT, 512, True) for n in range(2)])
    two = lambda name, k: [(f"{name}{n}", k, 512, True) for n in range(2)]
    return (ada(0)[:4]
            + [("nsa_kcvc", KT, 512, True)] + two("nsa_q", KT) + [("nsa_kskw", KT, 512, True)]
            + [("cmp_w1_0", CJ, 256, False), ("cmp_w1_1", CJ, 256, False)]
            + [("nsa_gate", KT, 48, True), ("nsa_vsvw", KT, 512, True)] + two("nsa_z", KT)
            + ada(0)[4:] + ada(1)[:4] + two("nsa_out", KT)
            + two("moba_q", KT) + [("moba_kv", KT, 512, True)] + two("moba_z", KT) + ada(1)[4:] + two("moba_out", KT)
            + ffn(1)
            + [("mix_lat", KT, LAT, True),
               ("fox_q", KT, 512, True), ("fox_k", KT, 512, True), ("fox_v", KT, 512, True),
               ("mla_qn", 2, 512, True), ("mla_qr", 2, 256, True),
               ("mla_kn", 1, 512, True), ("mla_v", 1, 512, True)]
            + two("gate_mla", KT) + two("gate_fox", KT)
            + two("br_fox", KT // 2) + two("br_mla", KT // 2) + two("mix_out", KT)
            + ffn(2))


def unit_list():
    units, at = [], 0
    for name, kt, n, split in chunk_list():
        per = UNIT // n
        for k in range(0, kt, per):
            m = min(per, kt - k)
            units.append((name, k, m, n, split, at))
            at += m * n
    return units, at


def layout(sizes):
    at, out = 0, {}
    for name, n in sizes:
        out[name] = (at, at + n)
        at += n
    return out, at


COLS, NCOLS = layout([("c", KT), ("norm0", KT), ("norm1", KT), ("ada0", 3 * KT), ("ada1", 3 * KT),
                      ("ffn1", KT), ("mix", KT), ("ffn2", KT), ("gate_mla", KT), ("gate_fox", KT),
                      ("b1_0", 2), ("b1_1", 2), ("q_lat", 2), ("kv_lat", 1), ("pe0", CJ), ("pe1", CJ),
                      ("w2_0", 2 * HD), ("w2_1", 2 * HD)])
ROWS, NROWS = layout([("nsa_q", HD), ("nsa_kc", HD), ("nsa_ks", HD), ("nsa_kw", HD), ("gate_b", 3 * NH),
                      ("moba_q", HD), ("moba_k", HD), ("mla_qn", MN), ("mla_qr", MR), ("mla_kn", MN),
                      ("mla_kr", MR), ("fox_q", HD), ("fox_k", HD), ("fox_bf", FH)])
ANG, NANG = layout([("tok", TT * 8), ("cmp", 8), ("tok2", TT * 16)])
CONST, NCONST = layout([("ident", P), ("causal", S), ("pair", P // 2), ("parity", 2), ("cmp_mask", TT * CPAD),
                        ("upto", P), ("ones", P), ("freq", NANG), ("lat_eps", 3)])


def shape_constants():
    c = np.zeros((P, NCONST), np.float32)
    put = lambda name, a: c.__setitem__((slice(None), slice(*CONST[name])), a)
    p = np.arange(P)[:, None]
    put("ident", np.eye(P))
    put("causal", np.where(np.arange(S)[None, :] - P <= p, 0.0, NEG))
    put("pair", p // 2 == np.arange(P // 2)[None, :])
    put("parity", p % 2 == np.arange(2)[None, :])
    ends = np.arange(CPAD) * CMP_STRIDE + CMP_LEN - 1
    ok = (ends[None, None, :] <= p[:, :, None] + P * np.arange(TT)[None, :, None]) & (np.arange(CPAD) < NCMP)
    put("cmp_mask", np.where(ok, 0.0, NEG).reshape(P, -1))
    put("upto", p <= np.arange(P)[None, :])
    put("ones", 1.0)
    f1 = np.float32(500000.0) ** (-np.arange(0, 16, 2, dtype=np.float32) / np.float32(16))
    f2 = np.float32(10000.0) ** (-np.arange(16, dtype=np.float32) / np.float32(16))
    put("freq", np.concatenate([np.tile(f1, TT), f1, np.tile(f2, TT)])[None, :])
    return c


class Engine:

    def __init__(self, sem):
        self.sem, self.count, self.steps = sem, 0, []

    def __call__(self, waits, emit):
        self.count += 1
        self.steps.append((list(waits), emit))
        return (self.sem, self.count)

    def run(self, eng):
        met = {}
        for waits, emit in self.steps:
            for sem, value in waits:
                if met.get(sem.name, 0) < value:
                    eng.wait_ge(sem, value)
                    met[sem.name] = value
            emit(eng).then_inc(self.sem, 1)


class Buf:

    def __init__(self, t):
        self.t, self.free = t, []


class TilesReady:

    def __init__(self, tickets, n):
        self.tickets = tickets

    def __getitem__(self, tiles):
        return [self.tickets[k] for k in range(tiles.start, tiles.stop)]


def drain_steps(gen):
    while True:
        try:
            next(gen)
        except StopIteration as e:
            return e.value


def program(nc, wts, cols_d, rows_d, const_d, pos_d, gate_bias_d, x_d, out_d):
    units, _ = unit_list()
    ctx = ExitStack()
    with ctx:
        sem = lambda n: ctx.enter_context(nc.semaphore(n))

        def sb(name, shape, dt=F32, on=ctx):
            return on.enter_context(nc.sbuf_tensor(name, shape, dt))

        PE, VE, SE, GP = (Engine(sem(n)) for n in ("pe_done", "dve_done", "act_done", "pool_done"))
        sync_steps = []

        raw = [Buf(sb(f"w_raw{i}", [P, UNIT])) for i in range(NRAW)]
        raw_sem = [sem(f"w_raw{i}_in") for i in range(NRAW)]
        w_hi = [Buf(sb(f"w_hi{i}", [P, UNIT], F32R)) for i in range(NSPLIT)]
        w_lo = [sb(f"w_lo{i}", [P, UNIT], F32R) for i in range(NSPLIT)]
        x = sb("x", [P, TT, D])
        h_hi, h_lo = (sb(n, [P, KT, S], F32R) for n in ("h_hi", "h_lo"))
        scr = sb("scr", [P, TT, D])
        cols, rows, const = sb("cols", [P, NCOLS]), sb("rows", [P, NROWS]), sb("const", [P, NCONST])
        pos = sb("pos", [P, NANG], I32)
        ada = sb("ada", [P, 2, 3 * KT])
        cond = sb("cond", [P, KT])
        stats = sb("stats", [P, 980])
        tmp = [Buf(sb(f"tmp{i}", [P, 512])) for i in range(2)]
        banks = [Buf(ctx.enter_context(nc.psum_tensor(f"bank{i}", [P, 512], F32))) for i in range(8)]

        col = lambda n: cols[:, COLS[n][0]:COLS[n][1]]
        row = lambda n: rows[:, ROWS[n][0]:ROWS[n][1]]
        con = lambda n: const[:, CONST[n][0]:CONST[n][1]]
        ident = con("ident")

        used = [0]

        def stat(n):
            used[0] += n
            assert used[0] <= 980
            return stats[:, used[0] - n:used[0]]

        def load(dst, src, name, after=()):
            s = sem(name)
            sync_steps.append((list(after), lambda e: e.dma_start(dst, src).then_inc(s, 16)))
            return (s, 16)

        const_in = load(const[:, :], const_d, "const_in")
        cols_in = load(cols[:, :], cols_d, "cols_in")

        fetched, split_done, turn = {}, {}, {}
        next_split, next_rest = [0, 0], [0]

        def fetch(u):
            if u >= len(units):
                return
            _, _, m, n, _, at = units[u]
            b, s = raw[u % NRAW], raw_sem[u % NRAW]
            sync_steps.append((list(b.free), lambda e: e.dma_start(
                b.t[:, 0:m * n], wts[:, at:at + m * n]).then_inc(s, 16)))
            fetched[u] = (s, 16 * (u // NRAW + 1))

        def round_unit(u):
            _, _, m, n, _, _ = units[u]
            i = next_split[1] % NSPLIT
            next_split[1] += 1
            r, hi, c = raw[u % NRAW], w_hi[i], m * n
            a = SE([fetched[u], *hi.free], lambda e: e.activation(hi.t[:, 0:c], r.t[:, 0:c], ACT.Copy))
            turn[u], split_done[u] = i, [a]

        def rest_of_unit(u):
            _, _, m, n, _, _ = units[u]
            r, hi, lo, c = raw[u % NRAW], w_hi[turn[u]], w_lo[turn[u]], m * n
            b = VE([*split_done[u], *hi.free], lambda e: e.tensor_tensor(
                lo[:, 0:c], r.t[:, 0:c], hi.t[:, 0:c].bitcast(F32), ALU.subtract))
            r.free = [b]
            split_done[u].append(b)
            fetch(u + NRAW)

        put_off = []

        def later(n, fn):
            put_off.append([n, fn])

        def run_due(step=1):
            for entry in list(put_off):
                entry[0] -= step
                if entry[0] <= 0:
                    put_off.remove(entry)
                    entry[1]()

        def run_all():
            while put_off:
                run_due(99)

        taken = [0]

        def take(name):
            u = taken[0]
            taken[0] += 1
            assert units[u][0] == name, (units[u][0], name)
            while next_split[0] <= min(u + NSPLIT - 1, len(units) - 1):
                v = next_split[0]
                next_split[0] += 1
                if units[v][4]:
                    round_unit(v)
            while next_rest[0] <= min(u + NSPLIT - 2, len(units) - 1):
                v = next_rest[0]
                next_rest[0] += 1
                if units[v][4]:
                    rest_of_unit(v)
            return u

        def used_split(u, t):
            assert len(split_done[u]) == 2
            w_hi[turn[u]].free = [t]

        def used_raw(u, t):
            raw[u % NRAW].free = [t]
            fetch(u + NRAW)

        acc_turn = [0]

        def acc_pair():
            acc_turn[0] += 1
            i = 2 * (acc_turn[0] % 2)
            return banks[i], banks[i + 1]

        def chunk_size(name):
            return next((kt, n) for c, kt, n, _ in chunk_list() if c == name)

        def linear(name, lhs, ready, tokens_out, k0=0):
            pair = acc_pair()
            hi, lo = lhs
            kts, n = chunk_size(name)
            done, k, ticket = 0, 0, None
            while k < kts:
                u = take(name)
                _, _, m, _, _, _ = units[u]
                wh, wl = w_hi[turn[u]].t, w_lo[turn[u]]

                def products(e, k=k, m=m, wh=wh, wl=wl):
                    for kk in range(m):
                        a = k0 + k + kk
                        if tokens_out:
                            for t in range(TT):
                                o = pair[t].t[:, 0:n]
                                xs = [z[:, a, t * P:(t + 1) * P] for z in (hi, lo)]
                                ws = [z[:, kk * n:(kk + 1) * n] for z in (wh, wl)]
                                for i, (q, w) in enumerate(((0, 0), (0, 1), (1, 0))):
                                    mm = e.matmul(o, xs[q], ws[w], start=(k + kk == 0 and i == 0),
                                                  stop=(k + kk == kts - 1 and i == 2))
                        else:
                            for b in range(n // P):
                                o = pair[b // 2].t[:, (b % 2) * S:(b % 2) * S + S]
                                xs = [z[:, a, :] for z in (hi, lo)]
                                ws = [z[:, kk * n + b * P:kk * n + (b + 1) * P] for z in (wh, wl)]
                                for i, (w, q) in enumerate(((0, 0), (0, 1), (1, 0))):
                                    mm = e.matmul(o, ws[w], xs[q], start=(k + kk == 0 and i == 0 and b % 2 == 0),
                                                  stop=(k + kk == kts - 1 and i == 2 and b % 2 == 1),
                                                  skip_group_check=True)
                    return mm

                acts = [w for a in ready[k0 + k:k0 + k + m] for w in a]
                waits = [*split_done[u], *acts] + (pair[0].free + pair[1].free if k == 0 else [])
                ticket = PE(waits, products)
                used_split(u, ticket)
                k += m
                run_due()
                yield
            return pair, ticket

        aux_turn = [0]

        def aux():
            aux_turn[0] += 1
            return banks[4 + aux_turn[0] % 3]

        def transposes(bank, waits, parts):
            def emit(e):
                for o, src in parts:
                    mm = e.transpose(bank.t[0:int(np.prod(src.shape[1:])), o:o + src.shape[0]], src, ident)
                return mm
            return PE([*waits, *bank.free, const_in], emit)

        def split_to(hi, lo, src, waits, scale=1.0):
            a = SE(waits, lambda e: e.activation(hi, src, ACT.Copy, scale=scale))
            b = VE([a, *waits], lambda e: e.scalar_tensor_tensor(lo, src, scale, hi.bitcast(F32), ALU.mult,
                                                                 ALU.subtract))
            return [a, b]

        tmp_turn = [0]

        def scratch():
            tmp_turn[0] += 1
            return tmp[tmp_turn[0] % 2]

        minus_half = stat(2 * NH)
        fill = GP([], lambda e: e.memset(minus_half, -0.5))

        def rsqrt(out, ms, waits):
            n = ms.shape[1]
            a = GP([*waits, fill], lambda e: e.tensor_scalar(ms, ms, EPS, None, ALU.add))
            return GP([a], lambda e: e.tensor_tensor(out, ms, minus_half[:, 0:n], ALU.pow))

        scr_buf = Buf(scr)

        def norm(ready, sc, sh=None, sc_ready=()):
            ms, rs = stat(TT), stat(TT)
            sq = [SE([*ready, *scr_buf.free], lambda e, t=t: e.activation(
                scr[:, t, :], x[:, t, :], ACT.Square, scale=D ** -0.5, accum_out=ms[:, t:t + 1])) for t in range(TT)]
            r = rsqrt(rs, ms, sq)
            xn = [VE([r, *ready], lambda e, t=t: e.tensor_scalar(scr[:, t, :], x[:, t, :], rs[:, t:t + 1], None,
                                                                 ALU.mult)) for t in range(TT)]
            out = []
            for k in range(0, KT, 2):
                b = aux()
                tr = transposes(b, xn, [((kk - k) * S + t * P, scr[:, t, kk * P:(kk + 1) * P])
                                        for kk in (k, k + 1) for t in range(TT)])
                v = scratch()
                for i, kk in enumerate((k, k + 1)):
                    src, dst = b.t[:, i * S:(i + 1) * S], v.t[:, i * S:(i + 1) * S]
                    w = [tr, *v.free, *sc_ready]
                    if sh is None:
                        last = VE(w, lambda e, s=src, d=dst, kk=kk: e.tensor_scalar(
                            d, s, sc[:, kk:kk + 1], None, ALU.mult))
                    else:
                        last = VE(w, lambda e, s=src, d=dst, kk=kk: e.tensor_scalar(
                            d, s, sc[:, kk:kk + 1], sh[:, kk:kk + 1], ALU.mult, ALU.add))
                b.free = [last]
                v.free = split_to(h_hi[:, k:k + 2, :], h_lo[:, k:k + 2, :],
                                  v.t[:, :].rearrange("p (k t) -> p k t", k=2), [last])
                out += [v.free, v.free]
            scr_buf.free = [tr]
            return out

        def bcast(a, shape):
            return a.to_broadcast(shape)

        sq_buf = Buf(sb("squares", [P, TT, 512]))

        rope_tmp = [sb(f"rope_tmp{i}", [P, S]) for i in range(2)]
        rope_free = []

        def rope(v, cs, sn, n, dim, ready):
            half = dim // 2
            a1, a2 = (z[:, 0:n * dim].rearrange("p (h d) -> p h d", d=dim) for z in rope_tmp)
            s = lambda z, a, b: bcast(z[:, a:b].unsqueeze(1), [P, n, b - a])
            w = [*ready, trig, *rope_free]
            GP(w, lambda e: e.tensor_tensor(a1, v, s(cs, 0, dim), ALU.mult))
            GP(w, lambda e: e.tensor_tensor(a2[:, :, 0:half], v[:, :, half:dim], s(sn, 0, half), ALU.mult))
            k = GP(w, lambda e: e.tensor_tensor(a2[:, :, half:dim], v[:, :, 0:half], s(sn, half, dim), ALU.mult))
            last = GP([k], lambda e: e.tensor_tensor(v, a1, a2, ALU.add))
            rope_free[:] = [last]
            return last

        def head_norm(pair, ready, parts, heads, dim, turn=None, war=(), then=None):
            ms, rs = stat(TT * heads), stat(TT * heads)
            tr = []
            for t in range(TT):
                src = pair[t].t[:, 0:heads * dim]
                a = SE([*ready, *sq_buf.free], lambda e, t=t, s=src: e.activation(
                    sq_buf.t[:, t, 0:heads * dim], s, ACT.Square, scale=dim ** -0.5))
                tr.append(VE([a], lambda e, t=t: e.reduce_sum(
                    ms[:, t * heads:(t + 1) * heads],
                    sq_buf.t[:, t, 0:heads * dim].rearrange("p (h d) -> p h d", d=dim), AX.X)))
            sq_buf.free = tr
            r = rsqrt(rs, ms, tr)
            pair[0].free = pair[1].free = None

            def rest():
                out = []
                for t in range(TT):
                    muls = []
                    for h0, n, gain, dst in parts:
                        src = pair[t].t[:, h0 * dim:(h0 + n) * dim].rearrange("p (h d) -> p h d", d=dim)
                        rr = rs[:, t * heads + h0:t * heads + h0 + n].unsqueeze(2)
                        a = VE([r, *ready, *war], lambda e, s=src, rr=rr, d=dst(t), n=n: e.tensor_tensor(
                            d, s, bcast(rr, [P, n, dim]), ALU.mult))
                        muls.append(a)
                        a = GP([a, rows_in], lambda e, d=dst(t), g=gain, n=n: e.tensor_tensor(
                            d, d, bcast(g.unsqueeze(1), [P, n, dim]), ALU.mult))
                        if turn is not None:
                            d0, dn, cs, sn = turn
                            a = rope(dst(t)[:, :, d0:d0 + dn], table(cs, t), table(sn, t), n, dn, [a])
                        out.append(a)
                    pair[t].free = muls
                if then is not None:
                    later(3, lambda: then(out))

            later(1, rest)

        fetch(0)
        x_in = load(x[:, :, :], x_d.rearrange("o (t p) d -> p (o t) d", p=P), "x_in")
        pos_in = load(pos[:, :], pos_d, "pos_in")
        rows_in = load(rows[:, :], rows_d.to_broadcast([P, NROWS]), "rows_in")
        for u in range(1, NRAW):
            fetch(u)

        cond_in = SE([cols_in], lambda e: e.activation(cond[:, :], col("c"), ACT.Silu))

        ang, turns, sin_t, cos_t = (sb(n, [P, NANG]) for n in ("ang", "turns", "sin_t", "cos_t"))
        a = VE([pos_in, const_in], lambda e: e.tensor_copy(ang[:, :], pos[:, :]))
        a = VE([a], lambda e: e.tensor_tensor(ang[:, :], ang[:, :], con("freq"), ALU.mult))
        a = VE([a], lambda e: e.tensor_scalar(turns[:, :], ang[:, :], 1.0 / TWO_PI, None, ALU.mult))
        a = VE([a], lambda e: e.tensor_scalar(turns[:, :], turns[:, :], ROUND, None, ALU.add))
        a = VE([a], lambda e: e.tensor_scalar(turns[:, :], turns[:, :], -ROUND, None, ALU.add))
        for part in PI_PARTS:
            a = VE([a], lambda e, c=part: e.scalar_tensor_tensor(ang[:, :], turns[:, :], -c, ang[:, :], ALU.mult,
                                                                 ALU.add))
        b = VE([a], lambda e: e.tensor_scalar(cos_t[:, :], ang[:, :], TWO_PI / 4, None, ALU.add))
        c = VE([b], lambda e: e.tensor_scalar(turns[:, :], cos_t[:, :], TWO_PI / 2, -TWO_PI, ALU.is_gt, ALU.mult))
        c = VE([c], lambda e: e.tensor_tensor(cos_t[:, :], cos_t[:, :], turns[:, :], ALU.add))
        c = VE([c], lambda e: e.tensor_scalar(cos_t[:, :], cos_t[:, :], PI_LOW, -PI_LOW, ALU.min, ALU.max))
        a = VE([a], lambda e: e.tensor_scalar(ang[:, :], ang[:, :], PI_LOW, -PI_LOW, ALU.min, ALU.max))
        sin_in = SE([a, c], lambda e: e.activation(sin_t[:, :], ang[:, :], ACT.Sin))
        cos_in = SE([c], lambda e: e.activation(cos_t[:, :], cos_t[:, :], ACT.Sin))
        cs1, sn1 = (sb(n, [P, TT + 1, 2, 8]) for n in ("cs1", "sn1"))
        cs2, sn2 = (sb(n, [P, TT, 2, 16]) for n in ("cs2", "sn2"))
        for cs, sn, n, w, lo in ((cs1, sn1, TT + 1, 8, 0), (cs2, sn2, TT, 16, (TT + 1) * 8)):
            ca = cos_t[:, lo:lo + n * w].rearrange("p (t f) -> p t f", f=w)
            sa = sin_t[:, lo:lo + n * w].rearrange("p (t f) -> p t f", f=w)
            for i in range(2):
                trig = VE([cos_in], lambda e, d=cs[:, :, i, :], s=ca: e.tensor_copy(d, s))
                trig = VE([sin_in], lambda e, d=sn[:, :, i, :], s=sa, i=i: e.tensor_scalar(
                    d, s, 2.0 * i - 1.0, None, ALU.mult))
        table = lambda z, t: z[:, t, :, :].rearrange("p a f -> p (a f)")

        ada_acc = [Buf(sb(f"ada_acc{i}", [P, 512])) for i in range(2)]
        ada_done, gate_ready, gate_free = {}, [], []
        ones = con("ones")

        def adaptive(i, chunks, engine):
            for n in chunks:
                b, eng, k = ada_acc[n % 2], engine(n), 0
                a = None
                while k < KT:
                    u = take(f"ada{i}_{n}")
                    m, w = units[u][2], raw[u % NRAW].t
                    for kk in range(m):
                        src, cc = w[:, kk * 512:(kk + 1) * 512], cond[:, k + kk:k + kk + 1]
                        waits = [fetched[u], cond_in, *b.free] + ([a] if a else [])
                        if k + kk == 0:
                            a = eng(waits, lambda e, b=b, s=src, c=cc: e.tensor_scalar(b.t[:, :], s, c, None, ALU.mult))
                        else:
                            a = eng(waits, lambda e, b=b, s=src, c=cc: e.scalar_tensor_tensor(
                                b.t[:, :], s, c, b.t[:, :], ALU.mult, ALU.add))
                    used_raw(u, a)
                    k += m
                    if k < KT:
                        yield
                if n < 4:
                    bank = acc_pair()[0]

                    def columns(e, b=b, bank=bank):
                        for j in range(4):
                            mm = e.matmul(bank.t[:, j:j + 1], b.t[:, j * P:(j + 1) * P], ones[:, 0:1],
                                          start=True, stop=True)
                        return mm

                    t = PE([a, const_in, *bank.free], columns)
                    bias = col(f"ada{i}")
                    c = VE([t, cols_in], lambda e, n=n, bank=bank, bias=bias: e.tensor_tensor(
                        ada[:, i, 4 * n:4 * n + 4], bank.t[:, 0:4], bias[:, 4 * n:4 * n + 4], ALU.add))
                    if n == 3:
                        ada_done[i] = VE([c], lambda e: e.scalar_tensor_tensor(
                            ada[:, i, KT:2 * KT], ada[:, i, KT:2 * KT], 1.0, col(f"norm{i}"), ALU.add, ALU.mult))
                else:
                    bank = acc_pair()[0]
                    t = PE([a, const_in, *bank.free], lambda e, b=b, bank=bank: e.matmul(
                        bank.t[:, :], ones, b.t[:, :], start=True, stop=True))
                    j = n - 4
                    c = VE([t, bias_in[i], *gate_free], lambda e, j=j, bank=bank: e.tensor_tensor(
                        gate_row[:, j * 512:(j + 1) * 512], bank.t[:, :], gate_bias[:, j * 512:(j + 1) * 512],
                        ALU.add))
                    gate_ready.append(c)
                bank.free = [c]
                b.free = [t]
                yield

        def attention(items, pt, sm, background, per_slot, hooks={}):
            state, closing = {}, []

            def scores(i):
                it, bank = items[i], banks[4 + i % 2]

                def emit(e):
                    e.matmul(bank.t[:, 0:P], it["q"](0), it["k"](P), start=True, stop=True)
                    return e.matmul(bank.t[:, P:3 * P], it["q"](1), it["k"](S), start=True, stop=True)

                state[i] = PE([*it["ready"], *bank.free], emit)

            def weights(i):
                it, bank, m, t = items[i], banks[4 + i % 2], sm[i % len(sm)], state[i]
                mx, ng, su, rc = (stat(TT) for _ in range(4))
                mask = con("causal")
                a = VE([t, *m.free], lambda e: e.tensor_tensor_reduce(
                    m.t[:, 0:P], bank.t[:, 0:P], mask[:, P:S], 1.0, -3e38, ALU.add, ALU.max, mx[:, 0:1]))
                b = VE([t, *m.free], lambda e: e.tensor_tensor_reduce(
                    m.t[:, P:3 * P], bank.t[:, P:3 * P], mask, 1.0, -3e38, ALU.add, ALU.max, mx[:, 1:2]))
                bank.free = [b]
                c = VE([a, b], lambda e: e.tensor_scalar(ng, mx, -it["scale"], None, ALU.mult))
                d = SE([c], lambda e: e.activation(m.t[:, 0:P], m.t[:, 0:P], ACT.Exp, bias=ng[:, 0:1],
                                                   scale=it["scale"], accum_out=su[:, 0:1]))
                d = SE([c], lambda e: e.activation(m.t[:, P:3 * P], m.t[:, P:3 * P], ACT.Exp, bias=ng[:, 1:2],
                                                   scale=it["scale"], accum_out=su[:, 1:2]))
                state[i] = [m, su, rc, d]

            def divide(i):
                it = items[i]
                m, su, rc, d = state[i]
                a = VE([d], lambda e: e.reciprocal(rc, su))
                if it["gate"] is not None:
                    a = VE([a, *it["gate_ready"]], lambda e: e.tensor_tensor(rc, rc, it["gate"], ALU.mult))
                b = VE([a], lambda e: e.tensor_scalar(m.t[:, 0:P], m.t[:, 0:P], rc[:, 0:1], None, ALU.mult))
                b = VE([a], lambda e: e.tensor_scalar(m.t[:, P:3 * P], m.t[:, P:3 * P], rc[:, 1:2], None, ALU.mult))
                state[i].append(b)

            def turn_over(i):
                m, p, bank = state[i][0], pt[i % len(pt)], banks[6]
                t = transposes(bank, [state[i][-1]], [(0, m.t[:, 0:P]), (P, m.t[:, P:2 * P]),
                                                      (2 * P, m.t[:, 2 * P:3 * P])])
                m.free = [t]
                a = SE([t, *p.free], lambda e: e.activation(p.t[:, :], bank.t[:, 0:3 * P], ACT.Copy))
                bank.free = [a]
                state[i] = [p, a]

            def values(i):
                it = items[i]
                p, a = state.pop(i)
                o = it["out"]

                def emit(e):
                    if it["before"]:
                        it["before"](e)
                    e.matmul(o, it["v"](0), p.t[:, 0:S], start=it["first"] and not it["before"], stop=False,
                             skip_group_check=True)
                    return e.matmul(o[:, P:S], it["v"](1), p.t[:, S:S + P], start=False, stop=it["last"],
                                    skip_group_check=True)

                t = PE([a, *it["v_ready"], *(it["o_buf"].free if it["first"] else [])], emit)
                p.free = [t]
                if it["close"]:
                    closing.append(it["close"](t))

            n = len(items)
            for i in range(n + 3):
                if i in hooks:
                    hooks[i]()
                if i < n:
                    scores(i)
                if 0 <= i - 1 < n:
                    weights(i - 1)
                while closing:
                    closing.pop(0)()
                if 0 <= i - 2 < n:
                    divide(i - 2)
                    turn_over(i - 2)
                if 0 <= i - 3 < n:
                    values(i - 3)
                for _ in range(per_slot):
                    next(background, None)
            while closing:
                closing.pop(0)()
            for _ in background:
                pass

        def gqa_item(q_t, k_t, pr, half, v, ready, v_ready, o_buf, out, **more):
            hs = slice(half * HD, (half + 1) * HD)
            return dict(q=lambda t: q_t[hs, pr, t * P:(t + 1) * P], k=lambda n: k_t[hs, 0:n], v=v, ready=ready,
                        v_ready=v_ready, scale=HD ** -0.5, o_buf=o_buf, out=out, **more)

        def residual(names, lhs, ready, scale, x_ready, src=None):
            last = []
            for j, name in enumerate(names):
                pair, t = yield from linear(name, lhs, ready, True)
                for tt in range(TT):
                    o = x[:, tt, j * 512:(j + 1) * 512]
                    if scale is None:
                        v = scratch()
                        a = VE([t, *gate_ready, *v.free], lambda e, v=v, tt=tt, j=j, pair=pair: e.tensor_tensor(
                            v.t[:, :], pair[tt].t[:, :], gate_row[:, j * 512:(j + 1) * 512], ALU.mult))
                        b = VE([a, *x_ready], lambda e, v=v, o=o: e.tensor_tensor(o, o, v.t[:, :], ALU.add))
                        v.free = [b]
                        pair[tt].free = [a]
                    else:
                        b = VE([t, *x_ready], lambda e, o=o, tt=tt, pair=pair: e.scalar_tensor_tensor(
                            o, pair[tt].t[:, :], scale, o, ALU.mult, ALU.add))
                        pair[tt].free = [b]
                    last.append(b)
            return last

        mix = ExitStack()
        tokq = sb("tokq", [P, TT, 1024], on=mix)
        tokk = sb("tokk", [P, TT, 512], on=mix)
        tokv = sb("tokv", [P, TT, 512], on=mix)
        q_t = sb("q_t", [P, NP, S], on=mix)
        k_t = sb("k_t", [P, 4, S], on=mix)
        zs = sb("zs", [P, 16, S], on=mix)
        o_hi, o_lo = (sb(n, [P, KT, S], F32R, on=mix) for n in ("o_hi", "o_lo"))
        soft = [Buf(sb(f"soft{i}", [P, 3 * P], on=mix)) for i in range(3)]
        prob_t = [Buf(sb(f"prob_t{i}", [P, 3 * P], on=mix)) for i in range(2)]
        gate_row = sb("gate_row", [P, D], on=mix)
        gate_bias = sb("gate_bias", [P, D], on=mix)
        gates = sb("gates", [P, TT, 3 * NH], on=mix)
        hid = sb("hid", [P, 2, 2, NKV, CPAD], on=mix)
        pre = sb("pre", [P, 2, 256], on=mix)
        kc2 = sb("kc2", [P, 2, HD], on=mix)
        kc_two = sb("kc_two", [P, 2, 2 * CPAD], on=mix)
        vc = sb("vc", [P, NKV, HD], on=mix)
        pc_t = zs[:, 8:8 + NKV, :]
        bias_in = {0: load(gate_bias[:, :], gate_bias_d[0:1, :].to_broadcast([P, D]), "gate_bias0_in")}

        def q_heads(names, gain, ready, out):
            for j, name in enumerate(names):
                pair, t = yield from linear(name, (h_hi, h_lo), ready, True)
                view = lambda tt, j=j: tokq[:, tt, j * 512:(j + 1) * 512].rearrange("p (h d) -> p h d", d=HD)

                def then(done, j=j):
                    for p2 in range(2):
                        b = aux()
                        tr = transposes(b, done, [((pp * TT + tt) * P, tokq[:, tt, (j * 4 + 2 * p2 + pp) * P:
                                                                           (j * 4 + 2 * p2 + pp + 1) * P])
                                                  for pp in range(2) for tt in range(TT)])
                        c = SE([tr], lambda e, b=b, k=j * 4 + 2 * p2: e.activation(
                            q_t[:, k:k + 2, :].rearrange("p k t -> p (k t)"), b.t[:, :], ACT.Copy))
                        b.free = [c]
                        out.append(c)

                head_norm(pair, [t], [(0, 8, row(gain), view)], 8, HD, (0, 16, cs1, sn1), (), then)

        def z_gate(names, ready):
            zs_ready.clear()
            for j, name in enumerate(names):
                pair, t = yield from linear(name, (h_hi, h_lo), ready, False)
                for i in range(2):
                    v = scratch()
                    a = SE([t, *v.free], lambda e, v=v, i=i, pair=pair: e.activation(v.t[:, :], pair[i].t[:, :],
                                                                                     ACT.Tanh, scale=0.5))
                    k = j * 4 + 2 * i
                    b = VE([a], lambda e, v=v, i=i, k=k, pair=pair: e.scalar_tensor_tensor(
                        zs[:, k:k + 2, :].rearrange("p k t -> p (k t)"), v.t[:, :], 1.0, pair[i].t[:, :], ALU.add,
                        ALU.mult))
                    v.free = [b]
                    pair[i].free = [b]
                    zs_ready.append(b)

        zs_ready = []
        o_acc = Buf(banks[7].t[:, 0:S])

        def close_gated(pr, ob):
            def close(t):
                v = gated[pr % 2]
                a = VE([t, *zs_ready, *v.free], lambda e, v=v: e.scalar_tensor_tensor(
                    v.t[:, 0:S], ob.t, 0.5, zs[:, pr, :], ALU.mult, ALU.mult))
                ob.free = [a]
                b = SE([a], lambda e: e.activation(o_hi[:, pr, :], v.t[:, 0:S], ACT.Copy))

                def rest():
                    c = VE([b], lambda e: e.tensor_tensor(o_lo[:, pr, :], v.t[:, 0:S], o_hi[:, pr, :].bitcast(F32),
                                                          ALU.subtract))
                    o_ready[pr] = v.free = [b, c]
                return rest
            return close

        gated = [Buf(sb(f"gated{i}", [P, S], on=mix)) for i in range(2)]
        o_ready = {}
        kv = lambda tt, c0, n: tokk[:, tt, c0:c0 + n * HD].rearrange("p (h d) -> p h d", d=HD)

        def k_pairs(branches, done, out):
            for br in range(branches):
                b = aux()
                tr = transposes(b, done, [((g2 * TT + tt) * P, tokk[:, tt, br * S + g2 * P:br * S + (g2 + 1) * P])
                                          for g2 in range(2) for tt in range(TT)])
                for g2 in range(2):
                    c = SE([tr], lambda e, b=b, g2=g2, br=br: e.activation(
                        k_t[:, g2 * branches + br, :], b.t[:, g2 * S:(g2 + 1) * S], ACT.Copy))
                b.free = [c]
                out.append(c)

        drain_steps(adaptive(0, range(4), lambda n: VE))
        h0 = norm([x_in], ada[:, 0, KT:2 * KT], ada[:, 0, 0:KT], [ada_done[0]])

        by_parity = scr[:, :, :].rearrange("p t (g l d) -> p t g l d", g=8, l=2)
        NB = NKV * NCMP
        flat = [zs[:, 8 + 4 * i:12 + 4 * i, :].rearrange("p k t -> p (k t)")[:, 0:CJ * NB]
                .rearrange("p (j n) -> p j n", j=CJ) for i in range(2)]
        flat_ready = []

        def kcvc():
            pair, t = yield from linear("nsa_kcvc", (h_hi, h_lo), h0, True)
            bp = []
            for tt in range(TT):
                for lo in range(2):
                    src = pair[tt].t[:, :].rearrange("p (g d) -> p g d", d=HD)
                    par = con("parity")[:, lo:lo + 1]
                    if lo == 0:
                        e_ = VE([t, *scr_buf.free], lambda e, tt=tt, s=src, par=par: e.tensor_scalar(
                            by_parity[:, tt, :, 0, :], s, par, None, ALU.mult))
                    else:
                        e_ = SE([t, *scr_buf.free, e_], lambda e, tt=tt, s=src, par=par: e.activation(
                            by_parity[:, tt, :, 1, :], s, ACT.Copy, scale=par))
                    bp.append(e_)
            pair[0].free = pair[1].free = list(bp)

            def pair_tokens():
                for i in range(2):
                    b = aux()

                    def emit(e, i=i, b=b):
                        for g in range(NKV):
                            for tt in range(TT):
                                mm = e.matmul(b.t[:, g * P + tt * 64:g * P + (tt + 1) * 64],
                                              by_parity[:, tt, i * NKV + g, :, :].rearrange("p l d -> p (l d)"),
                                              con("pair"), start=True, stop=True)
                        return mm

                    t = PE([*bp, const_in, *b.free], emit)
                    window = bass.AP(b.t[:, :].tensor, b.t[:, :].offset,
                                     [list(b.t[:, :].ap[0]), [1, CJ], [P, NKV], [CMP_STRIDE // 2, NCMP]])
                    pe = col(f"pe{i}").unsqueeze(2).unsqueeze(3)
                    a = VE([t, cols_in], lambda e, i=i, w=window, pe=pe: e.tensor_tensor(
                        flat[i].rearrange("p j (g n) -> p j g n", g=NKV), w,
                        bcast(pe, [P, CJ, NKV, NCMP]), ALU.add))
                    b.free = [a]
                    scr_buf.free = [t]
                    flat_ready.append(a)

            later(2, pair_tokens)

        drain_steps(kcvc())
        q_ready = []
        drain_steps(q_heads(["nsa_q0", "nsa_q1"], "nsa_q", h0, q_ready))
        k_ready = []
        pair, t = drain_steps(linear("nsa_kskw", (h_hi, h_lo), h0, True))
        head_norm(pair, [t], [(0, 4, row("nsa_ks"), lambda tt: kv(tt, 0, 4)),
                              (4, 4, row("nsa_kw"), lambda tt: kv(tt, S, 4))], 8, HD, (0, 16, cs1, sn1), (),
                  lambda done: k_pairs(2, done, k_ready))

        zeros = [GP([], lambda e, z=z: e.memset(z, 0.0)) for z in
                 (hid[:, :, :, :, :], kc_two[:, :, :], vc[:, :, :])]

        def compress_up(i):
            bank = acc_pair()[0]
            k = 0
            while k < CJ:
                u = take(f"cmp_w1_{i}")
                m = units[u][2]

                def products(e, k=k, m=m, w=raw[u % NRAW].t):
                    for kk in range(m):
                        mm = e.matmul(bank.t[0:NB, 0:256], flat[i][:, k + kk, :], w[:, kk * 256:(kk + 1) * 256],
                                      start=(k + kk == 0), stop=(k + kk == CJ - 1))
                    return mm

                t = PE([fetched[u], flat_ready[i], *(bank.free if k == 0 else [])], products)
                used_raw(u, t)
                k += m
                run_due()
            a = SE([t], lambda e: e.activation(pre[0:NB, i, :], bank.t[0:NB, 0:256], ACT.Copy))
            bank.free = [a]
            return a

        cmp_out = {}

        def compress_down(i, up):
            b = aux()

            def turned(e):
                for j in range(2):
                    mm = e.transpose(b.t[:, j * 64:j * 64 + NB], pre[0:NB, i, j * P:(j + 1) * P], ident[0:NB, 0:NB])
                return mm

            t = PE([up, const_in, *b.free], turned)
            b1 = col(f"b1_{i}")
            ev = [SE([t, *zeros, cols_in], lambda e, j=j: e.activation(
                hid[:, i, j, :, 0:NCMP], b.t[:, j * 64:j * 64 + NB].rearrange("p (g n) -> p g n", g=NKV),
                ACT.Gelu_apprx_tanh, bias=b1[:, j:j + 1])) for j in range(2)]
            b.free = ev
            yield
            b2 = aux()
            w2 = col(f"w2_{i}")

            def emit(e):
                for j in range(2):
                    mm = e.matmul(b2.t[:, 0:HD], hid[:, i, j, :, :].rearrange("p g n -> p (g n)"),
                                  w2[:, j * HD:(j + 1) * HD], start=(j == 0), stop=(j == 1))
                return mm

            t = PE([*ev, *b2.free], emit)
            if i == 1:
                for g in range(NKV):
                    gs = slice(g * CPAD, (g + 1) * CPAD)
                    a = SE([t, *zeros], lambda e, g=g, gs=gs: e.activation(vc[gs, g, :], b2.t[gs, 0:HD], ACT.Copy))
                b2.free = [a]
                cmp_out["v"] = a
                return
            ms, rs = stat(1), stat(1)
            a = SE([t], lambda e: e.activation(kc2[:, 0, :], b2.t[:, 0:HD], ACT.Square, scale=HD ** -0.5,
                                               accum_out=ms))
            r = rsqrt(rs, ms, [a])
            a = VE([r, rows_in], lambda e: e.scalar_tensor_tensor(
                kc2[:, 0, :], b2.t[:, 0:HD], rs, row("nsa_kc"), ALU.mult, ALU.mult))
            b2.free = [a]
            a = rope(kc2[:, 0:1, 0:16], table(cs1, TT), table(sn1, TT), 1, 16, [a])
            a = GP([a], lambda e: e.tensor_copy(kc2[:, 1, :], kc2[:, 0, :]))
            yield
            b3 = aux()
            t = transposes(b3, [a], [(0, kc2[:, :, :].rearrange("p a d -> p (a d)"))])
            for g in range(NKV):
                hs, half = slice((g % 2) * HD, (g % 2 + 1) * HD), g % 2
                a = SE([t, *zeros], lambda e, g=g, hs=hs, half=half: e.activation(
                    kc_two[hs, g // 2, half * CPAD:(half + 1) * CPAD], b3.t[hs, g * CPAD:(g + 1) * CPAD], ACT.Copy))
            b3.free = [a]
            cmp_out["k"] = a

        ups = [compress_up(i) for i in range(2)]

        gates_ready = []
        pair, t = drain_steps(linear("nsa_gate", (h_hi, h_lo), h0, True))
        for tt in range(TT):
            a = VE([t, rows_in], lambda e, tt=tt, pair=pair: e.tensor_tensor(
                gates[:, tt, :], pair[tt].t[:, 0:3 * NH], row("gate_b"), ALU.add))
            pair[tt].free = [a]
            b = SE([a], lambda e, tt=tt: e.activation(gates[:, tt, :], gates[:, tt, :], ACT.Tanh, scale=0.5))
            gates_ready.append(VE([b], lambda e, tt=tt: e.tensor_scalar(gates[:, tt, :], gates[:, tt, :], 1.0, 0.5,
                                                                        ALU.add, ALU.mult)))

        v_ready = []

        def nsa_values():
            pair, t = yield from linear("nsa_vsvw", (h_hi, h_lo), h0, True)
            for tt in range(TT):
                a = SE([t], lambda e, tt=tt: e.activation(tokv[:, tt, :], pair[tt].t[:, :], ACT.Copy))
                pair[tt].free = [a]
                v_ready.append(a)

        def cmp_attention(tt):
            b = banks[4 + tt]
            s_ = scr[:, tt, 0:512]
            sv = s_.rearrange("p (h n) -> p h n", n=CPAD)
            hb = lambda z: bcast(z.unsqueeze(2), [P, NH, CPAD])

            def emit(e):
                for pr in range(NP):
                    mm = e.matmul(b.t[:, pr * 2 * CPAD:(pr + 1) * 2 * CPAD], q_t[:, pr, tt * P:(tt + 1) * P],
                                  kc_two[:, pr // 4, :], start=True, stop=True)
                return mm

            t = PE([*q_ready, cmp_out["k"], *b.free], emit)
            mx, su = stat(NH), stat(NH)
            mask = con("cmp_mask")[:, tt * CPAD:(tt + 1) * CPAD].unsqueeze(1)
            a = VE([t, *scr_buf.free], lambda e: e.tensor_tensor(
                sv, b.t[:, :].rearrange("p (h n) -> p h n", n=CPAD), bcast(mask, [P, NH, CPAD]), ALU.add))
            b.free = [a]
            c = VE([a], lambda e: e.reduce_max(mx, sv, AX.X))
            c = VE([c], lambda e: e.tensor_scalar(mx, mx, FLOOR, None, ALU.max))
            c = VE([c], lambda e: e.tensor_tensor(sv, sv, hb(mx), ALU.subtract))
            d = SE([c], lambda e: e.activation(s_, s_, ACT.Exp, scale=HD ** -0.5))
            yield
            c = VE([d], lambda e: e.reduce_sum(su, sv, AX.X))
            c = VE([c], lambda e: e.tensor_scalar(su, su, 1e-30, None, ALU.max))
            c = VE([c], lambda e: e.reciprocal(su, su))
            c = VE([c, *gates_ready], lambda e: e.tensor_tensor(su, su, gates[:, tt, 0:NH], ALU.mult))
            dst = scr[:, tt, 512:1024].rearrange("p (r g a n) -> p g r a n", r=4, g=2, a=2)
            for gp in range(2):
                c2 = VE([c], lambda e, gp=gp: e.tensor_tensor(
                    dst[:, gp, :, :, :], s_[:, gp * S:(gp + 1) * S].rearrange("p (r a n) -> p r a n", r=4, a=2),
                    bcast(su[:, gp * 8:gp * 8 + 8].rearrange("p (r a) -> p r a", a=2).unsqueeze(3), [P, 4, 2, CPAD]),
                    ALU.mult))
            c = c2
            yield
            b6 = banks[6]
            t = transposes(b6, [c], [(r * P, scr[:, tt, 512 + r * P:512 + (r + 1) * P]) for r in range(4)])
            a = SE([t], lambda e: e.activation(pc_t[:, :, tt * P:(tt + 1) * P],
                                               b6.t[:, :].rearrange("p (r t) -> p r t", r=4), ACT.Copy))
            b6.free = [a]
            cmp_ready.append(a)
            cmp_last[:] = [t]

        cmp_ready, cmp_last = [], []

        def compression():
            for i in range(2):
                yield from compress_down(i, ups[i])
                yield
            for tt in range(TT):
                yield from cmp_attention(tt)
                yield

        side = compression()

        def with_side(gen):
            while True:
                try:
                    next(gen)
                except StopIteration:
                    return
                next(side, None)

        with_side(nsa_values())
        with_side(z_gate(["nsa_z0", "nsa_z1"], h0))
        for _ in side:
            pass
        run_all()
        scr_buf.free = list(cmp_last)

        def gqa_item(pr, half, k, v, v_ready, **more):
            hs = slice(half * HD, (half + 1) * HD)
            return dict(q=lambda t: q_t[hs, pr, t * P:(t + 1) * P], k=lambda n: k_t[hs, k, 0:n], v=v,
                        ready=[*q_ready, *k_ready], v_ready=v_ready, scale=HD ** -0.5, o_buf=o_acc,
                        out=o_acc.t[hs, :], **more)

        items = []
        for pr in range(NP):
            for half in range(2):
                g, r = 2 * (pr // 4) + half, pr % 4

                def before(e, g=g, r=r, half=half):
                    e.matmul(o_acc.t[half * HD:(half + 1) * HD, :], vc[:, g, :], pc_t[:, r, :], start=True, stop=False,
                             skip_group_check=True)

                for br in range(2):
                    c = (br + 1) * NH + 2 * pr + half
                    items.append(gqa_item(
                        pr, half, (pr // 4) * 2 + br,
                        lambda j, br=br, g=g: tokv[:, j, br * S + g * HD:br * S + (g + 1) * HD],
                        [*v_ready, *cmp_ready, cmp_out["v"]],
                        gate=gates[:, :, c:c + 1].rearrange("p t o -> p (t o)"), gate_ready=gates_ready,
                        first=br == 0, last=br == 1, before=before if br == 0 else None,
                        close=close_gated(pr, o_acc) if br == 1 and half == 1 else None))

        def nsa_background():
            yield from adaptive(0, range(4, 6), lambda n: VE)
            yield from adaptive(1, range(4), lambda n: VE)

        attention(items, prob_t, soft, nsa_background(), 1)
        x0 = drain_steps(residual(["nsa_out0", "nsa_out1"], (o_hi, o_lo), [o_ready[k] for k in range(KT)], None, [x_in]))
        gate_free[:] = x0
        bias_in[1] = load(gate_bias[:, :], gate_bias_d[1:2, :].to_broadcast([P, D]), "gate_bias1_in", gate_ready)
        gate_ready.clear()

        h1 = norm(x0, ada[:, 1, KT:2 * KT], ada[:, 1, 0:KT], [ada_done[1]])
        q_ready, k_ready = [], []
        drain_steps(q_heads(["moba_q0", "moba_q1"], "moba_q", h1, q_ready))
        pair, t = drain_steps(linear("moba_kv", (h_hi, h_lo), h1, True))
        v_ready = [SE([t], lambda e, tt=tt, pair=pair: e.activation(tokv[:, tt, 0:S], pair[tt].t[:, S:2 * S], ACT.Copy))
                   for tt in range(TT)]
        head_norm(pair, v_ready, [(0, 4, row("moba_k"), lambda tt: kv(tt, 0, 4))], 4, HD, (0, 16, cs1, sn1), (),
                  lambda done: k_pairs(1, done, k_ready))
        zg = z_gate(["moba_z0", "moba_z1"], h1)
        for _ in range(5):
            next(zg)
        run_all()
        items = []
        for pr in range(NP):
            for half in range(2):
                g = 2 * (pr // 4) + half
                items.append(gqa_item(
                    pr, half, pr // 4, lambda j, g=g: tokv[:, j, g * HD:(g + 1) * HD], v_ready, gate=None, first=True,
                    last=True, before=None, close=close_gated(pr, o_acc) if half == 1 else None))

        def moba_background():
            yield from zg
            yield from adaptive(1, range(4, 6), lambda n: VE)

        attention(items, prob_t, soft, moba_background(), 2)
        x1 = drain_steps(residual(["moba_out0", "moba_out1"], (o_hi, o_lo), [o_ready[k] for k in range(KT)], None, x0))
        mix.close()

        def ffn(i, ready):
            with ExitStack() as own:
                a_hi, a_lo = (sb(f"a{i}_{n}", [P, FT, S], F32R, on=own) for n in ("hi", "lo"))
                act = [Buf(sb(f"act{i}_{n}", [P, TT, S], on=own)) for n in range(2)]
                hr = norm(ready, col(f"ffn{i}"), None, [cols_in])
                a_ready = {}
                for n in range(FT // 2):
                    pair, t = drain_steps(linear(f"ffn{i}_up{n}", (h_hi, h_lo), hr, True))
                    v = act[n % 2]
                    done = []
                    for tt in range(TT):
                        a = SE([t, *v.free], lambda e, v=v, tt=tt, pair=pair: e.activation(
                            v.t[:, tt, :], pair[tt].t[:, 0:S], ACT.Silu))
                        b = VE([a], lambda e, v=v, tt=tt, pair=pair: e.tensor_tensor(
                            v.t[:, tt, :], v.t[:, tt, :], pair[tt].t[:, S:2 * S], ALU.mult))
                        pair[tt].free = [b]
                        done.append(b)

                    def turn_over(n=n, v=v, done=done):
                        b = aux()
                        t = transposes(b, done, [((k * TT + tt) * P, v.t[:, tt, k * P:(k + 1) * P])
                                                 for k in range(2) for tt in range(TT)])
                        v.free = [t]
                        s2 = split_to(a_hi[:, 2 * n:2 * n + 2, :], a_lo[:, 2 * n:2 * n + 2, :],
                                      b.t[:, :].rearrange("p (k t) -> p k t", k=2), [t])
                        b.free = s2
                        a_ready[2 * n] = a_ready[2 * n + 1] = s2

                    later(1, turn_over)
                down = residual([f"ffn{i}_down0", f"ffn{i}_down1"], (a_hi, a_lo), TilesReady(a_ready, FT), 0.5, ready)
                return drain_steps(down)

        x2 = ffn(1, x1)

        mix = ExitStack()
        tokq = sb("tok2_q", [P, TT, MH * MQ], on=mix)
        tokk = sb("tok2_k", [P, TT, MH * MQ], on=mix)
        tokv2 = sb("tok2_v", [P, TT, 1024], on=mix)
        q2_t = sb("q2_t", [P, 8, S], on=mix)
        k2_t = sb("k2_t", [P, 8, S], on=mix)
        gate2 = sb("gate2", [P, 16, S], on=mix)
        o2_hi, o2_lo = (sb(n, [P, KT, S], F32R, on=mix) for n in ("o2_hi", "o2_lo"))
        soft2 = [Buf(sb(f"soft2_{i}", [P, 3 * P], on=mix)) for i in range(3)]
        prob2_t = [Buf(sb(f"prob2_t{i}", [P, 3 * P], on=mix)) for i in range(2)]
        l_hi, l_lo = (sb(n, [P, 3, S], F32R, on=mix) for n in ("l_hi", "l_lo"))
        decay = sb("decay", [P, 3, TT, FH], on=mix)
        half_b = sb("half_b", [P, 2 * KT], on=mix)
        lat = scr[:, :, 0:LAT]
        lz = [GP([*x2], lambda e, z=z: e.memset(z[:, 1, :].bitcast(F32), 0.0)) for z in (l_hi, l_lo)]
        hb_ready = VE([cols_in, *x2], lambda e: e.tensor_scalar(
            half_b[:, :], cols[:, COLS["gate_mla"][0]:COLS["gate_fox"][1]], 0.5, None, ALU.mult))

        h2 = norm(x2, col("mix"), None, [cols_in])
        pair, t = drain_steps(linear("mix_lat", (h_hi, h_lo), h2, True))
        lat_in = [SE([t, *scr_buf.free], lambda e, tt=tt, pair=pair: e.activation(lat[:, tt, :], pair[tt].t[:, 0:LAT],
                                                                                  ACT.Copy)) for tt in range(TT)]
        for tt in range(TT):
            pair[tt].free = [lat_in[tt]]
        parts = ((0, QL), (QL, KVL), (QL + KVL, MR))
        ms, rs = stat(TT * 3), stat(TT * 3)
        sq = []
        for tt in range(TT):
            for j, (c0, n) in enumerate(parts):
                sq.append(SE([lat_in[tt], *sq_buf.free], lambda e, tt=tt, j=j, c0=c0, n=n, ms=ms: e.activation(
                    sq_buf.t[:, tt, c0:c0 + n], lat[:, tt, c0:c0 + n], ACT.Square, scale=n ** -0.5,
                    accum_out=ms[:, tt * 3 + j:tt * 3 + j + 1])))
        lat_r = rsqrt(rs, ms, sq)
        sq_buf.free = sq
        lat_rs = rs
        l_ready = {}
        kr = []

        fl = []
        for tt in range(TT):
            f, s1 = decay[:, 0, tt, :], decay[:, 1, tt, :]
            a = VE([lat_in[tt], rows_in], lambda e, tt=tt, f=f: e.tensor_tensor(
                f, lat[:, tt, LAT - FH:LAT], row("fox_bf"), ALU.add))
            b = VE([a], lambda e, f=f, s1=s1: e.tensor_scalar(s1, f, -1.0, None, ALU.mult))
            b = VE([b], lambda e, f=f, s1=s1: e.tensor_tensor(s1, s1, f, ALU.min))
            c = SE([b], lambda e, s1=s1: e.activation(s1, s1, ACT.Exp))
            c = SE([c], lambda e, s1=s1: e.activation(s1, s1, ACT.Ln, bias=1.0))
            fl.append(VE([c], lambda e, f=f, s1=s1: e.scalar_tensor_tensor(f, f, 0.0, s1, ALU.min, ALU.subtract)))

        heads = lambda z, tt, w: z[:, tt, 0:8 * w].rearrange("p (h d) -> p h d", d=w)
        sums = {}

        def latents():
            ln = []
            for tt in range(TT):
                for j, (c0, n) in enumerate(parts):
                    ln.append(VE([lat_r, *sq], lambda e, tt=tt, j=j, c0=c0, n=n: e.tensor_scalar(
                        lat[:, tt, c0:c0 + n], lat[:, tt, c0:c0 + n], lat_rs[:, tt * 3 + j:tt * 3 + j + 1], None,
                        ALU.mult)))
            b = aux()

            def running(e):
                e.matmul(b.t[:, 0:FH], con("upto"), decay[:, 0, 0, :], start=True, stop=True)
                e.matmul(b.t[:, FH:2 * FH], con("ones"), decay[:, 0, 0, :], start=True, stop=False)
                return e.matmul(b.t[:, FH:2 * FH], con("upto"), decay[:, 0, 1, :], start=False, stop=True)

            t = PE([*fl, const_in, *b.free], running)
            sums["c"] = VE([t], lambda e: e.tensor_copy(decay[:, 2, :, :].rearrange("p t h -> p (t h)"),
                                                        b.t[:, 0:2 * FH]))
            b.free = [sums["c"]]
            later(1, lambda: latents_turned(ln))

        def latents_turned(ln):
            for j, (c0, n, gain) in enumerate(((0, P, col("q_lat")[:, 0:1]), (P, QL - P, col("q_lat")[:, 1:2]),
                                               (QL, KVL, col("kv_lat")))):
                b = aux()
                t = transposes(b, ln, [(tt * P, lat[:, tt, c0:c0 + n]) for tt in range(TT)])
                v = scratch()
                a = VE([t, cols_in, *v.free], lambda e, v=v, b=b, n=n, gain=gain: e.tensor_scalar(
                    v.t[0:n, 0:S], b.t[0:n, 0:S], gain[0:n, :], None, ALU.mult))
                b.free = [a]
                v.free = split_to(l_hi[0:n, j, :], l_lo[0:n, j, :], v.t[0:n, 0:S], [a, *lz])
                l_ready[j] = [*v.free, *lz]
            for tt in range(TT):
                k1 = lat[:, tt, QL + KVL:QL + KVL + MR].unsqueeze(1)
                a = GP([*ln, rows_in], lambda e, k1=k1: e.tensor_tensor(k1, k1, row("mla_kr").unsqueeze(1), ALU.mult))
                kr.append(rope(k1, table(cs2, tt), table(sn2, tt), 1, MR, [a]))

        later(1, latents)

        def heads_turned(src, dst, w, ready, h, bank, out):
            t = transposes(bank, ready, [((j * TT + tt) * P, heads(src, tt, w)[:, h + j, :])
                                         for j in range(2) for tt in range(TT)])
            c = SE([t, *scored], lambda e: e.activation(
                dst[0:w, h:h + 2, :].rearrange("p k t -> p (k t)"), bank.t[0:w, :], ACT.Copy))
            bank.free = [c]
            out.append(c)
            return t

        scored = []
        fq_ready, fk_ready, read_by = [], [], []

        def fox_queries(done):
            for tt in range(TT):
                v, cu = heads(tokq, tt, FK), decay[:, 2, tt, :].unsqueeze(2)
                done = [*done,
                        GP([*done], lambda e, v=v: e.tensor_scalar(v[:, :, 0:HD], v[:, :, 0:HD], HD ** -0.5, None,
                                                                   ALU.mult)),
                        GP([sums["c"]], lambda e, v=v, cu=cu: e.tensor_copy(v[:, :, HD:HD + 1], cu)),
                        GP([], lambda e, v=v: e.memset(v[:, :, HD + 1:HD + 2], 1.0))]
            later(2, lambda: [read_by.append(heads_turned(tokq, q2_t, FK, done, h, aux(), fq_ready))
                              for h in range(0, 8, 2)])

        def fox_keys(done):
            for tt in range(TT):
                v, cu = heads(tokk, tt, FK), decay[:, 2, tt, :].unsqueeze(2)
                done = [*done,
                        GP([sums["c"]], lambda e, v=v, cu=cu: e.tensor_scalar(v[:, :, HD + 1:HD + 2], cu, -1.0, None,
                                                                              ALU.mult)),
                        GP([], lambda e, v=v: e.memset(v[:, :, HD:HD + 1], 1.0))]
            later(2, lambda: [read_by.append(heads_turned(tokk, k2_t, FK, done, h, aux(), fk_ready))
                              for h in range(0, 8, 2)])

        def to_tokv(pair, t, c0):
            out = [SE([t], lambda e, tt=tt: e.activation(tokv2[:, tt, c0:c0 + 512], pair[tt].t[:, :], ACT.Copy))
                   for tt in range(TT)]
            for tt in range(TT):
                pair[tt].free = [out[tt]]
            return out

        pair, t = drain_steps(linear("fox_q", (h_hi, h_lo), h2, True))
        head_norm(pair, [t], [(0, FH, row("fox_q"), lambda tt: heads(tokq, tt, FK)[:, :, 0:HD])], FH, HD, None, (),
                  fox_queries)
        pair, t = drain_steps(linear("fox_k", (h_hi, h_lo), h2, True))
        head_norm(pair, [t], [(0, FH, row("fox_k"), lambda tt: heads(tokk, tt, FK)[:, :, 0:HD])], FH, HD, None, (),
                  fox_keys)
        pair, t = drain_steps(linear("fox_v", (h_hi, h_lo), h2, True))
        fv = to_tokv(pair, t, 512)
        run_all()
        l_list = [l_ready[j] for j in range(3)]
        mla_ready = []
        pair, t = drain_steps(linear("mla_qn", (l_hi, l_lo), l_list, True))
        head_norm(pair, [t], [(0, MH, row("mla_qn"), lambda tt: heads(tokq, tt, MQ)[:, :, 0:MN])], MH, MN, None,
                  read_by, mla_ready.extend)
        pair, t = drain_steps(linear("mla_qr", (l_hi, l_lo), l_list, True))
        head_norm(pair, [t], [(0, MH, row("mla_qr"), lambda tt: heads(tokq, tt, MQ)[:, :, MN:MQ])], MH, MR,
                  (0, MR, cs2, sn2), read_by, mla_ready.extend)
        pair, t = drain_steps(linear("mla_kn", (l_hi, l_lo), l_list, True, k0=2))
        head_norm(pair, [t], [(0, MH, row("mla_kn"), lambda tt: heads(tokk, tt, MQ)[:, :, 0:MN])], MH, MN, None,
                  read_by, mla_ready.extend)
        pair, t = drain_steps(linear("mla_v", (l_hi, l_lo), l_list, True, k0=2))
        mv = to_tokv(pair, t, 0)
        for tt in range(TT):
            k1 = lat[:, tt, QL + KVL:QL + KVL + MR].unsqueeze(1)
            mla_ready.append(GP([*kr, *read_by], lambda e, tt=tt, k1=k1: e.tensor_copy(
                heads(tokk, tt, MQ)[:, :, MN:MQ], bcast(k1, [P, MH, MR]))))

        o_ready = {}

        def close_plain(kt, ob):
            def close(t):
                b = SE([t], lambda e: e.activation(o2_hi[:, kt, :], ob.t, ACT.Copy))
                c = VE([b], lambda e: e.tensor_tensor(o2_lo[:, kt, :], ob.t, o2_hi[:, kt, :].bitcast(F32),
                                                      ALU.subtract))
                o_ready[kt] = ob.free = [b, c]
                return lambda: None
            return close

        def head_items(w, scale, v0, kt0, ready, vr):
            return [dict(q=lambda t, h=h: q2_t[0:w, h, t * P:(t + 1) * P], k=lambda n, h=h: k2_t[0:w, h, 0:n],
                         v=lambda j, h=h: tokv2[:, j, v0 + h * HD:v0 + (h + 1) * HD], ready=ready, v_ready=vr,
                         scale=scale, o_buf=o_acc, out=o_acc.t[(h % 2) * HD:(h % 2 + 1) * HD, :], gate=None,
                         first=True, last=True, before=None, close=close_plain(kt0 + h // 2, o_acc) if h % 2 else None)
                    for h in range(8)]

        result = []

        def gates_2():
            for j, name in enumerate(("gate_mla0", "gate_mla1", "gate_fox0", "gate_fox1")):
                pair, t = yield from linear(name, (h_hi, h_lo), h2, False)
                for i in range(2):
                    for b in range(2):
                        k = 4 * j + 2 * i + b
                        a = SE([t, hb_ready], lambda e, k=k, i=i, b=b, pair=pair: e.activation(
                            gate2[:, k, :], pair[i].t[:, b * S:(b + 1) * S], ACT.Tanh, bias=half_b[:, k:k + 1],
                            scale=0.5))
                    pair[i].free = [a]
            result.append(a)

        mla_heads = []

        def place(h):
            def hook():
                run_all()
                scored[:] = [(PE.sem, PE.count)]
                heads_turned(tokq, q2_t, MQ, mla_ready, h, banks[6], mla_heads)
                heads_turned(tokk, k2_t, MQ, mla_ready, h, banks[6], mla_heads)
            return hook

        attention(head_items(FK, 1.0, 512, 4, [*fq_ready, *fk_ready], fv)
                  + head_items(MQ, MQ ** -0.5, 0, 0, mla_heads, mv), prob2_t, soft2, gates_2(), 2,
                  {4: place(0), 5: place(2), 7: place(4), 9: place(6)})
        gates2_ready = result[-1]
        o_list = [o_ready[k] for k in range(KT)]

        mixed = scr[:, :, :].rearrange("p t (k s) -> p (t k) s", s=S)
        mm_ready = []
        for j in range(2):
            pair, t = drain_steps(linear(f"br_fox{j}", (o2_hi, o2_lo), o_list, False, k0=4))
            for i in range(2):
                k = 4 * j + 2 * i
                a = VE([t, gates2_ready, *mla_ready], lambda e, k=k, i=i, pair=pair: e.scalar_tensor_tensor(
                    mixed[:, k:k + 2, :], gate2[:, 8 + k:10 + k, :], 1.0,
                    pair[i].t[:, :].rearrange("p (k s) -> p k s", k=2), ALU.add, ALU.mult))
                pair[i].free = [a]
                mm_ready.append(a)
        m_ready = []
        for j in range(2):
            pair, t = drain_steps(linear(f"br_mla{j}", (o2_hi, o2_lo), o_list, False))
            for i in range(2):
                k = 4 * j + 2 * i
                v = scratch()
                vv = v.t[:, :].rearrange("p (k s) -> p k s", k=2)
                a = VE([t, *v.free], lambda e, k=k, i=i, vv=vv, pair=pair: e.scalar_tensor_tensor(
                    vv, gate2[:, k:k + 2, :], 1.0, pair[i].t[:, :].rearrange("p (k s) -> p k s", k=2),
                    ALU.add, ALU.mult))
                pair[i].free = [a]
                a = VE([a, *mm_ready], lambda e, k=k, vv=vv: e.tensor_tensor(vv, vv, mixed[:, k:k + 2, :], ALU.add))
                v.free = split_to(h_hi[:, k:k + 2, :], h_lo[:, k:k + 2, :], vv, [a], 0.5)
                m_ready += [v.free, v.free]
        scr_buf.free = [a]
        x3 = drain_steps(residual(["mix_out0", "mix_out1"], (h_hi, h_lo), m_ready, 1.0, x2))
        mix.close()

        x4 = ffn(2, x3)
        assert taken[0] == len(units)

        out_sem = sem("out_stored")
        sync_steps.append((x4, lambda e: e.dma_start(out_d.rearrange("o (t p) d -> p (o t) d", p=P),
                                                     x[:, :, :]).then_inc(out_sem, 16)))

        block = ctx.enter_context(nc.Block())

        @block.sync
        def _(e):
            met = {}
            for waits, emit in sync_steps:
                for s, value in waits:
                    if met.get(s.name, 0) < value:
                        e.wait_ge(s, value)
                        met[s.name] = value
                emit(e)
            e.wait_ge(out_sem, 16)

        @block.tensor
        def _(e):
            PE.run(e)

        @block.vector
        def _(e):
            VE.run(e)

        @block.scalar
        def _(e):
            SE.run(e)

        @block.gpsimd
        def _(e):
            GP.run(e)


def head_order():
    return [gp * 8 + half * 4 + r for gp in range(2) for r in range(4) for half in range(2)]


def chunk_arrays(a):
    pairs = head_order()
    hd = lambda hs: np.concatenate([np.arange(h * HD, (h + 1) * HD) for h in hs])
    perm = hd(pairs)
    w = a["nsa_w_in"][0]
    q, kc, vc, ks, vs, kw, vw, gl, z = np.split(w, np.cumsum([D] + [256] * 6 + [48])[:8], axis=1)
    out = {}
    for i in range(2):
        for n in range(6):
            out[f"ada{i}_{n}"] = a["ada_w"][i][:, n * 512:(n + 1) * 512]
    halves = lambda name, m: out.update({f"{name}{j}": m[:, j * 512:(j + 1) * 512] for j in range(2)})
    cat = lambda *m: np.concatenate(m, axis=1)
    out["nsa_kcvc"], out["nsa_kskw"], out["nsa_vsvw"] = cat(kc, vc), cat(ks, kw), cat(vs, vw)
    out["nsa_gate"] = gl.reshape(D, NH, 3)[:, pairs].transpose(0, 2, 1).reshape(D, 48)
    halves("nsa_q", q[:, perm])
    halves("nsa_z", z[:, perm])
    halves("nsa_out", a["nsa_w_out"][0][perm])
    for i in range(2):
        out[f"cmp_w1_{i}"] = a["nsa_cmp_w1"][0, i]
    q, k, v, z = np.split(a["moba_w_in"][0], np.cumsum([D, 256, 256]), axis=1)
    halves("moba_q", q[:, perm])
    out["moba_kv"] = cat(k, v)
    halves("moba_z", z[:, perm])
    halves("moba_out", a["moba_w_out"][0][perm])
    for i in (1, 2):
        g, u, d = (a[f"ffn{i}_w_{n}_2"][0] for n in ("gate", "up", "down"))
        for n in range(FT // 2):
            out[f"ffn{i}_up{n}"] = cat(g[:, n * 256:(n + 1) * 256], u[:, n * 256:(n + 1) * 256])
        halves(f"ffn{i}_down", d)
    ql, kvl, kr, fq, fk, fv, fl, gm, gf = np.split(
        a["w_in_2"][0], np.cumsum([QL, KVL, MR, 512, 512, 512, FH, D]), axis=1)
    out["mix_lat"] = cat(ql, kvl, kr, fl)
    out["fox_q"], out["fox_k"], out["fox_v"] = fq, fk, fv
    halves("gate_mla", gm)
    halves("gate_fox", gf)
    qb = a["mla_w_qb_2"][0].reshape(QL, MH, MQ)
    qb = np.concatenate([qb, np.zeros((2 * P - QL, MH, MQ), qb.dtype)])
    out["mla_qn"], out["mla_qr"] = qb[:, :, :MN].reshape(2 * P, -1), qb[:, :, MN:].reshape(2 * P, -1)
    kvb = a["mla_w_kvb_2"][0].reshape(KVL, MH, 2 * MN)
    out["mla_kn"], out["mla_v"] = kvb[:, :, :MN].reshape(KVL, -1), kvb[:, :, MN:].reshape(KVL, -1)
    halves("br_mla", a["w_branch_mla_2"][0])
    halves("br_fox", a["w_branch_fox_2"][0])
    halves("mix_out", a["w_o_2"][0])
    return out


def packed_weights(a):
    units, total = unit_list()
    mats = chunk_arrays(a)
    out = np.empty((P, total), np.float32)
    for name, k, m, n, _, at in units:
        part = mats[name][k * P:(k + m) * P]
        out[:, at:at + m * n] = part.reshape(m, P, n).transpose(1, 0, 2).reshape(P, m * n)
    return out


def packed_columns(a):
    out = np.zeros((P, NCOLS), np.float32)
    put = lambda name, v: out.__setitem__((slice(None), slice(*COLS[name])), v)
    by = lambda v: v.reshape(-1, P).T
    put("c", by(a["c"][0]))
    for i in range(2):
        put(f"norm{i}", by(a["norm_g"][i]))
        put(f"ada{i}", by(a["ada_b"][i]))
        put(f"b1_{i}", by(a["nsa_cmp_b1"][0, i]))
        put(f"pe{i}", a["nsa_cmp_pe"][0, i].reshape(CJ, P).T)
        put(f"w2_{i}", a["nsa_cmp_w2"][0, i].reshape(2, P, HD).transpose(1, 0, 2).reshape(P, 2 * HD))
    put("ffn1", by(a["ffn1_norm_2"][0]))
    put("mix", by(a["mix_norm_2"][0]))
    put("ffn2", by(a["ffn2_norm_2"][0]))
    put("gate_mla", by(a["b_gate_2"][0, 0]))
    put("gate_fox", by(a["b_gate_2"][0, 1]))
    ql = a["mla_q_lat_norm_2"][0]
    put("q_lat", by(np.concatenate([ql, np.zeros(2 * P - QL, ql.dtype)])))
    put("kv_lat", by(a["mla_kv_lat_norm_2"][0]))
    return out


def packed_rows(a):
    kn = a["nsa_k_norm"][0]
    gb = a["nsa_gate_b"][0].reshape(NH, 3)[head_order()].T.reshape(-1)
    return np.concatenate([a["nsa_q_norm"][0], kn[0], kn[1], kn[2], gb, a["moba_q_norm"][0], a["moba_k_norm"][0],
                           a["mla_q_nope_gain_2"][0], a["mla_q_rope_gain_2"][0], a["mla_k_nope_gain_2"][0],
                           a["mla_k_rope_gain_2"][0], a["fox_q_gain_2"][0], a["fox_k_gain_2"][0],
                           a["fox_b_f_2"][0]])[None, :]


def packed_positions(a):
    by = lambda v: v.reshape(TT, P).T
    p1, p2 = a["positions"][0], a["positions_2"][0]
    ends = np.zeros(P, p1.dtype)
    at = np.arange(NKV)[:, None] * CPAD + np.arange(NCMP)[None, :]
    ends[at] = p1[np.arange(NCMP) * CMP_STRIDE + CMP_LEN - 1][None, :]
    return np.concatenate([np.repeat(by(p1), 8, axis=1), np.repeat(ends[:, None], 8, axis=1),
                           np.repeat(by(p2), 16, axis=1)], axis=1)


def kernel(**inputs):
    import concourse.bacc as bacc
    from concourse.bass_utils import run_bass_kernel_spmd

    a = {k: np.asarray(v) for k, v in inputs.items()}
    arrays = {"in_weights": packed_weights(a), "in_columns": packed_columns(a), "in_rows": packed_rows(a),
              "in_constants": shape_constants(), "in_positions": packed_positions(a),
              "in_gate_bias": a["ada_b"][:, 2 * D:], "in_x": a["x"]}
    arrays = {k: np.ascontiguousarray(v) for k, v in arrays.items()}
    nc = bacc.Bacc("TRN2", target_bir_lowering=False, num_devices=1)
    args = [nc.dram_tensor(k, v.shape, mybir.dt.from_np(v.dtype), kind="ExternalInput").ap()
            for k, v in arrays.items()]
    out = nc.dram_tensor("out", a["x"].shape, F32, kind="ExternalOutput").ap()
    program(nc, *args, out)
    return run_bass_kernel_spmd(nc, [arrays], core_ids=[0]).results[0]["out"]
```

```python
import numpy as np
import concourse.bass as bass
from concourse import mybir
from concourse.alu_op_type import AluOpType as ALU
from contextlib import ExitStack
from itertools import chain

F32, F32R, I32 = mybir.dt.float32, mybir.dt.float32r, mybir.dt.int32
ACT = mybir.ActivationFunctionType
AX = mybir.AxisListType

P = 128
D = 1024
S = 256
TT = S // P
KT = D // P
HD = 64
NH, NKV = 16, 4
NP = NH // 2
FFN = 2816
FT = FFN // P
CMP_LEN, CMP_STRIDE = 32, 16
NCMP = (S - CMP_LEN) // CMP_STRIDE + 1
CPAD = 32
CJ = CMP_LEN // 2
MH, MN, MR = 8, 64, 32
MQ = MN + MR
FH, FK = 8, HD + 2
QL, KVL = 192, 128
LAT = QL + KVL + MR + FH
EPS = 1e-6
NEG, FLOOR = -1e30, -1e29
UNIT = 1024
Z_FIRST = 5
NRAW, NSPLIT = 7, 4
TWO_PI = 6.283185307179586
PI_PARTS = (6.28125, 0.0019340515136718750, 1.2554228305816650e-06)
PI_PARTS = PI_PARTS + (TWO_PI - sum(PI_PARTS),)
PI_LOW = 3.1415925
ROUND = 12582912.0


def units_of(chunks):
    return [(name, k, min(UNIT // n, kt - k), n, split, kt)
            for name, kt, n, split in chunks for k in range(0, kt, UNIT // n)]


def in_turn(a, b):
    n = min(len(a), len(b))
    return [u for pair in zip(a[:n], b[:n]) for u in pair] + a[n:] + b[n:]


def unit_list():
    ada = lambda i, n0, n1: units_of([(f"ada{i}_{n}", KT, 512, False) for n in range(n0, n1)])
    ffn = lambda i: units_of([(f"ffn{i}_up{n}", KT, 512, True) for n in range(FT // 2)]
                             + [(f"ffn{i}_down{n}", FT, 512, True) for n in range(2)])
    one = lambda name, k=KT, n=512, split=True: units_of([(name, k, n, split)])
    two = lambda name, k=KT: one(f"{name}0", k) + one(f"{name}1", k)
    z = two("moba_z")
    order = (ada(0, 0, 4)
             + one("nsa_kcvc") + one("nsa_kskw") + one("nsa_q0") + one("cmp_w1_0", CJ, 256, False)
             + one("nsa_q1") + one("cmp_w1_1", CJ, 256, False) + one("nsa_gate", KT, P)
             + one("nsa_vsvw") + one("nsa_z0") + in_turn(ada(0, 4, 6) + ada(1, 0, 4), one("nsa_z1"))
             + two("nsa_out")
             + two("moba_q") + one("moba_kv") + z[:Z_FIRST] + in_turn(ada(1, 4, 6), z[Z_FIRST:]) + two("moba_out")
             + ffn(1)
             + one("mix_lat", KT, LAT) + one("fox_q") + one("fox_k") + one("fox_v")
             + one("mla_qn", 2) + one("mla_qr", 2, 256) + one("mla_kn", 1) + one("mla_v", 1)
             + two("gate_mla") + two("gate_fox") + two("br_fox", KT // 2) + two("br_mla", KT // 2) + two("mix_out")
             + ffn(2))
    units, at = [], 0
    for u in order:
        units.append(u + (at,))
        at += u[2] * u[3]
    return units, at


def layout(sizes):
    at, out = 0, {}
    for name, n in sizes:
        out[name] = (at, at + n)
        at += n
    return out, at


COLS, NCOLS = layout([("c", KT), ("norm0", KT), ("norm1", KT), ("ada0", 3 * KT), ("ada1", 3 * KT),
                      ("ffn1", KT), ("mix", KT), ("ffn2", KT), ("gate_mla", KT), ("gate_fox", KT),
                      ("b1_0", 2), ("b1_1", 2), ("q_lat", 2), ("kv_lat", 1), ("pe0", CJ), ("pe1", CJ),
                      ("w2_0", 2 * HD), ("w2_1", 2 * HD), ("gate_b", 1),
                      ("nsa_q", 1), ("nsa_ks", 1), ("nsa_kw", 1), ("moba_q", 1), ("moba_k", 1),
                      ("mla_q", 1), ("mla_k", 1), ("fox_q", 1), ("fox_k", 1)])
ROT = 16
ROWS, NROWS = layout([("nsa_kc", HD), ("nsa_q", ROT), ("nsa_ks", ROT), ("nsa_kw", ROT), ("moba_q", ROT),
                      ("moba_k", ROT), ("mla_qr", MR), ("mla_kr", MR), ("fox_bf", FH)])
ANG, NANG = layout([("tok", TT * 8), ("cmp", 8), ("tok2", TT * 16)])
CONST, NCONST = layout([("ident", P), ("causal", S), ("pair", P // 2), ("parity", 2), ("cmp_mask", TT * CPAD),
                        ("upto", P), ("ones", P), ("freq", NANG), ("fox_scale", 1)])


def shape_constants():
    c = np.zeros((P, NCONST), np.float32)
    put = lambda name, a: c.__setitem__((slice(None), slice(*CONST[name])), a)
    p = np.arange(P)[:, None]
    put("ident", np.eye(P))
    put("causal", np.where(np.arange(S)[None, :] - P <= p, 0.0, NEG))
    put("pair", p // 2 == np.arange(P // 2)[None, :])
    put("parity", p % 2 == np.arange(2)[None, :])
    ends = np.arange(CPAD) * CMP_STRIDE + CMP_LEN - 1
    ok = (ends[None, None, :] <= p[:, :, None] + P * np.arange(TT)[None, :, None]) & (np.arange(CPAD) < NCMP)
    put("cmp_mask", np.where(ok, 0.0, NEG).reshape(P, -1))
    put("upto", p <= np.arange(P)[None, :])
    put("ones", 1.0)
    put("fox_scale", np.where(p < HD, HD ** -0.5, 1.0))
    f1 = np.float32(500000.0) ** (-np.arange(0, 16, 2, dtype=np.float32) / np.float32(16))
    f2 = np.float32(10000.0) ** (-np.arange(16, dtype=np.float32) / np.float32(16))
    put("freq", np.concatenate([np.tile(f1, TT), f1, np.tile(f2, TT)])[None, :])
    return c


class Engine:

    def __init__(self, sem):
        self.sem, self.count, self.steps = sem, 0, []

    def __call__(self, waits, emit):
        self.count += 1
        self.steps.append((list(waits), emit))
        return (self.sem, self.count)

    def run(self, eng):
        met = {}
        for waits, emit in self.steps:
            for sem, value in waits:
                if met.get(sem.name, 0) < value:
                    eng.wait_ge(sem, value)
                    met[sem.name] = value
            emit(eng).then_inc(self.sem, 1)


class Buf:

    def __init__(self, t):
        self.t, self.free = t, []


class TilesReady:

    def __init__(self, tickets):
        self.tickets = tickets

    def __getitem__(self, tiles):
        return [self.tickets[k] for k in range(tiles.start, tiles.stop)]


def drain_steps(gen):
    while True:
        try:
            next(gen)
        except StopIteration as e:
            return e.value


def program(nc, wts, cols_d, rows_d, const_d, pos_d, gate_bias_d, x_d, out_d):
    units, _ = unit_list()
    ctx = ExitStack()
    with ctx:
        sem = lambda n: ctx.enter_context(nc.semaphore(n))

        def sb(name, shape, dt=F32, on=ctx):
            return on.enter_context(nc.sbuf_tensor(name, shape, dt))

        PE, VE, SE, GP = (Engine(sem(n)) for n in ("pe_done", "dve_done", "act_done", "pool_done"))
        sync_steps = []

        raw = [Buf(sb(f"w_raw{i}", [P, UNIT])) for i in range(NRAW)]
        raw_sem = [sem(f"w_raw{i}_in") for i in range(NRAW)]
        w_hi = [Buf(sb(f"w_hi{i}", [P, UNIT], F32R)) for i in range(NSPLIT)]
        w_lo = [sb(f"w_lo{i}", [P, UNIT], F32R) for i in range(NSPLIT)]
        x = sb("x", [P, TT, D])
        h_hi, h_lo = (sb(n, [P, KT, S], F32R) for n in ("h_hi", "h_lo"))
        scr = sb("scr", [P, TT, D])
        cols, rows, const = sb("cols", [P, NCOLS]), sb("rows", [P, NROWS]), sb("const", [P, NCONST])
        pos = sb("pos", [P, NANG], I32)
        ada = sb("ada", [P, 2, 3 * KT])
        cond = sb("cond", [P, KT])
        stats = sb("stats", [P, 1010])
        tmp = [Buf(sb(f"tmp{i}", [P, 512])) for i in range(2)]
        banks = [Buf(ctx.enter_context(nc.psum_tensor(f"bank{i}", [P, 512], F32))) for i in range(8)]

        col = lambda n: cols[:, COLS[n][0]:COLS[n][1]]
        row = lambda n: rows[:, ROWS[n][0]:ROWS[n][1]]
        con = lambda n: const[:, CONST[n][0]:CONST[n][1]]
        ident = con("ident")

        used = [0]

        def stat(n):
            used[0] += n
            assert used[0] <= 1010
            return stats[:, used[0] - n:used[0]]

        def load(dst, src, name, after=()):
            s = sem(name)
            sync_steps.append((list(after), lambda e: e.dma_start(dst, src).then_inc(s, 16)))
            return (s, 16)

        const_in = load(const[:, :], const_d, "const_in")
        cols_in = load(cols[:, :], cols_d, "cols_in")

        fetched, split_done, turn = {}, {}, {}
        next_split, next_rest = [0, 0], [0]

        def fetch(u):
            if u >= len(units):
                return
            _, _, m, n, _, _, at = units[u]
            b, s = raw[u % NRAW], raw_sem[u % NRAW]
            sync_steps.append((list(b.free), lambda e: e.dma_start(
                b.t[:, 0:m * n], wts[:, at:at + m * n]).then_inc(s, 16)))
            fetched[u] = (s, 16 * (u // NRAW + 1))

        def round_unit(u):
            m, n = units[u][2:4]
            i = next_split[1] % NSPLIT
            next_split[1] += 1
            r, hi, c = raw[u % NRAW], w_hi[i], m * n
            a = SE([fetched[u], *hi.free], lambda e: e.activation(hi.t[:, 0:c], r.t[:, 0:c], ACT.Copy))
            turn[u], split_done[u] = i, [a]

        def rest_of_unit(u):
            m, n = units[u][2:4]
            r, hi, lo, c = raw[u % NRAW], w_hi[turn[u]], w_lo[turn[u]], m * n
            b = VE([*split_done[u], *hi.free], lambda e: e.tensor_tensor(
                lo[:, 0:c], r.t[:, 0:c], hi.t[:, 0:c].bitcast(F32), ALU.subtract))
            r.free = [b]
            split_done[u].append(b)
            fetch(u + NRAW)

        put_off = []

        def later(n, fn):
            put_off.append([n, fn])

        def run_due(step=1):
            for entry in list(put_off):
                entry[0] -= step
                if entry[0] <= 0:
                    put_off.remove(entry)
                    entry[1]()

        def run_all():
            while put_off:
                run_due(99)

        taken = [0]

        def take(name):
            u = taken[0]
            taken[0] += 1
            assert units[u][0] == name, (units[u][0], name)
            while next_split[0] <= min(u + NSPLIT - 1, len(units) - 1):
                v = next_split[0]
                next_split[0] += 1
                if units[v][4]:
                    round_unit(v)
            while next_rest[0] <= min(u + NSPLIT - 2, len(units) - 1):
                v = next_rest[0]
                next_rest[0] += 1
                if units[v][4]:
                    rest_of_unit(v)
            return u

        def used_split(u, t):
            assert len(split_done[u]) == 2
            w_hi[turn[u]].free = [t]

        def used_raw(u, t):
            raw[u % NRAW].free = [t]
            fetch(u + NRAW)

        acc_turn = [0]

        def acc_pair():
            acc_turn[0] += 1
            i = 2 * (acc_turn[0] % 2)
            return banks[i], banks[i + 1]

        def chunk_size(name):
            return next((kt, n) for c, _, _, n, _, kt, _ in units if c == name)

        tile_done = []

        def linear(name, lhs, ready, tokens_out, k0=0):
            pair = acc_pair()
            hi, lo = lhs
            kts, n = chunk_size(name)
            done, k, ticket = 0, 0, None
            while k < kts:
                u = take(name)
                m = units[u][2]
                wh, wl = w_hi[turn[u]].t, w_lo[turn[u]]

                def of_tokens(e, t, k=k, m=m, wh=wh, wl=wl):
                    for kk in range(m):
                        o = pair[t].t[:, 0:n]
                        xs = [z[:, k0 + k + kk, t * P:(t + 1) * P] for z in (hi, lo)]
                        ws = [z[:, kk * n:(kk + 1) * n] for z in (wh, wl)]
                        for i, (q, w) in enumerate(((0, 0), (0, 1), (1, 0))):
                            mm = e.matmul(o, xs[q], ws[w], start=(k + kk == 0 and i == 0),
                                          stop=(k + kk == kts - 1 and i == 2))
                    return mm

                def products(e, k=k, m=m, wh=wh, wl=wl):
                    for kk in range(m):
                        a = k0 + k + kk
                        for b in range(n // P):
                            o = pair[b // 2].t[:, (b % 2) * S:(b % 2) * S + S]
                            xs = [z[:, a, :] for z in (hi, lo)]
                            ws = [z[:, kk * n + b * P:kk * n + (b + 1) * P] for z in (wh, wl)]
                            for i, (w, q) in enumerate(((0, 0), (0, 1), (1, 0))):
                                mm = e.matmul(o, ws[w], xs[q], start=(k + kk == 0 and i == 0 and b % 2 == 0),
                                              stop=(k + kk == kts - 1 and i == 2 and (b % 2 == 1 or b == n // P - 1)),
                                              skip_group_check=True)
                    return mm

                acts = [w for a in ready[k0 + k:k0 + k + m] for w in a]
                waits = [*split_done[u], *acts] + (pair[0].free + pair[1].free if k == 0 else [])
                if tokens_out:
                    tile_done[:] = [PE(waits, lambda e, t=t, f=of_tokens: f(e, t)) for t in range(TT)]
                    ticket = tile_done[-1]
                else:
                    ticket = PE(waits, products)
                used_split(u, ticket)
                k += m
                run_due()
                yield
            return pair, ticket

        aux_turn = [0]

        def aux():
            aux_turn[0] += 1
            return banks[4 + aux_turn[0] % 3]

        def transposes(bank, waits, parts):
            def emit(e):
                for o, src in parts:
                    mm = e.transpose(bank.t[0:int(np.prod(src.shape[1:])), o:o + src.shape[0]], src, ident)
                return mm
            return PE([*waits, *bank.free, const_in], emit)

        def split_to(hi, lo, src, waits, scale=1.0):
            a = SE(waits, lambda e: e.activation(hi, src, ACT.Copy, scale=scale))
            b = VE([a, *waits], lambda e: e.scalar_tensor_tensor(lo, src, scale, hi.bitcast(F32), ALU.mult,
                                                                 ALU.subtract))
            return [a, b]

        tmp_turn = [0]

        def scratch():
            tmp_turn[0] += 1
            return tmp[tmp_turn[0] % 2]

        minus_half = stat(2 * NH)
        fill = GP([], lambda e: e.memset(minus_half, -0.5))

        def rsqrt(out, ms, waits):
            n = ms.shape[1]
            a = GP([*waits, fill], lambda e: e.tensor_scalar(ms, ms, EPS, None, ALU.add))
            return GP([a], lambda e: e.tensor_tensor(out, ms, minus_half[:, 0:n], ALU.pow))

        scr_buf = Buf(scr)
        sq_buf = Buf(sb("squares", [P, TT, 512]))
        diag = Buf(sb("diag", [P, TT, P]))
        halves, half_sums = [stat(2 * TT)], []

        def square_half(t, j, waits):
            half_sums.append(SE([*waits, *sq_buf.free], lambda e, m=halves[0]: e.activation(
                sq_buf.t[:, t, :], x[:, t, j * 512:(j + 1) * 512], ACT.Square, scale=D ** -0.5,
                accum_out=m[:, j * TT + t:j * TT + t + 1])))
            sq_buf.free = [half_sums[-1]]

        def norm_factors(ready):
            ms, rs, m = stat(TT), stat(TT), halves[0]
            a = VE([*half_sums], lambda e: e.scalar_tensor_tensor(ms, m[:, 0:TT], EPS, m[:, TT:2 * TT], ALU.add,
                                                                  ALU.add))
            r = GP([a, fill], lambda e: e.tensor_tensor(rs, ms, minus_half[:, 0:TT], ALU.pow))
            dg = [VE([r, const_in, *diag.free], lambda e, t=t: e.tensor_scalar(
                diag.t[:, t, :], ident, rs[:, t:t + 1], None, ALU.mult)) for t in range(TT)]
            halves[0] = stat(2 * TT)
            half_sums.clear()
            return [*dg, *ready]

        def norm(xn, sc, sh=None, sc_ready=()):
            out, rests = [], []
            for k in range(0, KT, 2):
                b = aux()

                def turned(e, b=b, k=k):
                    for kk in (k, k + 1):
                        for t in range(TT):
                            o = (kk - k) * S + t * P
                            mm = e.matmul(b.t[:, o:o + P], x[:, t, kk * P:(kk + 1) * P], diag.t[:, t, :],
                                          start=True, stop=True)
                    return mm

                tr = PE([*xn, *b.free], turned)
                if sh is None:
                    for i, kk in enumerate((k, k + 1)):
                        src, g = b.t[:, i * S:(i + 1) * S], sc[:, kk:kk + 1]
                        hi, lo = h_hi[:, kk, :], h_lo[:, kk, :]
                        a = SE([tr, *sc_ready], lambda e, s=src, g=g, d=hi: e.activation(d, s, ACT.Copy, scale=g))
                        out.append([a])
                        rests.append((out[-1], b, a, lambda e, s=src, g=g, d=lo, hi=hi: e.scalar_tensor_tensor(
                            d, s, g, hi.bitcast(F32), ALU.mult, ALU.subtract)))
                    while rests:
                        tickets, b, a, emit = rests.pop(0)
                        tickets.append(VE([out[-1][0]], emit))
                        b.free = [tickets[-1]]
                else:
                    v = scratch()
                    for i, kk in enumerate((k, k + 1)):
                        src, dst = b.t[:, i * S:(i + 1) * S], v.t[:, i * S:(i + 1) * S]
                        last = VE([tr, *v.free, *sc_ready], lambda e, s=src, d=dst, kk=kk: e.tensor_scalar(
                            d, s, sc[:, kk:kk + 1], sh[:, kk:kk + 1], ALU.mult, ALU.add))
                    b.free = [last]
                    hi, lo = h_hi[:, k:k + 2, :], h_lo[:, k:k + 2, :]
                    vv = v.t[:, :].rearrange("p (k t) -> p k t", k=2)
                    a = SE([last], lambda e, d=hi, s=vv: e.activation(d, s, ACT.Copy))
                    while rests:
                        rests.pop(0)()
                    v.free = [a]
                    out += [v.free, v.free]
                    rests.append(lambda v=v, a=a, hi=hi, lo=lo, vv=vv: v.free.append(VE(
                        [a], lambda e: e.tensor_tensor(lo, vv, hi.bitcast(F32), ALU.subtract))))
            while rests:
                rests.pop(0)()
            diag.free = [tr]
            return out

        def bcast(a, shape):
            return a.to_broadcast(shape)

        rope_tmp = [sb(f"rope_tmp{i}", [P, S]) for i in range(2)]
        rope_free = []

        def rope(v, cs, sn, n, dim, ready):
            half = dim // 2
            a1, a2 = (z[:, 0:n * dim].rearrange("p (h d) -> p h d", d=dim) for z in rope_tmp)
            s = lambda z, a, b: bcast(z[:, a:b].unsqueeze(1), [P, n, b - a])
            w = [*ready, *tables, *rope_free]
            GP(w, lambda e: e.tensor_tensor(a1, v, s(cs, 0, dim), ALU.mult))
            GP(w, lambda e: e.tensor_tensor(a2[:, :, 0:half], v[:, :, half:dim], s(sn, 0, half), ALU.mult))
            k = GP(w, lambda e: e.tensor_tensor(a2[:, :, half:dim], v[:, :, 0:half], s(sn, half, dim), ALU.mult))
            last = GP([k], lambda e: e.tensor_tensor(v, a1, a2, ALU.add))
            rope_free[:] = [last]
            return last

        def head_norm(pair, ready, parts, heads, dim, war=(), then=None, wait=3, copied=False):
            ms, rs = stat(TT * heads), stat(TT * heads)
            tr = []
            by_head = lambda z: z.rearrange("p (h d) -> p h d", d=dim)
            srcs = [by_head(pair[t].t[:, 0:heads * dim]) for t in range(TT)]
            if copied:
                for t in range(TT):
                    a = SE([*ready, *war], lambda e, t=t, s=srcs[t], d=parts[0][3](t): e.activation(d, s, ACT.Copy))
                    pair[t].free, srcs[t], ready = [a], parts[0][3](t), [*ready, a]
            for t in range(TT):
                a = SE([*ready, *sq_buf.free], lambda e, t=t, s=srcs[t]: e.activation(
                    by_head(sq_buf.t[:, t, 0:heads * dim]), s, ACT.Square, scale=dim ** -0.5))
                tr.append(VE([a], lambda e, t=t: e.reduce_sum(
                    ms[:, t * heads:(t + 1) * heads],
                    sq_buf.t[:, t, 0:heads * dim].rearrange("p (h d) -> p h d", d=dim), AX.X)))
            sq_buf.free = tr
            r = rsqrt(rs, ms, tr)
            if not copied:
                pair[0].free = pair[1].free = None

            def rest():
                out = []
                for t in range(TT):
                    muls = []
                    for h0, n, turn, dst in parts:
                        src = srcs[t][:, h0:h0 + n, :]
                        rr = rs[:, t * heads + h0:t * heads + h0 + n].unsqueeze(2)
                        a = VE([r, *ready, *war], lambda e, s=src, rr=rr, d=dst(t), n=n: e.tensor_tensor(
                            d, s, bcast(rr, [P, n, dim]), ALU.mult))
                        muls.append(a)
                        if turn is not None:
                            dn, cs, sn = turn
                            a = rope(dst(t)[:, :, 0:dn], table(cs, t), table(sn, t), n, dn, [a])
                        out.append(a)
                    if not copied:
                        pair[t].free = muls
                if then is not None:
                    later(1 if copied else wait, lambda: then(out))

            later(3 if copied else 1, rest)

        for u in range(2):
            fetch(u)
        pos_in = load(pos[:, :], pos_d, "pos_in")
        rows_in = load(rows[:, :], rows_d.to_broadcast([P, NROWS]), "rows_in")
        for u in range(2, 4):
            fetch(u)
        x_in = load(x[:, :, :], x_d.rearrange("o (t p) d -> p (o t) d", p=P), "x_in")
        for u in range(4, NRAW):
            fetch(u)

        cond_in = SE([cols_in], lambda e: e.activation(cond[:, :], col("c"), ACT.Silu))

        ang, turns, sin_t, cos_t = (sb(n, [P, NANG]) for n in ("ang", "turns", "sin_t", "cos_t"))
        cs1, sn1 = (sb(n, [P, TT + 1, 2, 8]) for n in ("cs1", "sn1"))
        cs2, sn2 = (sb(n, [P, TT, 2, 16]) for n in ("cs2", "sn2"))
        table = lambda z, t: z[:, t, :, :].rearrange("p a f -> p (a f)")
        turn_of = {name: (n, *(sb(f"{name}_{k}", [P, TT, 2, n // 2]) for k in ("cos", "sin")))
                   for name, n in (("nsa_q", ROT), ("nsa_ks", ROT), ("nsa_kw", ROT), ("moba_q", ROT),
                                   ("moba_k", ROT), ("mla_qr", MR))}
        tables = []
        fox_q_gain = stat(1)

        def rotation_tables():
            a = VE([pos_in, const_in], lambda e: e.tensor_copy(ang[:, :], pos[:, :]))
            a = VE([a], lambda e: e.tensor_tensor(ang[:, :], ang[:, :], con("freq"), ALU.mult))
            a = VE([a], lambda e: e.tensor_scalar(turns[:, :], ang[:, :], 1.0 / TWO_PI, None, ALU.mult))
            a = VE([a], lambda e: e.tensor_scalar(turns[:, :], turns[:, :], ROUND, None, ALU.add))
            a = VE([a], lambda e: e.tensor_scalar(turns[:, :], turns[:, :], -ROUND, None, ALU.add))
            for part in PI_PARTS:
                a = VE([a], lambda e, c=part: e.scalar_tensor_tensor(ang[:, :], turns[:, :], -c, ang[:, :], ALU.mult,
                                                                     ALU.add))
            b = VE([a], lambda e: e.tensor_scalar(cos_t[:, :], ang[:, :], TWO_PI / 4, None, ALU.add))
            c = VE([b], lambda e: e.tensor_scalar(turns[:, :], cos_t[:, :], TWO_PI / 2, -TWO_PI, ALU.is_gt, ALU.mult))
            c = VE([c], lambda e: e.tensor_tensor(cos_t[:, :], cos_t[:, :], turns[:, :], ALU.add))
            c = VE([c], lambda e: e.tensor_scalar(cos_t[:, :], cos_t[:, :], PI_LOW, -PI_LOW, ALU.min, ALU.max))
            a = VE([a], lambda e: e.tensor_scalar(ang[:, :], ang[:, :], PI_LOW, -PI_LOW, ALU.min, ALU.max))
            sin_in = SE([a, c], lambda e: e.activation(sin_t[:, :], ang[:, :], ACT.Sin))
            cos_in = SE([c], lambda e: e.activation(cos_t[:, :], cos_t[:, :], ACT.Sin))
            for cs, sn, n, w, lo in ((cs1, sn1, TT + 1, 8, 0), (cs2, sn2, TT, 16, (TT + 1) * 8)):
                ca = cos_t[:, lo:lo + n * w].rearrange("p (t f) -> p t f", f=w)
                sa = sin_t[:, lo:lo + n * w].rearrange("p (t f) -> p t f", f=w)
                for i in range(2):
                    a = VE([cos_in], lambda e, d=cs[:, :, i, :], s=ca: e.tensor_copy(d, s))
                    a = VE([sin_in], lambda e, d=sn[:, :, i, :], s=sa, i=i: e.tensor_scalar(
                        d, s, 2.0 * i - 1.0, None, ALU.mult))
            for name, (n, cos_g, sin_g) in turn_of.items():
                cs, sn = (cs2, sn2) if n == MR else (cs1, sn1)
                for i in range(2):
                    for src, dst, j in ((cs, cos_g, i), (sn, sin_g, 1 - i)):
                        g = row(name)[:, j * (n // 2):(j + 1) * (n // 2)].unsqueeze(1)
                        t = VE([a, rows_in], lambda e, s=src, d=dst, i=i, g=g, n=n: e.tensor_tensor(
                            d[:, :, i, :], s[:, 0:TT, i, :], bcast(g, [P, TT, n // 2]), ALU.mult))
            tables.append(t)
            tables.append(VE([cols_in, const_in], lambda e: e.tensor_tensor(fox_q_gain, col("fox_q"),
                                                                            con("fox_scale"), ALU.mult)))

        ada_acc = [Buf(sb(f"ada_acc{i}", [P, 512])) for i in range(2)]
        ada_done, gate_ready, gate_free = {}, [], []
        ones = con("ones")

        def adaptive(i, chunks, engine):
            pending = []

            def finish(n, b, a):
                bank = acc_pair()[0]
                if n < 4:
                    def columns(e):
                        for j in range(4):
                            mm = e.matmul(bank.t[:, j:j + 1], b.t[:, j * P:(j + 1) * P], ones[:, 0:1],
                                          start=True, stop=True)
                        return mm

                    t = PE([a, const_in, *bank.free], columns)
                    bias = col(f"ada{i}")
                    c = VE([t, cols_in], lambda e: e.tensor_tensor(
                        ada[:, i, 4 * n:4 * n + 4], bank.t[:, 0:4], bias[:, 4 * n:4 * n + 4], ALU.add))
                    if n == 3:
                        ada_done[i] = VE([c], lambda e: e.scalar_tensor_tensor(
                            ada[:, i, KT:2 * KT], ada[:, i, KT:2 * KT], 1.0, col(f"norm{i}"), ALU.add, ALU.mult))
                else:
                    t = PE([a, const_in, *bank.free], lambda e: e.matmul(
                        bank.t[:, :], ones, b.t[:, :], start=True, stop=True))
                    j = n - 4
                    c = VE([t, bias_in[i], *gate_free], lambda e: e.tensor_tensor(
                        gate_row[:, j * 512:(j + 1) * 512], bank.t[:, :], gate_bias[:, j * 512:(j + 1) * 512],
                        ALU.add))
                    gate_ready.append(c)
                bank.free = [c]
                b.free = [t]

            for n in chunks:
                b, k, a = ada_acc[n % 2], 0, None
                while k < KT:
                    u = take(f"ada{i}_{n}")
                    m, w = units[u][2], raw[u % NRAW].t
                    waits = [fetched[u], cond_in, *b.free]
                    for kk in range(m):
                        src, cc, first = w[:, kk * 512:(kk + 1) * 512], cond[:, k + kk:k + kk + 1], k + kk == 0
                        if engine(n) is GP:
                            c = SE(waits, lambda e, d=b.t[:, :] if first else src, s=src, c=cc: e.activation(
                                d, s, ACT.Copy, scale=c))
                            a = c if first else GP([c, a], lambda e, b=b, s=src: e.tensor_tensor(
                                b.t[:, :], b.t[:, :], s, ALU.add))
                        elif first:
                            a = VE(waits, lambda e, b=b, s=src, c=cc: e.tensor_scalar(b.t[:, :], s, c, None, ALU.mult))
                        else:
                            a = VE([*waits, a], lambda e, b=b, s=src, c=cc: e.scalar_tensor_tensor(
                                b.t[:, :], s, c, b.t[:, :], ALU.mult, ALU.add))
                    used_raw(u, a)
                    k += m
                    if k >= KT - KT // 4 and pending:
                        finish(*pending.pop())
                    yield
                pending.append((n, b, a))
            for _ in range(2):
                yield
            finish(*pending.pop())

        def attention(items, pt, sm, background, per_slot, tail, tail_steps, hooks={}):
            state, closing = {}, []

            def scores(i):
                it, bank = items[i], banks[4 + i % 2]

                def emit(e):
                    e.matmul(bank.t[:, 0:P], it["q"](0), it["k"](P), start=True, stop=True)
                    return e.matmul(bank.t[:, P:3 * P], it["q"](1), it["k"](S), start=True, stop=True)

                state[i] = PE([*it["ready"], *bank.free], emit)

            def weights(i):
                it, bank, m, t = items[i], banks[4 + i % 2], sm[i % len(sm)], state[i]
                mx, ng, su, rc = (stat(TT) for _ in range(4))
                mask = con("causal")
                a = VE([t, *m.free], lambda e: e.tensor_tensor_reduce(
                    m.t[:, 0:P], bank.t[:, 0:P], mask[:, P:S], 1.0, -3e38, ALU.add, ALU.max, mx[:, 0:1]))
                b = VE([t, *m.free], lambda e: e.tensor_tensor_reduce(
                    m.t[:, P:3 * P], bank.t[:, P:3 * P], mask, 1.0, -3e38, ALU.add, ALU.max, mx[:, 1:2]))
                bank.free = [b]
                yield
                c = VE([a, b], lambda e: e.tensor_scalar(ng, mx, -it["scale"], None, ALU.mult))
                d = SE([c], lambda e: e.activation(m.t[:, 0:P], m.t[:, 0:P], ACT.Exp, bias=ng[:, 0:1],
                                                   scale=it["scale"], accum_out=su[:, 0:1]))
                d = SE([c], lambda e: e.activation(m.t[:, P:3 * P], m.t[:, P:3 * P], ACT.Exp, bias=ng[:, 1:2],
                                                   scale=it["scale"], accum_out=su[:, 1:2]))
                state[i] = [m, su, rc, d]

            def divide(i):
                it = items[i]
                m, su, rc, d = state[i]
                a = VE([d], lambda e: e.reciprocal(rc, su))
                yield
                if it["gate"] is not None:
                    a = VE([a, *it["gate_ready"]], lambda e: e.tensor_tensor(rc, rc, it["gate"], ALU.mult))
                b = VE([a], lambda e: e.tensor_scalar(m.t[:, 0:P], m.t[:, 0:P], rc[:, 0:1], None, ALU.mult))
                b = VE([a], lambda e: e.tensor_scalar(m.t[:, P:3 * P], m.t[:, P:3 * P], rc[:, 1:2], None, ALU.mult))
                state[i].append(b)

            def turn_over(i):
                m, p, bank = state[i][0], pt[i % len(pt)], banks[6]
                t = transposes(bank, [state[i][-1]], [(0, m.t[:, 0:P]), (P, m.t[:, P:2 * P]),
                                                      (2 * P, m.t[:, 2 * P:3 * P])])
                m.free = [t]
                a = SE([t, *p.free], lambda e: e.activation(p.t[:, :], bank.t[:, 0:3 * P], ACT.Copy))
                bank.free = [a]
                state[i] = [p, a]

            def values(i):
                it = items[i]
                p, a = state.pop(i)
                o = it["out"]

                def emit(e):
                    if it["before"]:
                        it["before"](e)
                    e.matmul(o, it["v"](0), p.t[:, 0:S], start=it["first"] and not it["before"], stop=False,
                             skip_group_check=True)
                    return e.matmul(o[:, P:S], it["v"](1), p.t[:, S:S + P], start=False, stop=it["last"],
                                    skip_group_check=True)

                t = PE([a, *it["v_ready"], *(it["o_buf"].free if it["first"] else [])], emit)
                p.free = [t]
                if it["close"]:
                    closing.append(lambda: it["close"](t))

            n = len(items)
            for i in range(n + 5):
                if i in hooks:
                    hooks[i]()
                if i < n:
                    scores(i)
                ends = [end() for end in closing]
                closing.clear()
                if 0 <= i - 4 < n:
                    turn_over(i - 4)
                steps = [f(j) for f, j in ((weights, i - 1), (divide, i - 2)) if 0 <= j < n]
                for _ in range(2):
                    for step in steps:
                        next(step, None)
                for end in ends:
                    end()
                for _ in range(per_slot):
                    next(background, None)
                if 0 <= i - 5 < n:
                    values(i - 5)
                if i >= n and tail_steps > 0:
                    drain_steps(background)
                    next(tail)
                    tail_steps -= 1
            for end in closing:
                end()()

        def gqa_item(q_t, k_t, pr, half, v, ready, v_ready, o_buf, out, **more):
            hs = slice(half * HD, (half + 1) * HD)
            return dict(q=lambda t: q_t[hs, pr, t * P:(t + 1) * P], k=lambda n: k_t[hs, 0:n], v=v, ready=ready,
                        v_ready=v_ready, scale=HD ** -0.5, o_buf=o_buf, out=out, **more)

        def residual(names, lhs, ready, scale, x_ready, squares=True):
            last = []
            for j, name in enumerate(names):
                pair, _ = yield from linear(name, lhs, ready, True)
                for tt in range(TT):
                    o, t = x[:, tt, j * 512:(j + 1) * 512], tile_done[tt]
                    if scale is None:
                        v = scratch()
                        a = VE([t, *gate_ready, *v.free], lambda e, v=v, tt=tt, j=j, pair=pair: e.tensor_tensor(
                            v.t[:, :], pair[tt].t[:, :], gate_row[:, j * 512:(j + 1) * 512], ALU.mult))
                        b = VE([a, *x_ready], lambda e, v=v, o=o: e.tensor_tensor(o, o, v.t[:, :], ALU.add))
                        v.free = [b]
                        pair[tt].free = [a]
                    else:
                        b = VE([t, *x_ready], lambda e, o=o, tt=tt, pair=pair: e.scalar_tensor_tensor(
                            o, pair[tt].t[:, :], scale, o, ALU.mult, ALU.add))
                        pair[tt].free = [b]
                    last.append(b)
                    if squares:
                        square_half(tt, j, [b])
            return last

        mix = ExitStack()
        tokq = sb("tokq", [P, TT, 1024], on=mix)
        tokk = sb("tokk", [P, TT, 512], on=mix)
        tokv = sb("tokv", [P, TT, 512], on=mix)
        q_t = sb("q_t", [P, NP, S], on=mix)
        k_t = sb("k_t", [P, 4, S], on=mix)
        zs = sb("zs", [P, 16, S], on=mix)
        o_hi, o_lo = (sb(n, [P, KT, S], F32R, on=mix) for n in ("o_hi", "o_lo"))
        soft = [Buf(sb(f"soft{i}", [P, 3 * P], on=mix)) for i in range(4)]
        prob_t = [Buf(sb(f"prob_t{i}", [P, 3 * P], on=mix)) for i in range(2)]
        gate_row = sb("gate_row", [P, D], on=mix)
        gate_bias = sb("gate_bias", [P, D], on=mix)
        gates = sb("gates", [P, TT, 3 * NH], on=mix)
        hid = sb("hid", [P, 2, 2, NKV, CPAD], on=mix)
        kc2 = sb("kc2", [P, 2, HD], on=mix)
        kc_two = sb("kc_two", [P, 2, 2 * CPAD], on=mix)
        vc = sb("vc", [P, NKV, HD], on=mix)
        pc_t = zs[:, 8:8 + NKV, :]
        bias_in = {0: load(gate_bias[:, :], gate_bias_d[0:1, :].to_broadcast([P, D]), "gate_bias0_in")}

        def q_heads(names, gain, ready, out, first=0):
            for j, name in enumerate(names, first):
                pair, t = yield from linear(name, (h_hi, h_lo), ready, True)
                view = lambda tt, j=j: tokq[:, tt, j * 512:(j + 1) * 512].rearrange("p (h d) -> p h d", d=HD)

                def then(done, j=j):
                    for p2 in range(2):
                        b = aux()
                        tr = transposes(b, done, [((pp * TT + tt) * P, tokq[:, tt, (j * 4 + 2 * p2 + pp) * P:
                                                                           (j * 4 + 2 * p2 + pp + 1) * P])
                                                  for pp in range(2) for tt in range(TT)])
                        c = SE([tr, cols_in], lambda e, b=b, k=j * 4 + 2 * p2: e.activation(
                            q_t[:, k:k + 2, :].rearrange("p k t -> p (k t)"), b.t[:, :], ACT.Copy, scale=col(gain)))
                        b.free = [c]
                        out.append(c)

                head_norm(pair, [t], [(0, 8, turn_of[gain], view)], 8, HD, (), then)

        def z_gate(names, ready, first=0):
            if first == 0:
                zs_ready.clear()
            for j, name in enumerate(names, first):
                pair, t = yield from linear(name, (h_hi, h_lo), ready, False)
                for i in range(2):
                    v = scratch()
                    a = SE([t, *v.free], lambda e, v=v, i=i, pair=pair: e.activation(v.t[:, :], pair[i].t[:, :],
                                                                                     ACT.Tanh, scale=0.5))
                    k = j * 4 + 2 * i
                    b = VE([a], lambda e, v=v, i=i, k=k, pair=pair: e.scalar_tensor_tensor(
                        zs[:, k:k + 2, :].rearrange("p k t -> p (k t)"), v.t[:, :], 1.0, pair[i].t[:, :], ALU.add,
                        ALU.mult))
                    v.free = [b]
                    pair[i].free = [b]
                    zs_ready.append(b)

        zs_ready = []
        o_acc = Buf(banks[7].t[:, 0:S])

        def close_gated(pr, ob):
            def close(t):
                v = gated[pr % 2]
                a = VE([t, *zs_ready, *v.free], lambda e, v=v: e.scalar_tensor_tensor(
                    v.t[:, 0:S], ob.t, 0.5, zs[:, pr, :], ALU.mult, ALU.mult))
                ob.free = [a]
                b = SE([a], lambda e: e.activation(o_hi[:, pr, :], v.t[:, 0:S], ACT.Copy))

                def rest():
                    c = VE([b], lambda e: e.tensor_tensor(o_lo[:, pr, :], v.t[:, 0:S], o_hi[:, pr, :].bitcast(F32),
                                                          ALU.subtract))
                    o_ready[pr] = v.free = [b, c]
                return rest
            return close

        gated = [Buf(sb(f"gated{i}", [P, S], on=mix)) for i in range(2)]
        o_ready = {}
        kv = lambda tt, c0, n: tokk[:, tt, c0:c0 + n * HD].rearrange("p (h d) -> p h d", d=HD)

        def k_pairs(gains, done, out):
            branches = len(gains)
            for br in range(branches):
                b = aux()
                tr = transposes(b, done, [((g2 * TT + tt) * P, tokk[:, tt, br * S + g2 * P:br * S + (g2 + 1) * P])
                                          for g2 in range(2) for tt in range(TT)])
                for g2 in range(2):
                    c = SE([tr, cols_in], lambda e, b=b, g2=g2, br=br: e.activation(
                        k_t[:, g2 * branches + br, :], b.t[:, g2 * S:(g2 + 1) * S], ACT.Copy, scale=col(gains[br])))
                b.free = [c]
                out.append(c)

        sums = adaptive(0, range(4), lambda n: VE if n % 2 else GP)
        for _ in range(KT * 512 // UNIT):
            next(sums)
        rotation_tables()
        for t in range(TT):
            for j in range(2):
                square_half(t, j, [x_in])
        xn = norm_factors([x_in])
        drain_steps(sums)
        h0 = norm(xn, ada[:, 0, KT:2 * KT], ada[:, 0, 0:KT], [ada_done[0]])

        by_parity = scr[:, :, :].rearrange("p t (g l d) -> p t g l d", g=8, l=2)
        NB = NKV * NCMP
        flat = [zs[:, 8 + 4 * i:12 + 4 * i, :].rearrange("p k t -> p (k t)")[:, 0:CJ * NB]
                .rearrange("p (j n) -> p j n", j=CJ) for i in range(2)]
        flat_ready = []

        def kcvc():
            pair, t = yield from linear("nsa_kcvc", (h_hi, h_lo), h0, True)
            bp = []
            for tt in range(TT):
                for lo in range(2):
                    src = pair[tt].t[:, :].rearrange("p (g d) -> p g d", d=HD)
                    par = con("parity")[:, lo:lo + 1]
                    if lo == 0:
                        e_ = VE([t, *scr_buf.free], lambda e, tt=tt, s=src, par=par: e.tensor_scalar(
                            by_parity[:, tt, :, 0, :], s, par, None, ALU.mult))
                    else:
                        e_ = SE([t, *scr_buf.free, e_], lambda e, tt=tt, s=src, par=par: e.activation(
                            by_parity[:, tt, :, 1, :], s, ACT.Copy, scale=par))
                    bp.append(e_)
            pair[0].free = pair[1].free = list(bp)

            def pair_tokens():
                for i in range(2):
                    b = aux()

                    def emit(e, i=i, b=b):
                        for g in range(NKV):
                            for tt in range(TT):
                                mm = e.matmul(b.t[:, g * P + tt * 64:g * P + (tt + 1) * 64],
                                              by_parity[:, tt, i * NKV + g, :, :].rearrange("p l d -> p (l d)"),
                                              con("pair"), start=True, stop=True)
                        return mm

                    t = PE([*bp, const_in, *b.free], emit)
                    window = bass.AP(b.t[:, :].tensor, b.t[:, :].offset,
                                     [list(b.t[:, :].ap[0]), [1, CJ], [P, NKV], [CMP_STRIDE // 2, NCMP]])
                    pe = col(f"pe{i}").unsqueeze(2).unsqueeze(3)
                    a = VE([t, cols_in], lambda e, i=i, w=window, pe=pe: e.tensor_tensor(
                        flat[i].rearrange("p j (g n) -> p j g n", g=NKV), w,
                        bcast(pe, [P, CJ, NKV, NCMP]), ALU.add))
                    b.free = [a]
                    scr_buf.free = [t]
                    flat_ready.append(a)

            later(2, pair_tokens)

        zeros = [GP([], lambda e, z=z: e.memset(z, 0.0)) for z in
                 (hid[:, :, :, :, :], kc_two[:, :, :], vc[:, :, :])]

        def compress_up(i):
            bank = acc_pair()[0]
            k = 0
            while k < CJ:
                u = take(f"cmp_w1_{i}")
                m = units[u][2]

                def products(e, k=k, m=m, w=raw[u % NRAW].t):
                    for kk in range(m):
                        for j in range(2):
                            mm = e.matmul(bank.t[:, j * P:j * P + NB], w[:, kk * 256 + j * P:kk * 256 + (j + 1) * P],
                                          flat[i][:, k + kk, :], start=(k + kk == 0 and j == 0),
                                          stop=(k + kk == CJ - 1 and j == 1), skip_group_check=True)
                    return mm

                t = PE([fetched[u], flat_ready[i], *(bank.free if k == 0 else [])], products)
                used_raw(u, t)
                k += m
                run_due()
            return bank, t

        cmp_out = {}

        def compress_down(i, up):
            bank, t = up
            b1 = col(f"b1_{i}")
            ev = [SE([t, *zeros, cols_in], lambda e, j=j: e.activation(
                hid[:, i, j, :, 0:NCMP], bank.t[:, j * P:j * P + NB].rearrange("p (g n) -> p g n", g=NKV),
                ACT.Gelu_apprx_tanh, bias=b1[:, j:j + 1])) for j in range(2)]
            bank.free = ev
            yield
            b2 = aux()
            w2 = col(f"w2_{i}")

            def emit(e):
                for j in range(2):
                    mm = e.matmul(b2.t[:, 0:HD], hid[:, i, j, :, :].rearrange("p g n -> p (g n)"),
                                  w2[:, j * HD:(j + 1) * HD], start=(j == 0), stop=(j == 1))
                return mm

            t = PE([*ev, *b2.free], emit)
            if i == 1:
                for g in range(NKV):
                    gs = slice(g * CPAD, (g + 1) * CPAD)
                    a = SE([t, *zeros], lambda e, g=g, gs=gs: e.activation(vc[gs, g, :], b2.t[gs, 0:HD], ACT.Copy))
                b2.free = [a]
                cmp_out["v"] = a
                return
            ms, rs = stat(1), stat(1)
            a = SE([t], lambda e: e.activation(kc2[:, 0, :], b2.t[:, 0:HD], ACT.Square, scale=HD ** -0.5,
                                               accum_out=ms))
            r = rsqrt(rs, ms, [a])
            a = VE([r, rows_in], lambda e: e.scalar_tensor_tensor(
                kc2[:, 0, :], b2.t[:, 0:HD], rs, row("nsa_kc"), ALU.mult, ALU.mult))
            b2.free = [a]
            a = rope(kc2[:, 0:1, 0:16], table(cs1, TT), table(sn1, TT), 1, 16, [a])
            a = GP([a], lambda e: e.tensor_copy(kc2[:, 1, :], kc2[:, 0, :]))
            yield
            b3 = aux()
            t = transposes(b3, [a], [(0, kc2[:, :, :].rearrange("p a d -> p (a d)"))])
            for g in range(NKV):
                hs, half = slice((g % 2) * HD, (g % 2 + 1) * HD), g % 2
                a = SE([t, *zeros], lambda e, g=g, hs=hs, half=half: e.activation(
                    kc_two[hs, g // 2, half * CPAD:(half + 1) * CPAD], b3.t[hs, g * CPAD:(g + 1) * CPAD], ACT.Copy))
            b3.free = [a]
            cmp_out["k"] = a

        drain_steps(kcvc())
        q_ready, k_ready = [], []
        pair, t = drain_steps(linear("nsa_kskw", (h_hi, h_lo), h0, True))
        head_norm(pair, [t], [(0, 4, turn_of["nsa_ks"], lambda tt: kv(tt, 0, 4)),
                              (4, 4, turn_of["nsa_kw"], lambda tt: kv(tt, S, 4))], 8, HD, (),
                  lambda done: k_pairs(["nsa_ks", "nsa_kw"], done, k_ready), 4)

        def with_side(gen, side):
            while True:
                try:
                    next(gen)
                except StopIteration:
                    return
                next(side, None)

        drain_steps(q_heads(["nsa_q0"], "nsa_q", h0, q_ready))
        up = compress_up(0)
        with_side(q_heads(["nsa_q1"], "nsa_q", h0, q_ready, 1), compress_down(0, up))
        up = compress_up(1)

        gates_ready = []
        pair, t = drain_steps(linear("nsa_gate", (h_hi, h_lo), h0, False))
        gt = scratch()
        a = VE([t, cols_in, *gt.free], lambda e, pair=pair: e.tensor_scalar(
            gt.t[:, 0:S], pair[0].t[:, 0:S], col("gate_b"), None, ALU.add))
        pair[0].free = [a]
        gate_tanh = SE([a], lambda e: e.activation(gt.t[:, 0:S], gt.t[:, 0:S], ACT.Tanh, scale=0.5))

        def gates_turned():
            b = aux()
            t = transposes(b, [gate_tanh], [(tt * P, gt.t[:, tt * P:(tt + 1) * P]) for tt in range(TT)])
            gt.free = [t]
            c = VE([t], lambda e: e.tensor_scalar(
                gates[:, :, :], b.t[:, 0:S].rearrange("p (t c) -> p t c", t=TT)[:, :, 0:3 * NH], 1.0, 0.5,
                ALU.add, ALU.mult))
            b.free = [c]
            gates_ready.append(c)

        v_ready = []

        def nsa_values():
            pair, t = yield from linear("nsa_vsvw", (h_hi, h_lo), h0, True)
            for tt in range(TT):
                a = SE([t], lambda e, tt=tt: e.activation(tokv[:, tt, :], pair[tt].t[:, :], ACT.Copy))
                pair[tt].free = [a]
                v_ready.append(a)

        def cmp_attention(tt):
            b = banks[4 + tt]
            s_ = scr[:, tt, 0:512]
            sv = s_.rearrange("p (h n) -> p h n", n=CPAD)
            hb = lambda z: bcast(z.unsqueeze(2), [P, NH, CPAD])

            def emit(e):
                for pr in range(NP):
                    mm = e.matmul(b.t[:, pr * 2 * CPAD:(pr + 1) * 2 * CPAD], q_t[:, pr, tt * P:(tt + 1) * P],
                                  kc_two[:, pr // 4, :], start=True, stop=True)
                return mm

            t = PE([*q_ready, cmp_out["k"], *b.free], emit)
            mx, su = stat(NH), stat(NH)
            mask = con("cmp_mask")[:, tt * CPAD:(tt + 1) * CPAD].unsqueeze(1)
            a = VE([t, *scr_buf.free], lambda e: e.tensor_tensor(
                sv, b.t[:, :].rearrange("p (h n) -> p h n", n=CPAD), bcast(mask, [P, NH, CPAD]), ALU.add))
            b.free = [a]
            c = VE([a], lambda e: e.reduce_max(mx, sv, AX.X))
            c = VE([c], lambda e: e.tensor_scalar(mx, mx, FLOOR, None, ALU.max))
            c = VE([c], lambda e: e.tensor_tensor(sv, sv, hb(mx), ALU.subtract))
            d = SE([c], lambda e: e.activation(s_, s_, ACT.Exp, scale=HD ** -0.5))
            yield
            c = VE([d], lambda e: e.reduce_sum(su, sv, AX.X))
            c = VE([c], lambda e: e.tensor_scalar(su, su, 1e-30, None, ALU.max))
            c = VE([c], lambda e: e.reciprocal(su, su))
            c = VE([c, *gates_ready], lambda e: e.tensor_tensor(su, su, gates[:, tt, 0:NH], ALU.mult))
            dst = scr[:, tt, 512:1024].rearrange("p (r g a n) -> p g r a n", r=4, g=2, a=2)
            for gp in range(2):
                c2 = VE([c], lambda e, gp=gp: e.tensor_tensor(
                    dst[:, gp, :, :, :], s_[:, gp * S:(gp + 1) * S].rearrange("p (r a n) -> p r a n", r=4, a=2),
                    bcast(su[:, gp * 8:gp * 8 + 8].rearrange("p (r a) -> p r a", a=2).unsqueeze(3), [P, 4, 2, CPAD]),
                    ALU.mult))
            c = c2
            yield
            b6 = banks[6]
            t = transposes(b6, [c], [(r * P, scr[:, tt, 512 + r * P:512 + (r + 1) * P]) for r in range(4)])
            a = SE([t], lambda e: e.activation(pc_t[:, :, tt * P:(tt + 1) * P],
                                               b6.t[:, :].rearrange("p (r t) -> p r t", r=4), ACT.Copy))
            b6.free = [a]
            cmp_ready.append(a)
            cmp_last[:] = [t]

        cmp_ready, cmp_last = [], []

        def compression():
            yield from compress_down(1, up)
            yield
            for tt in range(TT):
                yield from cmp_attention(tt)
                yield

        side = compression()

        next(side)
        later(1, gates_turned)
        with_side(nsa_values(), side)
        with_side(z_gate(["nsa_z0"], h0), side)
        for _ in side:
            pass
        run_all()
        scr_buf.free = list(cmp_last)

        def gqa_item(pr, half, k, v, v_ready, **more):
            hs = slice(half * HD, (half + 1) * HD)
            return dict(q=lambda t: q_t[hs, pr, t * P:(t + 1) * P], k=lambda n: k_t[hs, k, 0:n], v=v,
                        ready=[*q_ready, *k_ready], v_ready=v_ready, scale=HD ** -0.5, o_buf=o_acc,
                        out=o_acc.t[hs, :], **more)

        items = []
        for pr in range(NP):
            for half in range(2):
                g, r = 2 * (pr // 4) + half, pr % 4

                def before(e, g=g, r=r, half=half):
                    e.matmul(o_acc.t[half * HD:(half + 1) * HD, :], vc[:, g, :], pc_t[:, r, :], start=True, stop=False,
                             skip_group_check=True)

                for br in range(2):
                    c = (br + 1) * NH + 2 * pr + half
                    items.append(gqa_item(
                        pr, half, (pr // 4) * 2 + br,
                        lambda j, br=br, g=g: tokv[:, j, br * S + g * HD:br * S + (g + 1) * HD],
                        [*v_ready, *cmp_ready, cmp_out["v"]],
                        gate=gates[:, :, c:c + 1].rearrange("p t o -> p (t o)"), gate_ready=gates_ready,
                        first=br == 0, last=br == 1, before=before if br == 0 else None,
                        close=close_gated(pr, o_acc) if br == 1 and half == 1 else None))

        def nsa_background():
            z = z_gate(["nsa_z1"], h0, 1)
            sums = chain(adaptive(0, range(4, 6), lambda n: GP), adaptive(1, range(4), lambda n: GP))
            for _ in sums:
                next(z, None)
                yield

        out_steps = residual(["nsa_out0", "nsa_out1"], (o_hi, o_lo), TilesReady(o_ready), None, [x_in])
        attention(items, prob_t, soft, nsa_background(), 1, out_steps, 3)
        x0 = drain_steps(out_steps)
        gate_free[:] = x0
        bias_in[1] = load(gate_bias[:, :], gate_bias_d[1:2, :].to_broadcast([P, D]), "gate_bias1_in", gate_ready)
        gate_ready.clear()

        h1 = norm(norm_factors(x0), ada[:, 1, KT:2 * KT], ada[:, 1, 0:KT], [ada_done[1]])
        q_ready, k_ready = [], []
        drain_steps(q_heads(["moba_q0", "moba_q1"], "moba_q", h1, q_ready))
        pair, t = drain_steps(linear("moba_kv", (h_hi, h_lo), h1, True))
        v_ready = [SE([t], lambda e, tt=tt, pair=pair: e.activation(tokv[:, tt, 0:S], pair[tt].t[:, S:2 * S], ACT.Copy))
                   for tt in range(TT)]
        head_norm(pair, v_ready, [(0, 4, turn_of["moba_k"], lambda tt: kv(tt, 0, 4))], 4, HD, (),
                  lambda done: k_pairs(["moba_k"], done, k_ready))
        zg = z_gate(["moba_z0", "moba_z1"], h1)
        for _ in range(Z_FIRST):
            next(zg)
        run_all()
        items = []
        for pr in range(NP):
            for half in range(2):
                g = 2 * (pr // 4) + half
                items.append(gqa_item(
                    pr, half, pr // 4, lambda j, g=g: tokv[:, j, g * HD:(g + 1) * HD], v_ready, gate=None, first=True,
                    last=True, before=None, close=close_gated(pr, o_acc) if half == 1 else None))

        def moba_background():
            for _ in adaptive(1, range(4, 6), lambda n: GP):
                next(zg, None)
                yield

        o_ready.clear()
        out_steps = residual(["moba_out0", "moba_out1"], (o_hi, o_lo), TilesReady(o_ready), None, x0)
        attention(items, prob_t, soft, moba_background(), 1, out_steps, 3)
        x1 = drain_steps(out_steps)
        mix.close()

        def ffn(i, ready):
            with ExitStack() as own:
                a_hi, a_lo = (sb(f"a{i}_{n}", [P, FT, S], F32R, on=own) for n in ("hi", "lo"))
                act = [Buf(sb(f"act{i}_{n}", [P, TT, S], on=own)) for n in range(2)]
                hr = norm(norm_factors(ready), col(f"ffn{i}"), None, [cols_in])
                a_ready = {}
                for n in range(FT // 2):
                    pair, t = drain_steps(linear(f"ffn{i}_up{n}", (h_hi, h_lo), hr, True))
                    v = act[n % 2]
                    done = []
                    for tt in range(TT):
                        a = SE([t, *v.free], lambda e, v=v, tt=tt, pair=pair: e.activation(
                            v.t[:, tt, :], pair[tt].t[:, 0:S], ACT.Silu))
                        b = VE([a], lambda e, v=v, tt=tt, pair=pair: e.tensor_tensor(
                            v.t[:, tt, :], v.t[:, tt, :], pair[tt].t[:, S:2 * S], ALU.mult))
                        pair[tt].free = [b]
                        done.append(b)

                    def turn_over(n=n, v=v, done=done):
                        b = aux()
                        t = transposes(b, done, [((k * TT + tt) * P, v.t[:, tt, k * P:(k + 1) * P])
                                                 for k in range(2) for tt in range(TT)])
                        v.free = [t]
                        s2 = split_to(a_hi[:, 2 * n:2 * n + 2, :], a_lo[:, 2 * n:2 * n + 2, :],
                                      b.t[:, :].rearrange("p (k t) -> p k t", k=2), [t])
                        b.free = s2
                        a_ready[2 * n] = a_ready[2 * n + 1] = s2

                    later(1, turn_over)
                down = residual([f"ffn{i}_down0", f"ffn{i}_down1"], (a_hi, a_lo), TilesReady(a_ready), 0.5, ready,
                                i != 2)
                return drain_steps(down)

        x2 = ffn(1, x1)

        mix = ExitStack()
        tokq = sb("tok2_q", [P, TT, MH * MQ], on=mix)
        tokk = sb("tok2_k", [P, TT, MH * MQ], on=mix)
        tokv2 = sb("tok2_v", [P, TT, 1024], on=mix)
        q2_t = sb("q2_t", [P, 8, S], on=mix)
        k2_t = sb("k2_t", [P, 8, S], on=mix)
        gate2 = sb("gate2", [P, 16, S], on=mix)
        o2_hi, o2_lo = (sb(n, [P, KT, S], F32R, on=mix) for n in ("o2_hi", "o2_lo"))
        soft2 = [Buf(sb(f"soft2_{i}", [P, 3 * P], on=mix)) for i in range(4)]
        prob2_t = [Buf(sb(f"prob2_t{i}", [P, 3 * P], on=mix)) for i in range(2)]
        l_hi, l_lo = (sb(n, [P, 3, S], F32R, on=mix) for n in ("l_hi", "l_lo"))
        decay = sb("decay", [P, 3, TT, FH], on=mix)
        half_b = sb("half_b", [P, 2 * KT], on=mix)
        lat = scr[:, :, 0:LAT]
        lz = [GP([*x2], lambda e, z=z: e.memset(z[:, 1, :].bitcast(F32), 0.0)) for z in (l_hi, l_lo)]
        hb_ready = VE([cols_in, *x2], lambda e: e.tensor_scalar(
            half_b[:, :], cols[:, COLS["gate_mla"][0]:COLS["gate_fox"][1]], 0.5, None, ALU.mult))

        h2 = norm(norm_factors(x2), col("mix"), None, [cols_in])
        pair, t = drain_steps(linear("mix_lat", (h_hi, h_lo), h2, True))
        lat_in = [SE([t, *scr_buf.free], lambda e, tt=tt, pair=pair: e.activation(lat[:, tt, :], pair[tt].t[:, 0:LAT],
                                                                                  ACT.Copy)) for tt in range(TT)]
        for tt in range(TT):
            pair[tt].free = [lat_in[tt]]
        parts = ((0, QL), (QL, KVL), (QL + KVL, MR))
        ms, rs = stat(TT * 3), stat(TT * 3)
        sq = []
        for tt in range(TT):
            for j, (c0, n) in enumerate(parts):
                sq.append(SE([lat_in[tt], *sq_buf.free], lambda e, tt=tt, j=j, c0=c0, n=n, ms=ms: e.activation(
                    sq_buf.t[:, tt, c0:c0 + n], lat[:, tt, c0:c0 + n], ACT.Square, scale=n ** -0.5,
                    accum_out=ms[:, tt * 3 + j:tt * 3 + j + 1])))
        lat_r = rsqrt(rs, ms, sq)
        sq_buf.free = sq
        lat_rs = rs
        l_ready = {}
        kr = []

        fl = []

        def forget_gates():
            f, s1 = decay[:, 0, :, :], decay[:, 1, :, :]
            a = VE([*lat_in, rows_in], lambda e: e.tensor_tensor(
                f, lat[:, :, LAT - FH:LAT], bcast(row("fox_bf").unsqueeze(1), [P, TT, FH]), ALU.add))
            b = VE([a], lambda e: e.tensor_scalar(s1, f, -1.0, None, ALU.mult))
            b = VE([b], lambda e: e.tensor_tensor(s1, s1, f, ALU.min))
            c = SE([b], lambda e: e.activation(s1, s1, ACT.Exp))
            c = SE([c], lambda e: e.activation(s1, s1, ACT.Ln, bias=1.0))
            later(1, lambda: fl.append(VE([c], lambda e: e.scalar_tensor_tensor(f, f, 0.0, s1, ALU.min,
                                                                                ALU.subtract))))

        heads = lambda z, tt, w: z[:, tt, 0:8 * w].rearrange("p (h d) -> p h d", d=w)
        sums = {}

        def latents():
            ln = []
            for tt in range(TT):
                for j, (c0, n) in enumerate(parts):
                    ln.append(VE([lat_r, *sq], lambda e, tt=tt, j=j, c0=c0, n=n: e.tensor_scalar(
                        lat[:, tt, c0:c0 + n], lat[:, tt, c0:c0 + n], lat_rs[:, tt * 3 + j:tt * 3 + j + 1], None,
                        ALU.mult)))
            b = aux()

            def running(e):
                e.matmul(b.t[:, 0:FH], con("upto"), decay[:, 0, 0, :], start=True, stop=True)
                e.matmul(b.t[:, FH:2 * FH], con("ones"), decay[:, 0, 0, :], start=True, stop=False)
                return e.matmul(b.t[:, FH:2 * FH], con("upto"), decay[:, 0, 1, :], start=False, stop=True)

            t = PE([*fl, const_in, *b.free], running)
            sums["c"] = VE([t], lambda e: e.tensor_copy(decay[:, 2, :, :].rearrange("p t h -> p (t h)"),
                                                        b.t[:, 0:2 * FH]))
            b.free = [sums["c"]]
            later(2, lambda: latents_turned(ln))

        def latents_turned(ln):
            for j, (c0, n, gain) in enumerate(((0, P, col("q_lat")[:, 0:1]), (P, QL - P, col("q_lat")[:, 1:2]),
                                               (QL, KVL, col("kv_lat")))):
                b = aux()
                t = transposes(b, ln, [(tt * P, lat[:, tt, c0:c0 + n]) for tt in range(TT)])
                v = scratch()
                a = VE([t, cols_in, *v.free], lambda e, v=v, b=b, n=n, gain=gain: e.tensor_scalar(
                    v.t[0:n, 0:S], b.t[0:n, 0:S], gain[0:n, :], None, ALU.mult))
                b.free = [a]
                v.free = split_to(l_hi[0:n, j, :], l_lo[0:n, j, :], v.t[0:n, 0:S], [a, *lz])
                l_ready[j] = [*v.free, *lz]
            for tt in range(TT):
                k1 = lat[:, tt, QL + KVL:QL + KVL + MR].unsqueeze(1)
                a = GP([*ln, rows_in], lambda e, k1=k1: e.tensor_tensor(k1, k1, row("mla_kr").unsqueeze(1), ALU.mult))
                kr.append(rope(k1, table(cs2, tt), table(sn2, tt), 1, MR, [a]))

        later(1, forget_gates)
        later(3, latents)

        def heads_turned(src, dst, w, ready, h, bank, out, gain):
            t = transposes(bank, ready, [((j * TT + tt) * P, heads(src, tt, w)[:, h + j, :])
                                         for j in range(2) for tt in range(TT)])
            c = SE([t, cols_in, *tables, *scored], lambda e: e.activation(
                dst[0:w, h:h + 2, :].rearrange("p k t -> p (k t)"), bank.t[0:w, :], ACT.Copy, scale=gain[0:w, :]))
            bank.free = [c]
            out.append(c)
            return t

        scored = []
        fq_ready, fk_ready, read_by = [], [], []

        def fox_queries(done):
            for tt in range(TT):
                v, cu = heads(tokq, tt, FK), decay[:, 2, tt, :].unsqueeze(2)
                done = [*done,
                        GP([sums["c"]], lambda e, v=v, cu=cu: e.tensor_copy(v[:, :, HD:HD + 1], cu)),
                        GP([], lambda e, v=v: e.memset(v[:, :, HD + 1:HD + 2], 1.0))]
            later(2, lambda: [read_by.append(heads_turned(tokq, q2_t, FK, done, h, aux(), fq_ready, fox_q_gain))
                              for h in range(0, 8, 2)])

        def fox_keys(done):
            for tt in range(TT):
                v, cu = heads(tokk, tt, FK), decay[:, 2, tt, :].unsqueeze(2)
                done = [*done,
                        GP([sums["c"]], lambda e, v=v, cu=cu: e.tensor_scalar(v[:, :, HD + 1:HD + 2], cu, -1.0, None,
                                                                              ALU.mult)),
                        GP([], lambda e, v=v: e.memset(v[:, :, HD:HD + 1], 1.0))]
            later(2, lambda: [read_by.append(heads_turned(tokk, k2_t, FK, done, h, aux(), fk_ready, col("fox_k")))
                              for h in range(0, 8, 2)])

        def to_tokv(pair, t, c0):
            out = [SE([t], lambda e, tt=tt: e.activation(tokv2[:, tt, c0:c0 + 512], pair[tt].t[:, :], ACT.Copy))
                   for tt in range(TT)]
            for tt in range(TT):
                pair[tt].free = [out[tt]]
            return out

        pair, t = drain_steps(linear("fox_q", (h_hi, h_lo), h2, True))
        head_norm(pair, [t], [(0, FH, None, lambda tt: heads(tokq, tt, FK)[:, :, 0:HD])], FH, HD, (),
                  fox_queries)
        pair, t = drain_steps(linear("fox_k", (h_hi, h_lo), h2, True))
        head_norm(pair, [t], [(0, FH, None, lambda tt: heads(tokk, tt, FK)[:, :, 0:HD])], FH, HD, (),
                  fox_keys)
        pair, t = drain_steps(linear("fox_v", (h_hi, h_lo), h2, True))
        fv = to_tokv(pair, t, 512)
        run_all()
        l_list = [l_ready[j] for j in range(3)]
        mla_ready = []
        pair, t = drain_steps(linear("mla_qn", (l_hi, l_lo), l_list, True))
        head_norm(pair, [t], [(0, MH, None, lambda tt: heads(tokq, tt, MQ)[:, :, 0:MN])], MH, MN,
                  read_by, mla_ready.extend, copied=True)
        pair, t = drain_steps(linear("mla_qr", (l_hi, l_lo), l_list, True))
        head_norm(pair, [t], [(0, MH, turn_of["mla_qr"], lambda tt: heads(tokq, tt, MQ)[:, :, MN:MQ])], MH, MR,
                  read_by, mla_ready.extend, copied=True)
        pair, t = drain_steps(linear("mla_kn", (l_hi, l_lo), l_list, True, k0=2))
        head_norm(pair, [t], [(0, MH, None, lambda tt: heads(tokk, tt, MQ)[:, :, 0:MN])], MH, MN,
                  read_by, mla_ready.extend, copied=True)
        pair, t = drain_steps(linear("mla_v", (l_hi, l_lo), l_list, True, k0=2))
        mv = to_tokv(pair, t, 0)
        for tt in range(TT):
            k1 = lat[:, tt, QL + KVL:QL + KVL + MR].unsqueeze(1)
            mla_ready.append(GP([*kr, *read_by], lambda e, tt=tt, k1=k1: e.tensor_copy(
                heads(tokk, tt, MQ)[:, :, MN:MQ], bcast(k1, [P, MH, MR]))))

        o_ready = {}

        def close_plain(kt, ob):
            def close(t):
                b = SE([t], lambda e: e.activation(o2_hi[:, kt, :], ob.t, ACT.Copy))
                c = VE([b], lambda e: e.tensor_tensor(o2_lo[:, kt, :], ob.t, o2_hi[:, kt, :].bitcast(F32),
                                                      ALU.subtract))
                o_ready[kt] = ob.free = [b, c]
                return lambda: None
            return close

        def head_items(w, scale, v0, kt0, ready, vr):
            return [dict(q=lambda t, h=h: q2_t[0:w, h, t * P:(t + 1) * P], k=lambda n, h=h: k2_t[0:w, h, 0:n],
                         v=lambda j, h=h: tokv2[:, j, v0 + h * HD:v0 + (h + 1) * HD], ready=ready, v_ready=vr,
                         scale=scale, o_buf=o_acc, out=o_acc.t[(h % 2) * HD:(h % 2 + 1) * HD, :], gate=None,
                         first=True, last=True, before=None, close=close_plain(kt0 + h // 2, o_acc) if h % 2 else None)
                    for h in range(8)]

        result = []

        def gates_2():
            for j, name in enumerate(("gate_mla0", "gate_mla1", "gate_fox0", "gate_fox1")):
                pair, t = yield from linear(name, (h_hi, h_lo), h2, False)
                for i in range(2):
                    for b in range(2):
                        k = 4 * j + 2 * i + b
                        a = SE([t, hb_ready], lambda e, k=k, i=i, b=b, pair=pair: e.activation(
                            gate2[:, k, :], pair[i].t[:, b * S:(b + 1) * S], ACT.Tanh, bias=half_b[:, k:k + 1],
                            scale=0.5))
                    pair[i].free = [a]
            result.append(a)

        mla_heads = []

        def place(h):
            def hook():
                run_all()
                scored[:] = [(PE.sem, PE.count)]
                heads_turned(tokq, q2_t, MQ, mla_ready, h, banks[6], mla_heads, col("mla_q"))
                heads_turned(tokk, k2_t, MQ, mla_ready, h, banks[6], mla_heads, col("mla_k"))
            return hook

        mixed = scr[:, :, :].rearrange("p t (k s) -> p (t k) s", s=S)
        mm_ready = []

        def fox_branch():
            for j in range(2):
                pair, t = yield from linear(f"br_fox{j}", (o2_hi, o2_lo), TilesReady(o_ready), False, k0=4)
                for i in range(2):
                    k = 4 * j + 2 * i
                    a = VE([t, result[-1], *mla_ready], lambda e, k=k, i=i, pair=pair: e.scalar_tensor_tensor(
                        mixed[:, k:k + 2, :], gate2[:, 8 + k:10 + k, :], 1.0,
                        pair[i].t[:, :].rearrange("p (k s) -> p k s", k=2), ALU.add, ALU.mult))
                    pair[i].free = [a]
                    mm_ready.append(a)

        branch_steps = fox_branch()
        attention(head_items(FK, 1.0, 512, 4, [*fq_ready, *fk_ready], fv)
                  + head_items(MQ, MQ ** -0.5, 0, 0, mla_heads, mv), prob2_t, soft2, gates_2(), 1, branch_steps, 4,
                  {6: place(0), 8: place(2), 9: place(4), 10: place(6)})
        drain_steps(branch_steps)
        o_list = [o_ready[k] for k in range(KT)]
        m_ready = {}

        def split_sum(k, v, vv, a):
            v.free = split_to(h_hi[:, k:k + 2, :], h_lo[:, k:k + 2, :], vv, [a], 0.5)
            m_ready[k] = m_ready[k + 1] = v.free

        for j in range(2):
            pair, t = drain_steps(linear(f"br_mla{j}", (o2_hi, o2_lo), o_list, False))
            sums = []
            for i in range(2):
                k = 4 * j + 2 * i
                v = scratch()
                vv = v.t[:, :].rearrange("p (k s) -> p k s", k=2)
                a = VE([t, *v.free], lambda e, k=k, i=i, vv=vv, pair=pair: e.scalar_tensor_tensor(
                    vv, gate2[:, k:k + 2, :], 1.0, pair[i].t[:, :].rearrange("p (k s) -> p k s", k=2),
                    ALU.add, ALU.mult))
                pair[i].free = [a]
                a = GP([a, *mm_ready], lambda e, k=k, vv=vv: e.tensor_tensor(vv, vv, mixed[:, k:k + 2, :], ALU.add))
                sums.append((k, v, vv, a))
            later(1, lambda sums=sums: [split_sum(*s_) for s_ in sums])
        run_all()
        scr_buf.free = [a]
        x3 = drain_steps(residual(["mix_out0", "mix_out1"], (h_hi, h_lo), TilesReady(m_ready), 1.0, x2))
        mix.close()

        x4 = ffn(2, x3)
        assert taken[0] == len(units)

        out_sem = sem("out_stored")
        sync_steps.append((x4, lambda e: e.dma_start(out_d.rearrange("o (t p) d -> p (o t) d", p=P),
                                                     x[:, :, :]).then_inc(out_sem, 16)))

        block = ctx.enter_context(nc.Block())

        @block.sync
        def _(e):
            met = {}
            for waits, emit in sync_steps:
                for s, value in waits:
                    if met.get(s.name, 0) < value:
                        e.wait_ge(s, value)
                        met[s.name] = value
                emit(e)
            e.wait_ge(out_sem, 16)

        @block.tensor
        def _(e):
            PE.run(e)

        @block.vector
        def _(e):
            VE.run(e)

        @block.scalar
        def _(e):
            SE.run(e)

        @block.gpsimd
        def _(e):
            GP.run(e)


def head_order():
    return [gp * 8 + half * 4 + r for gp in range(2) for r in range(4) for half in range(2)]


def chunk_arrays(a):
    pairs = head_order()
    hd = lambda hs: np.concatenate([np.arange(h * HD, (h + 1) * HD) for h in hs])
    perm = hd(pairs)
    w = a["nsa_w_in"][0]
    q, kc, vc, ks, vs, kw, vw, gl, z = np.split(w, np.cumsum([D] + [256] * 6 + [48])[:8], axis=1)
    out = {}
    for i in range(2):
        for n in range(6):
            out[f"ada{i}_{n}"] = a["ada_w"][i][:, n * 512:(n + 1) * 512]
    halves = lambda name, m: out.update({f"{name}{j}": m[:, j * 512:(j + 1) * 512] for j in range(2)})
    cat = lambda *m: np.concatenate(m, axis=1)
    out["nsa_kcvc"], out["nsa_kskw"], out["nsa_vsvw"] = cat(kc, vc), cat(ks, kw), cat(vs, vw)
    out["nsa_gate"] = np.concatenate([gl.reshape(D, NH, 3)[:, pairs].transpose(0, 2, 1).reshape(D, 3 * NH),
                                      np.zeros((D, P - 3 * NH), gl.dtype)], 1)
    halves("nsa_q", q[:, perm])
    halves("nsa_z", z[:, perm])
    halves("nsa_out", a["nsa_w_out"][0][perm])
    for i in range(2):
        out[f"cmp_w1_{i}"] = a["nsa_cmp_w1"][0, i]
    q, k, v, z = np.split(a["moba_w_in"][0], np.cumsum([D, 256, 256]), axis=1)
    halves("moba_q", q[:, perm])
    out["moba_kv"] = cat(k, v)
    halves("moba_z", z[:, perm])
    halves("moba_out", a["moba_w_out"][0][perm])
    for i in (1, 2):
        g, u, d = (a[f"ffn{i}_w_{n}_2"][0] for n in ("gate", "up", "down"))
        for n in range(FT // 2):
            out[f"ffn{i}_up{n}"] = cat(g[:, n * 256:(n + 1) * 256], u[:, n * 256:(n + 1) * 256])
        halves(f"ffn{i}_down", d)
    ql, kvl, kr, fq, fk, fv, fl, gm, gf = np.split(
        a["w_in_2"][0], np.cumsum([QL, KVL, MR, 512, 512, 512, FH, D]), axis=1)
    out["mix_lat"] = cat(ql, kvl, kr, fl)
    out["fox_q"], out["fox_k"], out["fox_v"] = fq, fk, fv
    halves("gate_mla", gm)
    halves("gate_fox", gf)
    qb = a["mla_w_qb_2"][0].reshape(QL, MH, MQ)
    qb = np.concatenate([qb, np.zeros((2 * P - QL, MH, MQ), qb.dtype)])
    out["mla_qn"], out["mla_qr"] = qb[:, :, :MN].reshape(2 * P, -1), qb[:, :, MN:].reshape(2 * P, -1)
    kvb = a["mla_w_kvb_2"][0].reshape(KVL, MH, 2 * MN)
    out["mla_kn"], out["mla_v"] = kvb[:, :, :MN].reshape(KVL, -1), kvb[:, :, MN:].reshape(KVL, -1)
    halves("br_mla", a["w_branch_mla_2"][0])
    halves("br_fox", a["w_branch_fox_2"][0])
    halves("mix_out", a["w_o_2"][0])
    return out


def packed_weights(a):
    units, total = unit_list()
    mats = chunk_arrays(a)
    out = np.empty((P, total), np.float32)
    for name, k, m, n, _, _, at in units:
        part = mats[name][k * P:(k + m) * P]
        out[:, at:at + m * n] = part.reshape(m, P, n).transpose(1, 0, 2).reshape(P, m * n)
    return out


def packed_columns(a):
    out = np.zeros((P, NCOLS), np.float32)
    put = lambda name, v: out.__setitem__((slice(None), slice(*COLS[name])), v)
    by = lambda v: v.reshape(-1, P).T
    put("c", by(a["c"][0]))
    for i in range(2):
        put(f"norm{i}", by(a["norm_g"][i]))
        put(f"ada{i}", by(a["ada_b"][i]))
        put(f"b1_{i}", by(a["nsa_cmp_b1"][0, i]))
        put(f"pe{i}", a["nsa_cmp_pe"][0, i].reshape(CJ, P).T)
        put(f"w2_{i}", a["nsa_cmp_w2"][0, i].reshape(2, P, HD).transpose(1, 0, 2).reshape(P, 2 * HD))
    put("ffn1", by(a["ffn1_norm_2"][0]))
    put("mix", by(a["mix_norm_2"][0]))
    put("ffn2", by(a["ffn2_norm_2"][0]))
    put("gate_mla", by(a["b_gate_2"][0, 0]))
    put("gate_fox", by(a["b_gate_2"][0, 1]))
    ql = a["mla_q_lat_norm_2"][0]
    put("q_lat", by(np.concatenate([ql, np.zeros(2 * P - QL, ql.dtype)])))
    put("kv_lat", by(a["mla_kv_lat_norm_2"][0]))
    ones = lambda n: np.ones(n, np.float32)
    column = lambda *parts: np.concatenate([*parts, ones(P - sum(len(v) for v in parts))])[:, None]
    pair = lambda gain: column(ones(ROT), gain[ROT:], ones(ROT), gain[ROT:])
    put("gate_b", np.concatenate([a["nsa_gate_b"][0].reshape(NH, 3)[head_order()].T.reshape(-1),
                                  np.zeros(P - 3 * NH, np.float32)])[:, None])
    put("nsa_q", pair(a["nsa_q_norm"][0]))
    put("nsa_ks", pair(a["nsa_k_norm"][0][1]))
    put("nsa_kw", pair(a["nsa_k_norm"][0][2]))
    put("moba_q", pair(a["moba_q_norm"][0]))
    put("moba_k", pair(a["moba_k_norm"][0]))
    put("mla_q", column(a["mla_q_nope_gain_2"][0]))
    put("mla_k", column(a["mla_k_nope_gain_2"][0]))
    put("fox_q", column(a["fox_q_gain_2"][0]))
    put("fox_k", column(a["fox_k_gain_2"][0]))
    return out


def packed_rows(a):
    kn = a["nsa_k_norm"][0]
    return np.concatenate([kn[0], a["nsa_q_norm"][0][:ROT], kn[1][:ROT], kn[2][:ROT], a["moba_q_norm"][0][:ROT],
                           a["moba_k_norm"][0][:ROT], a["mla_q_rope_gain_2"][0], a["mla_k_rope_gain_2"][0],
                           a["fox_b_f_2"][0]])[None, :]


def packed_positions(a):
    by = lambda v: v.reshape(TT, P).T
    p1, p2 = a["positions"][0], a["positions_2"][0]
    ends = np.zeros(P, p1.dtype)
    at = np.arange(NKV)[:, None] * CPAD + np.arange(NCMP)[None, :]
    ends[at] = p1[np.arange(NCMP) * CMP_STRIDE + CMP_LEN - 1][None, :]
    return np.concatenate([np.repeat(by(p1), 8, axis=1), np.repeat(ends[:, None], 8, axis=1),
                           np.repeat(by(p2), 16, axis=1)], axis=1)


def kernel(**inputs):
    import concourse.bacc as bacc
    from concourse.bass_utils import run_bass_kernel_spmd

    a = {k: np.asarray(v) for k, v in inputs.items()}
    arrays = {"in_weights": packed_weights(a), "in_columns": packed_columns(a), "in_rows": packed_rows(a),
              "in_constants": shape_constants(), "in_positions": packed_positions(a),
              "in_gate_bias": a["ada_b"][:, 2 * D:], "in_x": a["x"]}
    arrays = {k: np.ascontiguousarray(v) for k, v in arrays.items()}
    nc = bacc.Bacc("TRN2", target_bir_lowering=False, num_devices=1)
    args = [nc.dram_tensor(k, v.shape, mybir.dt.from_np(v.dtype), kind="ExternalInput").ap()
            for k, v in arrays.items()]
    out = nc.dram_tensor("out", a["x"].shape, F32, kind="ExternalOutput").ap()
    program(nc, *args, out)
    return run_bass_kernel_spmd(nc, [arrays], core_ids=[0]).results[0]["out"]
```
